# Optimizing a Trainium2 kernel written in Bass

```python
import math
import jax, jax.numpy as jnp
from jax import lax
import numpy as np

D_MODEL = 2048
BATCH = 1
SEQ = 256
DEPTH = 1

SSM_WIDTH = D_MODEL // 2
SSM_GROUP = 16
SSM_GROUPS = SSM_WIDTH // SSM_GROUP
SSM_STATE = 64
ATTN_WIDTH = D_MODEL - SSM_WIDTH
HEAD_DIM = 128
N_HEADS = ATTN_WIDTH // HEAD_DIM
DILATED_BRANCHES = ((128, 1), (512, 4), (2048, 16))
FFN_HIDDEN = ((8 * D_MODEL + 3 * 256 - 1) // (3 * 256)) * 256
IN_PROJ_WIDTH = SSM_WIDTH + 3 * ATTN_WIDTH
N_MOD = 6
DT_MIN = 1e-3
DT_MAX = 1e-1
NORM_EPS = 1e-6
MASK_VALUE = -1e30


def _rms(x, w):
    xf = x.astype(jnp.float32)
    y = xf * lax.rsqrt(jnp.mean(xf * xf, axis=-1, keepdims=True) + NORM_EPS)
    return y * w.astype(jnp.float32)

def _modulate(y, shift, scale):
    return y * (1.0 + scale.astype(jnp.float32)[:, None, :]) + shift.astype(jnp.float32)[:, None, :]

def _complex_linear_combine(e1, e2):
    a1r, a1i, b1r, b1i = e1
    a2r, a2i, b2r, b2i = e2
    ar = a1r * a2r - a1i * a2i
    ai = a1r * a2i + a1i * a2r
    br = a2r * b1r - a2i * b1i + b2r
    bi = a2r * b1i + a2i * b1r + b2i
    return ar, ai, br, bi

def _s5_mixer(u, a_re, a_im, log_dt, b_re, b_im, c_re, c_im, d, w_glu):
    B, S, _ = u.shape
    f32 = jnp.float32
    uf = u.astype(f32).reshape(B, S, SSM_GROUPS, SSM_GROUP)
    a_re = a_re.astype(f32)
    a_im = a_im.astype(f32)
    dt = jnp.exp(log_dt.astype(f32))[:, None]
    mag = jnp.exp(a_re * dt)
    abar_re = mag * jnp.cos(a_im * dt)
    abar_im = mag * jnp.sin(a_im * dt)
    num_re = abar_re - 1.0
    num_im = abar_im
    den = a_re * a_re + a_im * a_im
    z_re = (num_re * a_re + num_im * a_im) / den
    z_im = (num_im * a_re - num_re * a_im) / den
    b_re = b_re.astype(f32)
    b_im = b_im.astype(f32)
    bbar_re = z_re[..., None] * b_re - z_im[..., None] * b_im
    bbar_im = z_re[..., None] * b_im + z_im[..., None] * b_re
    bu_re = jnp.einsum('bsgc,gnc->sbgn', uf, bbar_re)
    bu_im = jnp.einsum('bsgc,gnc->sbgn', uf, bbar_im)
    a_seq_re = jnp.broadcast_to(abar_re[None, None], (S, 1, SSM_GROUPS, SSM_STATE))
    a_seq_im = jnp.broadcast_to(abar_im[None, None], (S, 1, SSM_GROUPS, SSM_STATE))
    _, _, h_re, h_im = lax.associative_scan(
        _complex_linear_combine, (a_seq_re, a_seq_im, bu_re, bu_im), axis=0)
    y = (jnp.einsum('sbgn,gcn->bsgc', h_re, c_re.astype(f32))
         - jnp.einsum('sbgn,gcn->bsgc', h_im, c_im.astype(f32))
         + d.astype(f32) * uf)
    y = jax.nn.gelu(y.reshape(B, S, SSM_WIDTH))
    return y * jax.nn.sigmoid(y @ w_glu.astype(f32))

def _dilated_branch(q, k, v, slopes, window, dilation):
    B, S, H, E = q.shape
    blk = window // dilation
    span = blk * dilation
    s_pad = ((S + span - 1) // span) * span
    pad = s_pad - S
    L = s_pad // dilation
    nb = L // blk

    def strided_blocks(t):
        t = jnp.pad(t, ((0, 0), (0, pad), (0, 0), (0, 0)))
        t = t.reshape(B, L, dilation, H, E).transpose(0, 2, 3, 1, 4)
        return t.reshape(B, dilation, H, nb, blk, E)

    qb, kb, vb = strided_blocks(q), strided_blocks(k), strided_blocks(v)

    def with_prev(t):
        prev = jnp.concatenate([jnp.zeros_like(t[:, :, :, :1]), t[:, :, :, :-1]], axis=3)
        return jnp.concatenate([prev, t], axis=4)

    kc, vc = with_prev(kb), with_prev(vb)
    scores = jnp.einsum('bdhnqe,bdhnke->bdhnqk', qb, kc)
    qi = jnp.arange(blk)[:, None]
    ki = jnp.arange(2 * blk)[None, :]
    dist = qi + blk - ki
    band = (dist >= 0) & (dist <= blk)
    first = (jnp.arange(nb) == 0)[:, None, None]
    valid = band[None] & ~(first & (ki < blk)[None])
    bias = -slopes[:, None, None, None] * (dilation * dist).astype(jnp.float32)[None, None]
    scores = jnp.where(valid, scores + bias, MASK_VALUE)
    m = jnp.max(scores, axis=-1)
    p = jnp.exp(scores - m[..., None])
    l = jnp.sum(p, axis=-1)
    o = jnp.einsum('bdhnqk,bdhnke->bdhnqe', p, vc)

    m = m.reshape(B, dilation, H, L).transpose(0, 3, 1, 2).reshape(B, s_pad, H)[:, :S]
    l = l.reshape(B, dilation, H, L).transpose(0, 3, 1, 2).reshape(B, s_pad, H)[:, :S]
    o = o.reshape(B, dilation, H, L, E).transpose(0, 3, 1, 2, 4).reshape(B, s_pad, H, E)[:, :S]
    return m, l, o

def _dilated_attention(q, k, v, q_norm_w, k_norm_w):
    B, S, _ = q.shape
    q = _rms(q.reshape(B, S, N_HEADS, HEAD_DIM), q_norm_w) * (HEAD_DIM ** -0.5)
    k = _rms(k.reshape(B, S, N_HEADS, HEAD_DIM), k_norm_w)
    v = v.astype(jnp.float32).reshape(B, S, N_HEADS, HEAD_DIM)
    slopes = jnp.exp2(-8.0 * jnp.arange(1, N_HEADS + 1, dtype=jnp.float32) / N_HEADS)
    outs = [_dilated_branch(q, k, v, slopes, w, dl) for (w, dl) in DILATED_BRANCHES]
    ms = jnp.stack([o[0] for o in outs])
    ls = jnp.stack([o[1] for o in outs])
    os_ = jnp.stack([o[2] for o in outs])
    w = jnp.exp(ms - jnp.max(ms, axis=0, keepdims=True))
    num = jnp.sum(w[..., None] * os_, axis=0)
    den = jnp.sum(w * ls, axis=0)
    return (num / den[..., None]).reshape(B, S, ATTN_WIDTH)

def first_inputs(seed: int = 0) -> dict:
    key = jax.random.key(seed)
    ks = jax.random.split(key, 24)
    f32 = jnp.float32
    nrm = lambda k, shape, s: jax.random.normal(k, shape, f32) * s
    D, G, N, C = D_MODEL, SSM_GROUPS, SSM_STATE, SSM_GROUP
    x = jax.random.normal(ks[0], (BATCH, SEQ, D), f32)
    c = jax.random.normal(ks[1], (BATCH, D), f32)
    w_ada = nrm(ks[2], (DEPTH, D, N_MOD * D), 0.5 * D ** -0.5)
    b_ada = nrm(ks[3], (DEPTH, N_MOD * D), 0.05)
    norm1_w = 1.0 + nrm(ks[4], (DEPTH, D), 0.02)
    w_in = nrm(ks[5], (DEPTH, D, IN_PROJ_WIDTH), D ** -0.5)
    ssm_a_re = -0.5 + nrm(ks[6], (DEPTH, G, N), 0.01)
    ssm_a_im = jnp.pi * jnp.arange(N, dtype=f32)[None, None, :] + nrm(ks[7], (DEPTH, G, N), 0.01)
    ssm_log_dt = jax.random.uniform(ks[8], (DEPTH, G), f32, math.log(DT_MIN), math.log(DT_MAX))
    ssm_b_re = nrm(ks[9], (DEPTH, G, N, C), (2 * C) ** -0.5)
    ssm_b_im = nrm(ks[10], (DEPTH, G, N, C), (2 * C) ** -0.5)
    ssm_c_re = nrm(ks[11], (DEPTH, G, C, N), (2 * N) ** -0.5)
    ssm_c_im = nrm(ks[12], (DEPTH, G, C, N), (2 * N) ** -0.5)
    ssm_d = nrm(ks[13], (DEPTH, G, C), 1.0)
    ssm_w_glu = nrm(ks[14], (DEPTH, SSM_WIDTH, SSM_WIDTH), SSM_WIDTH ** -0.5)
    q_norm_w = 1.0 + nrm(ks[15], (DEPTH, HEAD_DIM), 0.02)
    k_norm_w = 1.0 + nrm(ks[16], (DEPTH, HEAD_DIM), 0.02)
    w_out = nrm(ks[17], (DEPTH, D, D), D ** -0.5)
    norm2_w = 1.0 + nrm(ks[18], (DEPTH, D), 0.02)
    w_ffn_gate = nrm(ks[19], (DEPTH, D, FFN_HIDDEN), D ** -0.5)
    w_ffn_up = nrm(ks[20], (DEPTH, D, FFN_HIDDEN), D ** -0.5)
    w_ffn_down = nrm(ks[21], (DEPTH, FFN_HIDDEN, D), FFN_HIDDEN ** -0.5)
    return {"x": x, "c": c, "w_ada": w_ada, "b_ada": b_ada, "norm1_w": norm1_w,
            "w_in": w_in, "ssm_a_re": ssm_a_re, "ssm_a_im": ssm_a_im,
            "ssm_log_dt": ssm_log_dt, "ssm_b_re": ssm_b_re, "ssm_b_im": ssm_b_im,
            "ssm_c_re": ssm_c_re, "ssm_c_im": ssm_c_im, "ssm_d": ssm_d,
            "ssm_w_glu": ssm_w_glu, "q_norm_w": q_norm_w, "k_norm_w": k_norm_w,
            "w_out": w_out, "norm2_w": norm2_w, "w_ffn_gate": w_ffn_gate,
            "w_ffn_up": w_ffn_up, "w_ffn_down": w_ffn_down}

def first_block(x, c, w_ada, b_ada, norm1_w, w_in, ssm_a_re, ssm_a_im, ssm_log_dt,
              ssm_b_re, ssm_b_im, ssm_c_re, ssm_c_im, ssm_d, ssm_w_glu,
              q_norm_w, k_norm_w, w_out, norm2_w, w_ffn_gate, w_ffn_up, w_ffn_down):
    cond = jax.nn.silu(c)
    splits = [SSM_WIDTH, SSM_WIDTH + ATTN_WIDTH, SSM_WIDTH + 2 * ATTN_WIDTH]
    for i in range(DEPTH):
        mod = cond @ w_ada[i] + b_ada[i]
        shift1, scale1, gate1, shift2, scale2, gate2 = jnp.split(mod, N_MOD, axis=-1)

        h = _modulate(_rms(x, norm1_w[i]), shift1, scale1).astype(x.dtype)
        proj = h @ w_in[i]
        u, q, k, v = jnp.split(proj, splits, axis=-1)
        y_ssm = _s5_mixer(u, ssm_a_re[i], ssm_a_im[i], ssm_log_dt[i], ssm_b_re[i], ssm_b_im[i],
                          ssm_c_re[i], ssm_c_im[i], ssm_d[i], ssm_w_glu[i])
        y_att = _dilated_attention(q, k, v, q_norm_w[i], k_norm_w[i])
        mixed = jnp.concatenate([y_ssm, y_att], axis=-1).astype(x.dtype) @ w_out[i]
        x = x + gate1[:, None, :] * mixed

        h2 = _modulate(_rms(x, norm2_w[i]), shift2, scale2).astype(x.dtype)
        ffn = (jax.nn.silu(h2 @ w_ffn_gate[i]) * (h2 @ w_ffn_up[i])) @ w_ffn_down[i]
        x = x + gate2[:, None, :] * ffn
    return x


DEPTH_2 = 2

GRID_W = 64
CTX_LEN = 256
ROPE_THETA = 10000.0
Q_BLOCK = 128
LN_EPS = 1e-6
RMS_EPS = 1e-6

A_HEADS = 8
A_Q_LORA = 768
A_KV_LORA = 512
A_NOPE = 128
A_ROPE = 64
A_V = 128
A_SCALE = (A_NOPE + A_ROPE) ** -0.5
B_HEADS = 8
B_KV_HEADS = 2
B_GROUP = B_HEADS // B_KV_HEADS
B_HEAD_DIM = 128
B_SCALE = B_HEAD_DIM ** -0.5
A_WIDTH = A_HEADS * A_V
B_WIDTH = B_HEADS * B_HEAD_DIM
ATTN_WIDTH_2 = A_WIDTH + B_WIDTH
ATTN_IN = A_Q_LORA + A_KV_LORA + A_ROPE + B_WIDTH + 2 * B_KV_HEADS * B_HEAD_DIM + ATTN_WIDTH_2
C_EXPAND = 2
C_WIDTH = C_EXPAND * D_MODEL
C_GROUPS = 16
C_GROUP_DIM = C_WIDTH // C_GROUPS

N_EVEN = (DEPTH_2 + 1) // 2
N_ODD = DEPTH_2 // 2
DEEPNORM_ALPHA = (2.0 * DEPTH_2) ** 0.25
DEEPNORM_BETA = (8.0 * DEPTH_2) ** -0.25


def layer_norm(x):
    xf = x.astype(jnp.float32)
    mu = jnp.mean(xf, axis=-1, keepdims=True)
    var = jnp.mean(jnp.square(xf - mu), axis=-1, keepdims=True)
    return ((xf - mu) * lax.rsqrt(var + LN_EPS)).astype(x.dtype)

def rms_norm(x, g):
    xf = x.astype(jnp.float32)
    y = xf * lax.rsqrt(jnp.mean(xf * xf, axis=-1, keepdims=True) + RMS_EPS)
    return (y * g.astype(jnp.float32)).astype(x.dtype)

def axial_rope_angles(rows, rot_dim):
    r, col = jnp.meshgrid(jnp.arange(rows), jnp.arange(GRID_W), indexing="ij")
    r = r.reshape(-1).astype(jnp.float32)
    col = col.reshape(-1).astype(jnp.float32)
    n_freq = rot_dim // 4
    inv = ROPE_THETA ** (-jnp.arange(n_freq, dtype=jnp.float32) / n_freq)
    return jnp.concatenate([r[:, None] * inv, col[:, None] * inv], axis=-1)

def apply_rope(x, ang):
    cos = jnp.cos(ang)[None, :, None, :]
    sin = jnp.sin(ang)[None, :, None, :]
    xf = x.astype(jnp.float32).reshape(*x.shape[:-1], -1, 2)
    x1, x2 = xf[..., 0], xf[..., 1]
    out = jnp.stack([x1 * cos - x2 * sin, x1 * sin + x2 * cos], axis=-1)
    return out.reshape(x.shape).astype(x.dtype)

def block_attention(q, k, v, scale):
    b, s, g, r, dk = q.shape
    nblk = s // Q_BLOCK
    qb = jnp.moveaxis(q.reshape(b, nblk, Q_BLOCK, g, r, dk), 1, 0)

    def one_block(qi):
        sc = jnp.einsum("bqgrd,bkgd->bgrqk", qi, k, preferred_element_type=jnp.float32) * scale
        p = jax.nn.softmax(sc, axis=-1).astype(v.dtype)
        return jnp.einsum("bgrqk,bkge->bqgre", p, v)

    out = lax.map(one_block, qb)
    return jnp.moveaxis(out, 0, 1).reshape(b, s, g, r, v.shape[-1])

def attn_project(h, w_in, wq_b, q_lora_g, kv_lora_g, wkv_b, qn_g, kn_g):
    b, l, _ = h.shape
    splits = np.cumsum([A_Q_LORA, A_KV_LORA, A_ROPE, B_WIDTH,
                        B_KV_HEADS * B_HEAD_DIM, B_KV_HEADS * B_HEAD_DIM]).tolist()
    z = h @ w_in
    c_q, c_kv, k_pe, q_b, k_b, v_b, gate = jnp.split(z, splits, axis=-1)
    q_a = (rms_norm(c_q, q_lora_g) @ wq_b).reshape(b, l, A_HEADS, A_NOPE + A_ROPE)
    kv_a = (rms_norm(c_kv, kv_lora_g) @ wkv_b).reshape(b, l, A_HEADS, A_NOPE + A_V)
    q_nope, q_pe = q_a[..., :A_NOPE], q_a[..., A_NOPE:]
    k_nope, v_a = kv_a[..., :A_NOPE], kv_a[..., A_NOPE:]
    k_pe = k_pe.reshape(b, l, 1, A_ROPE)
    q_b = rms_norm(q_b.reshape(b, l, B_HEADS, B_HEAD_DIM), qn_g)
    k_b = rms_norm(k_b.reshape(b, l, B_KV_HEADS, B_HEAD_DIM), kn_g)
    v_b = v_b.reshape(b, l, B_KV_HEADS, B_HEAD_DIM)
    return q_nope, q_pe, k_nope, k_pe, v_a, q_b, k_b, v_b, gate

def mla_qk(q_nope, q_pe, k_nope, k_pe):
    b, l, h, _ = q_nope.shape
    q = jnp.concatenate([q_nope, q_pe], axis=-1)[:, :, :, None, :]
    k = jnp.concatenate([k_nope, jnp.broadcast_to(k_pe, (b, l, h, A_ROPE))], axis=-1)
    return q, k

def gated_out(y_a, y_b, gate, w_out):
    b, l = y_a.shape[:2]
    y = jnp.concatenate([y_a.reshape(b, l, A_WIDTH), y_b.reshape(b, l, B_WIDTH)], axis=-1)
    return (y * jax.nn.silu(gate)) @ w_out

def attention_mixer(h_lat, h_ctx, ang_a, ang_b, w_in, wq_b, q_lora_g, kv_lora_g, wkv_b,
                    qn_g, kn_g, w_out, with_ctx_queries):
    b, s, _ = h_lat.shape
    lqn, lqp, lkn, lkp, lva, lqb, lkb, lvb, lgate = attn_project(
        h_lat, w_in, wq_b, q_lora_g, kv_lora_g, wkv_b, qn_g, kn_g)
    cqn, cqp, ckn, ckp, cva, cqb, ckb, cvb, cgate = attn_project(
        h_ctx, w_in, wq_b, q_lora_g, kv_lora_g, wkv_b, qn_g, kn_g)
    lqp, lkp = apply_rope(lqp, ang_a), apply_rope(lkp, ang_a)
    lqb, lkb = apply_rope(lqb, ang_b), apply_rope(lkb, ang_b)
    lq_a, lk_a = mla_qk(lqn, lqp, lkn, lkp)
    cq_a, ck_a = mla_qk(cqn, cqp, ckn, ckp)
    k_a_all = jnp.concatenate([ck_a, lk_a], axis=1)
    v_a_all = jnp.concatenate([cva, lva], axis=1)
    k_b_all = jnp.concatenate([ckb, lkb], axis=1)
    v_b_all = jnp.concatenate([cvb, lvb], axis=1)
    y_a = block_attention(lq_a, k_a_all, v_a_all, A_SCALE)
    y_b = block_attention(lqb.reshape(b, s, B_KV_HEADS, B_GROUP, B_HEAD_DIM), k_b_all, v_b_all, B_SCALE)
    out_lat = gated_out(y_a, y_b, lgate, w_out)
    out_ctx = None
    if with_ctx_queries:
        lc = h_ctx.shape[1]
        yc_a = block_attention(cq_a, ck_a, cva, A_SCALE)
        yc_b = block_attention(cqb.reshape(b, lc, B_KV_HEADS, B_GROUP, B_HEAD_DIM), ckb, cvb, B_SCALE)
        out_ctx = gated_out(yc_a, yc_b, cgate, w_out)
    return out_lat, out_ctx

def fourier_mixer(h, w_in, w_out):
    b, l, _ = h.shape
    u, gate = jnp.split(h @ w_in, 2, axis=-1)
    ug = u.reshape(b, l, C_GROUPS, C_GROUP_DIM).astype(jnp.float32)
    f = jnp.fft.fft2(ug, axes=(1, 3), norm="ortho").real.astype(h.dtype)
    y = f.reshape(b, l, C_WIDTH) * jax.nn.silu(gate)
    return y @ w_out

def modulation(cvec, ada_w, ada_b):
    m = jax.nn.silu(cvec) @ ada_w + ada_b
    return jnp.split(m, 3, axis=-1)

def modulate(x, shift, scale):
    return layer_norm(x) * (1.0 + scale) + shift

def post_norm(x, out, gate, g, bias):
    return layer_norm(DEEPNORM_ALPHA * x + gate * out) * g + bias

def second_inputs(seed: int = 0) -> dict:
    key = jax.random.key(seed)
    ks = jax.random.split(key, 24)

    def nrm(k, shape, s):
        return jax.random.normal(k, shape, jnp.float32) * s

    def gain(k, shape):
        return 1.0 + 0.02 * jax.random.normal(k, shape, jnp.float32)

    return {
        "x": nrm(ks[0], (BATCH, SEQ, D_MODEL), 1.0),
        "c": nrm(ks[1], (BATCH, D_MODEL), 1.0),
        "ctx": nrm(ks[2], (BATCH, CTX_LEN, D_MODEL), 1.0),
        "c_ctx": nrm(ks[3], (D_MODEL,), 1.0),
        "ada_w": nrm(ks[4], (DEPTH_2, D_MODEL, 3 * D_MODEL), 0.5 * D_MODEL ** -0.5),
        "ada_b": nrm(ks[5], (DEPTH_2, 3 * D_MODEL), 0.01),
        "ln_g": gain(ks[6], (DEPTH_2, D_MODEL)),
        "ln_b": nrm(ks[7], (DEPTH_2, D_MODEL), 0.01),
        "w_in_attn": nrm(ks[8], (N_EVEN, D_MODEL, ATTN_IN), D_MODEL ** -0.5),
        "wq_b": nrm(ks[9], (N_EVEN, A_Q_LORA, A_HEADS * (A_NOPE + A_ROPE)), A_Q_LORA ** -0.5),
        "q_lora_norm": gain(ks[10], (N_EVEN, A_Q_LORA)),
        "kv_lora_norm": gain(ks[11], (N_EVEN, A_KV_LORA)),
        "wkv_b": nrm(ks[12], (N_EVEN, A_KV_LORA, A_HEADS * (A_NOPE + A_V)), A_KV_LORA ** -0.5),
        "q_norm_b": gain(ks[13], (N_EVEN, B_HEAD_DIM)),
        "k_norm_b": gain(ks[14], (N_EVEN, B_HEAD_DIM)),
        "w_out_attn": nrm(ks[15], (N_EVEN, ATTN_WIDTH_2, D_MODEL), DEEPNORM_BETA * ATTN_WIDTH_2 ** -0.5),
        "w_in_fourier": nrm(ks[16], (N_ODD, D_MODEL, 2 * C_WIDTH), D_MODEL ** -0.5),
        "w_out_fourier": nrm(ks[17], (N_ODD, C_WIDTH, D_MODEL), DEEPNORM_BETA * C_WIDTH ** -0.5),
    }

def second_block(x, c, ctx, c_ctx, ada_w, ada_b, ln_g, ln_b, w_in_attn, wq_b, q_lora_norm,
              kv_lora_norm, wkv_b, q_norm_b, k_norm_b, w_out_attn, w_in_fourier, w_out_fourier):
    rows = x.shape[1] // GRID_W
    ang_a = axial_rope_angles(rows, A_ROPE)
    ang_b = axial_rope_angles(rows, B_HEAD_DIM)
    xc = ctx
    for i in range(DEPTH_2):
        j = i // 2
        ctx_needed = i < DEPTH_2 - 1
        sh_l, sc_l, g_l = [m[:, None, :] for m in modulation(c, ada_w[i], ada_b[i])]
        h_lat = modulate(x, sh_l, sc_l)
        o_ctx = None
        g_c = None
        if i % 2 == 0:
            sh_c, sc_c, g_c = modulation(c_ctx, ada_w[i], ada_b[i])
            h_ctx = modulate(xc, sh_c, sc_c)
            o_lat, o_ctx = attention_mixer(
                h_lat, h_ctx, ang_a, ang_b, w_in_attn[j], wq_b[j], q_lora_norm[j],
                kv_lora_norm[j], wkv_b[j], q_norm_b[j], k_norm_b[j], w_out_attn[j], ctx_needed)
        else:
            o_lat = fourier_mixer(h_lat, w_in_fourier[j], w_out_fourier[j])
            if ctx_needed:
                sh_c, sc_c, g_c = modulation(c_ctx, ada_w[i], ada_b[i])
                o_ctx = fourier_mixer(modulate(xc, sh_c, sc_c), w_in_fourier[j], w_out_fourier[j])
        x = post_norm(x, o_lat, g_l, ln_g[i], ln_b[i])
        if ctx_needed:
            xc = post_norm(xc, o_ctx, g_c, ln_g[i], ln_b[i])
    return x


def setup_inputs(seed=0):
    out = dict(first_inputs(seed))
    for name, value in second_inputs(seed + 1).items():
        if name != "x":
            out[name + "_2"] = value
    return out


def reference(
    x, c, w_ada, b_ada, norm1_w, w_in, ssm_a_re, ssm_a_im, ssm_log_dt, ssm_b_re, ssm_b_im,
    ssm_c_re, ssm_c_im, ssm_d, ssm_w_glu, q_norm_w, k_norm_w, w_out, norm2_w, w_ffn_gate,
    w_ffn_up, w_ffn_down, c_2, ctx_2, c_ctx_2, ada_w_2, ada_b_2, ln_g_2, ln_b_2, w_in_attn_2,
    wq_b_2, q_lora_norm_2, kv_lora_norm_2, wkv_b_2, q_norm_b_2, k_norm_b_2, w_out_attn_2,
    w_in_fourier_2, w_out_fourier_2,
):
    x = first_block(
        x, c, w_ada, b_ada, norm1_w, w_in, ssm_a_re, ssm_a_im, ssm_log_dt, ssm_b_re, ssm_b_im,
        ssm_c_re, ssm_c_im, ssm_d, ssm_w_glu, q_norm_w, k_norm_w, w_out, norm2_w, w_ffn_gate,
        w_ffn_up, w_ffn_down,
    )
    return second_block(
        x, c_2, ctx_2, c_ctx_2, ada_w_2, ada_b_2, ln_g_2, ln_b_2, w_in_attn_2, wq_b_2,
        q_lora_norm_2, kv_lora_norm_2, wkv_b_2, q_norm_b_2, k_norm_b_2, w_out_attn_2,
        w_in_fourier_2, w_out_fourier_2,
    )


_drawn_inputs = setup_inputs


def setup_inputs(seed=0):
    import zlib

    import numpy as np

    out = dict(_drawn_inputs(seed))
    spreads = {}
    factors = {'norm1_w': 8.0,
     'ssm_a_re': 64.0,
     'ssm_a_im': 64.0,
     'ssm_log_dt': 64.0,
     'ssm_b_re': 64.0,
     'ssm_b_im': 64.0,
     'ssm_c_re': 64.0,
     'ssm_c_im': 64.0,
     'q_norm_w': 8.0,
     'k_norm_w': 8.0,
     'norm2_w': 8.0,
     'ctx_2': 8.0,
     'c_ctx_2': 5.682,
     'ada_b_2': 8.0,
     'ln_b_2': 4.135,
     'w_in_attn_2': 3.416,
     'wq_b_2': 8.0,
     'q_lora_norm_2': 8.0,
     'kv_lora_norm_2': 8.0,
     'wkv_b_2': 5.081,
     'q_norm_b_2': 24.734,
     'k_norm_b_2': 26.119,
     'w_out_attn_2': 3.517}
    for name, (base, spread) in spreads.items():
        noise = np.random.default_rng([zlib.crc32(name.encode()), seed]).standard_normal(out[name].shape)
        drawn = base * np.exp(spread * noise) if base else spread * noise
        out[name] = __import__('jax').numpy.asarray(drawn.astype(out[name].dtype))
    for name, factor in factors.items():
        out[name] = (out[name] * factor).astype(out[name].dtype)
    return out
```

```python
from contextlib import ExitStack

import numpy as np

import concourse.bass as bass
from concourse import mybir

P = 128
D = 2048
S = 256
TT = S // P
KT = D // P
CW = 512
F32 = mybir.dt.float32
F32R = mybir.dt.float32r
ACT = mybir.ActivationFunctionType
ALU = mybir.AluOpType
AX = mybir.AxisListType.X

SSM_W = 1024
GROUPS, STATE, GCH = 64, 64, 16
PAIRS = GROUPS // 2
HEADS, HD = 8, 128
FFN = 5632
FFN_CH = FFN // CW
QL, KVL, ROPE = 768, 512, 64
LN_EPS = RMS_EPS = 1e-6
ALPHA = 4.0 ** 0.25
A_SCALE = (128 + 64) ** -0.5
B_SCALE = 128 ** -0.5
FCH = 8

RING = 8
SPLITS = 4
UPC = KT // 2

U_IN = 0
U_GLU = U_IN + 8 * UPC
U_OUT = U_GLU + 8
U_FFN = U_OUT + 4 * UPC
U_AIN = U_FFN + FFN_CH * 24
U_PAIR = U_AIN + 11 * UPC
U_AOUT = U_PAIR + 4 * 8
U_FOU = U_AOUT + 4 * UPC

COLS = {}
_o = 0
for _n, _w in (("c", 16), ("c2", 16), ("cctx", 16), ("n1", 16), ("n2", 16), ("bada", 96), ("bada2", 96), ("qn", 1),
               ("kn", 1), ("ssmd", 8), ("ql", 6), ("kvl", 4), ("are", 32), ("aim", 32), ("ldt", 32), ("slope", 8)):
    COLS[_n] = slice(_o, _o + _w)
    _o += _w
NCOLS = _o


def at(n, per=0, i=None):
    return n if i is None else i * per + n


class Chain:

    def __init__(self, eng, sem):
        self.eng, self.sem, self.n, self.i, self.lo, self.per, self.n0 = eng, sem, 0, None, 0, 0, 0

    def __call__(self, ins):
        ins.then_inc(self.sem, 1)
        self.n += 1

    def wait(self):
        if self.i is None:
            self.eng.wait_ge(self.sem, self.n)
        else:
            self.eng.wait_ge(self.sem, self.i * self.per + (self.n - self.lo * self.per))

    def enter(self, i, lo, per):
        self.i, self.lo, self.per, self.n0 = i, lo, per, self.n

    def leave(self, hi):
        assert self.n - self.n0 == self.per, (self.n - self.n0, self.per)
        self.n = self.n0 + self.per * (hi - self.lo)
        self.i = None


def acc_ops(q):
    return 16 * q + 16 * max(0, min(q, 32) - 24)


def program(nc, dram, out):
    ctx = ExitStack()
    sem_names = {}

    def sem(name):
        if name not in sem_names:
            sem_names[name] = ctx.enter_context(nc.semaphore(name))
        return sem_names[name]

    def sb(stack, name, shape, dt=F32):
        return stack.enter_context(nc.sbuf_tensor(name, shape, dt))

    raw = sb(ctx, "raw", [P, RING, 2, CW])
    whi = sb(ctx, "whi", [P, SPLITS, 2, CW], F32R)
    wlo = sb(ctx, "wlo", [P, SPLITS, 2, CW], F32R)
    araw = sb(ctx, "araw", [P, 2, 4, CW])
    acc = sb(ctx, "acc", [P, 2, CW])
    accx = sb(ctx, "accx", [P, 2, CW])
    hh = sb(ctx, "hh", [P, KT, S], F32R)
    hl = sb(ctx, "hl", [P, KT, S], F32R)
    x = sb(ctx, "x", [P, TT, D])
    xacc = sb(ctx, "xacc", [P, TT, D])
    ident = sb(ctx, "ident", [P, P])
    ones = sb(ctx, "ones", [P, P])
    cols = sb(ctx, "cols", [P, NCOLS])
    cond = sb(ctx, "cond", [P, 48])
    modc = sb(ctx, "modc", [P, 192])
    modx = sb(ctx, "modx", [P, 32])
    mscalex = sb(ctx, "mscalex", [P, KT])
    mscale = sb(ctx, "mscale", [P, KT])
    stat = sb(ctx, "stat", [P, TT, 4, 6])
    mv = sb(ctx, "mv", [P, TT, 2])
    rstd = sb(ctx, "rstd", [P, TT, 1])
    ms = sb(ctx, "ms", [P, TT, 1])
    mhalf = sb(ctx, "mhalf", [P, 32])

    psum = ctx.enter_context(nc.psum_tensor("psum", [P, 8, CW], F32))

    h32 = sb(ctx, "h32", [P, 2, 2, S])
    aim2 = sb(ctx, "aim2", [P, 2, 2, PAIRS])
    msq = sb(ctx, "msq", [P, TT, 16])
    rqk = sb(ctx, "rqk", [P, TT, 16])
    neg = sb(ctx, "neg", [P, TT])
    den = sb(ctx, "den", [P, TT])
    rden = sb(ctx, "rden", [P, 2, TT])
    qcol = sb(ctx, "qcol", [P, 1])

    m = ExitStack()
    proj = sb(m, "proj", [P, TT, 4096])
    hB = sb(m, "hB", [P, 2, 8, S])
    BT = sb(m, "BT", [P, 2, 8, P])
    m.close()
    row1 = proj[:, 1, 1024:3072]
    hA = xacc[:].rearrange("p a b -> p (a b)").rearrange("p (r g t) -> p r g t", r=2, g=8)

    s_raw = [sem(f"raw_landed{j}") for j in range(RING)]
    s_araw = [sem(f"ada_landed{j}") for j in range(2)]
    s_hi, s_lo, s_mm = sem("unit_high"), sem("unit_low"), sem("unit_used")
    s_acc, s_red, s_mod = sem("ada_ops"), sem("ada_reduced"), sem("mod_ready")
    block = ctx.enter_context(nc.Block())

    def w_rows(w, kt, kn):
        return w.rearrange("(k p) n -> p k n", p=P)[:, kt:kt + kn]

    def load(sp, u, src, w=CW, per=0, i=None):
        kn = src.shape[1]
        if i is not None or u >= RING:
            sp.wait_ge(s_lo, at(u - RING + 1, per, i))
        sp.dma_start(raw[:, u % RING, 0:kn, 0:w], src).then_inc(s_raw[u % RING], 16)

    def high(act, u, w=CW, kn=2, per=0, i=None):
        act.wait_ge(s_raw[u % RING], at(16 * (u // RING + 1), 16 * (per // RING), i))
        if i is not None or u >= SPLITS:
            act.wait_ge(s_mm, at(u - SPLITS + 1, per, i))
        nc.scalar.copy(whi[:, u % SPLITS, 0:kn, 0:w], raw[:, u % RING, 0:kn, 0:w]).then_inc(s_hi, 1)

    def low(dve, u, w=CW, kn=2, per=0, i=None):
        dve.wait_ge(s_hi, at(u + 1, per, i))
        if i is not None or u >= SPLITS:
            dve.wait_ge(s_mm, at(u - SPLITS + 1, per, i))
        nc.vector.tensor_tensor(wlo[:, u % SPLITS, 0:kn, 0:w], raw[:, u % RING, 0:kn, 0:w],
                                whi[:, u % SPLITS, 0:kn, 0:w].bitcast(F32), ALU.subtract).then_inc(s_lo, 1)

    def multiply(pe, u, tiles, kt, last_kt, w=CW, kn=2, per=0, i=None, first_kt=0):
        pe.wait_ge(s_lo, at(u + 1, per, i))
        for k in range(kn):
            for ah, al, t, bank in tiles:
                o = psum[:, bank, 0:w]
                a = slice(t * P, t * P + P)
                h, lw = whi[:, u % SPLITS, k, 0:w], wlo[:, u % SPLITS, k, 0:w]
                nc.tensor.matmul(o, ah[:, kt + k, a], h, start=(kt + k == first_kt), stop=False)
                nc.tensor.matmul(o, ah[:, kt + k, a], lw, start=False, stop=False)
                ins = nc.tensor.matmul(o, al[:, kt + k, a], h, start=False, stop=(kt + k == last_kt))
        ins.then_inc(s_mm, 1)

    def lat(b0):
        return [(hh, hl, t, b0 + t) for t in range(TT)]

    def ada_src(q, perq=0, i=None):
        if q < 24:
            w, c = dram["w_ada"][0], q
        elif q < 36:
            w, c = dram["ada_w_2"][0], q - 24
        else:
            w, c = dram["ada_w_2"][1], q - 36
        return w.rearrange("(k p) n -> p k n", p=P), at(c * CW, perq * CW, i)

    def ada_load(sp, q, jj, perq=0, i=None):
        src, c = ada_src(q, perq, i)
        r = 2 if 24 <= q < 32 else 1
        done = acc_ops(q) + r * 4 * (jj - 1) if jj >= 2 else acc_ops(q) - (4 if jj == 0 else 0)
        if i is not None or q >= 1 or jj >= 2:
            sp.wait_ge(s_acc, at(done, 16 * r * perq, i))
        sp.dma_start(araw[:, jj % 2], src[:, 4 * jj:4 * jj + 4, bass.ds(c, CW)]).then_inc(s_araw[jj % 2], 16)

    def ada_sum(dve, q, jj, perq=0, i=None):
        both = 24 <= q < 32
        r = 2 if both else 1
        if jj == 0 and (i is not None or q >= 2):
            dve.wait_ge(s_red, at(q - q % 2, perq, i))
        dve.wait_ge(s_araw[jj % 2], at(16 * (2 * q + jj // 2 + 1), 32 * perq, i))
        c0 = 0 if q < 24 else 16
        for kk in range(4):
            kt = 4 * jj + kk
            for n, (a, cc) in enumerate(((acc, c0), (accx, 32))[:r]):
                dst, w, s = a[:, q % 2], araw[:, jj % 2, kk], cond[:, cc + kt:cc + kt + 1]
                if kt == 0:
                    ins = nc.vector.tensor_scalar(dst, w, s, None, ALU.mult)
                else:
                    dve.wait_ge(s_acc, at(acc_ops(q) + r * (kt - 1) + n + 1, 16 * r * perq, i))
                    ins = nc.vector.scalar_tensor_tensor(out=dst, in0=w, scalar=s, in1=dst, op0=ALU.mult, op1=ALU.add)
                ins.then_inc(s_acc, 1)

    def ada_reduce(pe, q, perq=0, i=None):
        both = 24 <= q < 32
        pe.wait_ge(s_acc, at(acc_ops(q + 2), 16 * (2 if both else 1) * perq, i))
        if i is not None or q >= 2:
            pe.wait_ge(s_mod, at(q, perq, i))
        for n, a in enumerate((acc, accx)[:2 if both else 1]):
            for c in range(2):
                for j in range(4):
                    o = 8 * n + 4 * c + j
                    ins = nc.tensor.matmul(psum[:, 7, o:o + 1], a[:, c, j * P:(j + 1) * P], ones[:, 0:1],
                                           start=True, stop=True)
        ins.then_inc(s_red, 2)

    def ada_store(dve, q, perq=0, i=None):
        both = 24 <= q < 32
        dve.wait_ge(s_red, at(q + 2, perq, i))
        bias = cols[:, bass.ds(at(COLS["bada"].start + 4 * q, 4 * perq, i), 8)]
        if both:
            nc.vector.tensor_tensor(modx[:, bass.ds(at(4 * (q - 24), 4 * perq, i), 8)], psum[:, 7, 8:16], bias, ALU.add)
        nc.vector.tensor_tensor(modc[:, bass.ds(at(4 * q, 4 * perq, i), 8)], psum[:, 7, 0:8], bias,
                                ALU.add).then_inc(s_mod, 2)

    s_st, s_rs, s_xn = sem("norm_stats"), sem("norm_rstd"), sem("normed")
    s_tp, s_h32, s_hh, s_hl = sem("turned"), sem("turned32"), sem("turned_high"), sem("turned_low")
    s_turn_mod = sem("turn_factors")

    def norm_dve(dve, ch, k, src, xn, rms):
        for t in range(TT):
            for c in range(4):
                ch(nc.vector.bn_stats(stat[:, t, c], src[:, t, c * CW:(c + 1) * CW]))
        ch.wait()
        for t in range(TT):
            ch(nc.vector.bn_aggr(mv[:, t], stat[:, t].rearrange("p c s -> p (c s)")))
        ch.wait()
        if rms:
            ch(nc.vector.tensor_tensor(ms[:], mv[:, :, 0:1], mv[:, :, 0:1], ALU.mult))
            ch.wait()
            ch(nc.vector.tensor_tensor(ms[:], ms[:], mv[:, :, 1:2], ALU.add))
            ch.wait()
            nc.vector.tensor_scalar(ms[:], ms[:], LN_EPS, None, ALU.add).then_inc(s_st, 1)
        else:
            nc.vector.tensor_scalar(ms[:], mv[:, :, 1:2], LN_EPS, None, ALU.add).then_inc(s_st, 1)
        dve.wait_ge(s_rs, k + 1)
        for t in range(TT):
            if rms:
                ins = nc.vector.tensor_scalar(xn[:, t], src[:, t], rstd[:, t], None, ALU.mult)
            else:
                ins = nc.vector.tensor_scalar(xn[:, t], src[:, t], mv[:, t, 0:1], rstd[:, t], ALU.subtract, ALU.mult)
            ins.then_inc(s_xn, 1)

    def norm_pool(pool, k):
        pool.wait_ge(s_st, k + 1)
        nc.gpsimd.tensor_tensor(rstd[:], ms[:], mhalf[:, 0:2].unsqueeze(2), ALU.pow).then_inc(s_rs, 1)

    def turn_pe(pe, k, xn, kn):
        pe.wait_ge(s_xn, 2 * kn + 2)
        for r in range(8):
            if 8 * k + r >= 2:
                pe.wait_ge(s_h32, 8 * k + r - 1)
            for j in range(2):
                for t in range(TT):
                    kt = 2 * r + j
                    ins = nc.tensor.transpose(psum[:, 4 + r % 2, j * S + t * P:j * S + t * P + P],
                                              xn[:, t, kt * P:(kt + 1) * P], ident[:])
            ins.then_inc(s_tp, 1)

    def turn_dve(dve, k, h32, scale, shift):
        for r in range(8):
            n = 8 * k + r
            dve.wait_ge(s_tp, n + 1)
            if n >= 2:
                dve.wait_ge(s_hl, n - 1)
            for j in range(2):
                kt = 2 * r + j
                ins = nc.vector.tensor_scalar(h32[:, r % 2, j], psum[:, 4 + r % 2, j * S:(j + 1) * S],
                                              scale[:, kt:kt + 1], shift[:, kt:kt + 1], ALU.mult, ALU.add)
            ins.then_inc(s_h32, 1)

    def turn_act(act, k, h32, oh):
        for r in range(8):
            act.wait_ge(s_h32, 8 * k + r + 1)
            nc.scalar.copy(oh[:, 2 * r:2 * r + 2], h32[:, r % 2]).then_inc(s_hh, 1)

    def turn_pool(pool, k, h32, oh, ol):
        for r in range(8):
            pool.wait_ge(s_hh, 8 * k + r + 1)
            nc.gpsimd.tensor_tensor(ol[:, 2 * r:2 * r + 2], h32[:, r % 2], oh[:, 2 * r:2 * r + 2].bitcast(F32),
                                    ALU.subtract).then_inc(s_hl, 1)

    s_diag, s_grow, s_growc = sem("gate_diag"), sem("gate_spread"), sem("gate_row")

    def gate_dve(dve, k, col0, diag):
        for r in range(4):
            n = 4 * k + r
            if n >= 2:
                dve.wait_ge(s_grow, n - 1)
            for j in range(4):
                c = col0 + 4 * r + j
                ins = nc.vector.tensor_scalar(diag[:, r % 2, j * P:(j + 1) * P], ident[:], modc[:, c:c + 1], None,
                                              ALU.mult)
            ins.then_inc(s_diag, 1)

    def gate_pe(pe, k, diag):
        for r in range(4):
            n = 4 * k + r
            pe.wait_ge(s_diag, n + 1)
            if n >= 1:
                pe.wait_ge(s_growc, n)
            nc.tensor.matmul(psum[:, 6], ones[:], diag[:, r % 2], start=True, stop=True).then_inc(s_grow, 1)

    def gate_act(act, k, row):
        for r in range(4):
            act.wait_ge(s_grow, 4 * k + r + 1)
            nc.scalar.copy(row[:, r * CW:(r + 1) * CW], psum[:, 6]).then_inc(s_growc, 1)

    rawf = raw[:].rearrange("p a b c -> p (a b c)")
    arawf = araw[:].rearrange("p a b c -> p (a b c)")
    xn = xacc
    diag = h32[:].rearrange("p a b c -> p a (b c)")

    small = [rawf[:, 32 * n:32 * n + 32] for n in range(24)]
    bpad = rawf[:, 1024:3072].rearrange("p (r g c) -> p r g c", r=2, g=PAIRS)
    bbar = rawf[:, 3072:5120].rearrange("p (r g c) -> p r g c", r=2, g=PAIRS)
    btmp = rawf[:, 5120:6144].rearrange("p (g c) -> p g c", g=PAIRS)
    apow = accx[:].rearrange("p a b -> p (a b)").rearrange("p (r g j) -> p r g j", r=2, g=PAIRS)
    cpad = arawf[:, 0:2048].rearrange("p (r g c) -> p r g c", r=2, g=PAIRS)
    staged = arawf[:, 2048:2560].rearrange("p (t q e) -> p t q e", t=TT, q=2)
    qkT = arawf[:, 2560:3072].rearrange("p (q s) -> p q s", q=2)
    prob = arawf[:, 3072:3584].rearrange("p (t s) -> p t s", t=TT)
    probT = arawf[:, 3584:4096].rearrange("p (k s) -> p k s", k=2)
    dist = rawf[:, 0:512].rearrange("p (t s) -> p t s", t=TT)
    count = rawf[:, 512:1024].rearrange("p (t s) -> p t s", t=TT)
    scan_tmp = {"pool": rawf[:, 1024:4608], "dve": rawf[:, 4608:8192]}

    s_const, s_x, s_sil, s_one = sem("consts_landed"), sem("x_landed"), sem("cond_ready"), sem("ones_set")
    s_b, s_cpad, s_dist = sem("b_landed"), sem("c_landed"), sem("masks_landed")
    s_fun, s_arg = sem("ssm_functions"), sem("ssm_arguments")
    s_bbar, s_bt, s_BT = sem("bbar_ready"), sem("bbar_turned"), sem("BT_ready")
    s_inev = sem("proj_stored")
    s_ut, s_uT = sem("u_turned"), sem("uT_ready")
    s_bu, s_H = sem("bu_summed"), sem("bu_stored")
    s_scan = {"pool": sem("pool_scanned"), "dve": sem("dve_scanned")}
    s_y, s_yv, s_yg, s_yh, s_yl = (sem(n) for n in ("y_summed", "y_skipped", "y_gelu", "y_high", "y_low"))
    s_stg, s_qkt, s_qkT, s_sc, s_mx, s_ex, s_pr, s_pt, s_pT, s_pv, s_ya = (sem("a1_" + n) for n in (
        "staged", "qk_turned", "qkT", "scores", "max", "exp", "prob", "p_turned", "pT", "pv", "y"))
    s_ms, s_rq, s_qc = sem("qk_squares"), sem("qk_rstd"), sem("q_factor")
    s_at, s_ah, s_al = sem("attn_turned"), sem("attn_high"), sem("attn_low")
    s_glu, s_sg, s_gt, s_gy, s_gh, s_gl = (sem("glu_" + n) for n in ("done", "sigmoid", "turned", "y", "high", "low"))
    s_chd, s_chp, s_cha = sem("dve_chain"), sem("pool_chain"), sem("act_chain")
    s_cneg = sem("c_negated")
    s_chd_ssm, s_mh, s_ones = sem("ssm_params"), sem("minus_half"), sem("ones")

    TWO_PI = 2.0 * np.pi
    C1 = 6.28125
    C2 = float(np.float32(np.round((TWO_PI - C1) * 2 ** 20) / 2 ** 20))
    C3 = float(np.float32(TWO_PI - C1 - C2))
    MAGIC = 12582912.0
    PI_IN = float(np.nextafter(np.float32(np.pi), np.float32(0)))

    def ssm_params_dve(dve, ch):
        V = nc.vector
        def tt(o, a, b, op):
            ch(V.tensor_tensor(o, a, b, op))
            ch.wait()
        are, aim = cols[:, COLS["are"]], cols[:, COLS["aim"]]
        dt, lg, th, mag, kk, r, r2, cs, sn, nr, dn, zr, zi, t0, t1 = small[:15]
        dve.wait_ge(s_fun, 1)
        V.tensor_tensor(lg, are, dt, ALU.mult).then_inc(s_arg, 1)
        tt(th, aim, dt, ALU.mult)
        ch(V.tensor_scalar(kk, th, float(np.float32(1 / TWO_PI)), MAGIC, ALU.mult, ALU.add))
        ch.wait()
        ch(V.tensor_scalar(kk, kk, MAGIC, None, ALU.subtract))
        ch.wait()
        for n, (c, a) in enumerate(((C1, th), (C2, r), (C3, r))):
            ch(V.scalar_tensor_tensor(out=r, in0=kk, scalar=-c, in1=a, op0=ALU.mult, op1=ALU.add))
            ch.wait()
        ch(V.tensor_scalar(r, r, PI_IN, -PI_IN, ALU.min, ALU.max))
        ch.wait()
        ch(V.scalar_tensor_tensor(out=r2, in0=r, scalar=-1.0, in1=r, op0=ALU.mult, op1=ALU.max))
        ch.wait()
        V.tensor_scalar(r2, r2, -1.0, float(np.pi / 2), ALU.mult, ALU.add).then_inc(s_arg, 1)
        dve.wait_ge(s_fun, 4)
        ar, ai = apow[:, 0, :, 0], apow[:, 1, :, 0]
        tt(ar, mag, cs, ALU.mult)
        tt(ai, mag, sn, ALU.mult)
        ch(V.tensor_scalar(nr, ar, 1.0, None, ALU.subtract))
        tt(t0, are, are, ALU.mult)
        tt(t1, aim, aim, ALU.mult)
        tt(dn, t0, t1, ALU.add)
        ch(V.reciprocal(dn, dn))
        tt(t0, nr, are, ALU.mult)
        tt(t1, ai, aim, ALU.mult)
        tt(zr, t0, t1, ALU.add)
        tt(zr, zr, dn, ALU.mult)
        tt(t0, ai, are, ALU.mult)
        tt(t1, nr, aim, ALU.mult)
        tt(zi, t0, t1, ALU.subtract)
        tt(zi, zi, dn, ALU.mult)
        zrb, zib = (z.unsqueeze(2).broadcast_to([P, PAIRS, 2 * GCH]) for z in (zr, zi))
        dve.wait_ge(s_b, 16)
        tt(bbar[:, 0], zrb, bpad[:, 0], ALU.mult)
        tt(btmp, zib, bpad[:, 1], ALU.mult)
        tt(bbar[:, 0], bbar[:, 0], btmp, ALU.subtract)
        tt(bbar[:, 1], zrb, bpad[:, 1], ALU.mult)
        tt(btmp, zib, bpad[:, 0], ALU.mult)
        V.tensor_tensor(bbar[:, 1], bbar[:, 1], btmp, ALU.add).then_inc(s_bbar, 1)
        for n in (1, 2, 4, 8):
            br, bi = (apow[:, q, :, n - 1:n].broadcast_to([P, PAIRS, n]) for q in range(2))
            pr, pi = apow[:, 0, :, 0:n], apow[:, 1, :, 0:n]
            ta, tb = (rawf[:, 6144 + 512 * q:6144 + 512 * q + PAIRS * n].rearrange("p (g j) -> p g j", g=PAIRS)
                      for q in range(2))
            tt(ta, pr, br, ALU.mult)
            tt(tb, pi, bi, ALU.mult)
            tt(apow[:, 0, :, n:2 * n], ta, tb, ALU.subtract)
            tt(ta, pr, bi, ALU.mult)
            tt(tb, pi, br, ALU.mult)
            tt(apow[:, 1, :, n:2 * n], ta, tb, ALU.add)
        for e, j in enumerate((0, 15)):
            ch(V.tensor_scalar(aim2[:, e, 1], apow[:, 1, :, j], -1.0, None, ALU.mult))
            ch(V.tensor_copy(aim2[:, e, 0], apow[:, 1, :, j]))
        ch.wait()

    def ssm_params_act(act):
        act.wait_ge(s_const, 16)
        nc.scalar.activation(small[0], cols[:, COLS["ldt"]], ACT.Exp).then_inc(s_fun, 1)
        act.wait_ge(s_arg, 1)
        nc.scalar.activation(small[3], small[1], ACT.Exp).then_inc(s_fun, 1)
        act.wait_ge(s_arg, 2)
        nc.scalar.activation(small[8], small[5], ACT.Sin).then_inc(s_fun, 1)
        nc.scalar.activation(small[7], small[6], ACT.Sin).then_inc(s_fun, 1)

    def bbar_turn_pe(pe):
        pe.wait_ge(s_bbar, 1)
        for n in range(4):
            if n >= 2:
                pe.wait_ge(s_BT, n - 1)
            for j in range(4):
                st = 4 * (n % 2) + j
                ins = nc.tensor.transpose(psum[:, n % 2, j * P:(j + 1) * P], bbar[:, n // 2, 4 * st:4 * st + 4]
                                          .rearrange("p g c -> p (g c)"), ident[:])
            ins.then_inc(s_bt, 1)

    def bbar_turn_act(act):
        for n in range(4):
            act.wait_ge(s_bt, n + 1)
            nc.scalar.copy(BT[:, n // 2, 4 * (n % 2):4 * (n % 2) + 4], psum[:, n % 2]
                           .rearrange("p (a b) -> p a b", a=4)).then_inc(s_BT, 1)

    def uT(a, n=1):
        return proj[:, a // 4, (a % 4) * S:(a % 4 + n) * S].rearrange("p (f s) -> p f s", f=n)

    def u_turn_pe(pe):
        pe.wait_ge(s_inev, 8)
        pe.wait_ge(s_mod, 16)
        for r in range(4):
            for j in range(2):
                for t in range(TT):
                    ft = 2 * r + j
                    ins = nc.tensor.transpose(psum[:, 4 + r, j * S + t * P:j * S + t * P + P],
                                              proj[:, t, ft * P:(ft + 1) * P], ident[:])
            ins.then_inc(s_ut, 1)

    def u_turn_act(act):
        for r in range(4):
            act.wait_ge(s_ut, 4)
            nc.scalar.copy(uT(2 * r, 2), psum[:, 4 + r].rearrange("p (a b) -> p a b", a=2)
                           ).then_inc(s_uT, 1)

    def bu_pe(pe, q):
        for st in (2 * q, 2 * q + 1):
            pe.wait_ge(s_uT, 4)
            if st >= 1:
                pe.wait_ge(s_H, st)
            for pp in range(4):
                rows = slice(32 * pp, 32 * pp + 32)
                for ri in range(2):
                    ins = nc.tensor.matmul(psum[:, 4 + pp, ri * S:(ri + 1) * S], BT[rows, ri, st], uT(st)[rows, 0],
                                           start=True, stop=True)
            ins.then_inc(s_bu, 1)

    def bu_act(act, q):
        h = (hA, hB)[q % 2]
        if q == 1:
            act.wait_ge(s_ms, 1)
        if q >= 2:
            act.wait_ge(s_y, q - 1)
        for st in (2 * q, 2 * q + 1):
            act.wait_ge(s_bu, st + 1)
            for ri in range(2):
                ins = nc.scalar.copy(h[:, ri, 4 * (st % 2):4 * (st % 2) + 4],
                                     psum[:, 4:8, ri * S:(ri + 1) * S])
            ins.then_inc(s_H, 1)

    def scan(eng, isa, ch, q, who):
        h = (hA, hB)[q % 2]
        hv = h.rearrange("p r g (c j) -> p r g c j", j=16)
        g = slice(8 * q, 8 * q + 8)
        T = scan_tmp[who]
        eng.wait_ge(s_H, 2 * q + 2)

        def tt(o, a, b, op):
            ch(isa.tensor_tensor(o, a, b, op))
            ch.wait()

        def advance(e, prev, nxt, t0, t1, wide):
            ar = apow[:, 0:1, g, 15 * e:15 * e + 1].rearrange("p r g j -> p r (g j)").broadcast_to([P, 2, 8])
            ai = aim2[:, e, :, g]
            if wide:
                ar, ai = ar.unsqueeze(3).broadcast_to([P, 2, 8, 16]), ai.unsqueeze(3).broadcast_to([P, 2, 8, 16])
            ch(isa.tensor_tensor(t0, ar, prev, ALU.mult))
            tt(t1[:, ::-1], ai, prev, ALU.mult)
            tt(t0, t0, t1, ALU.add)
            tt(nxt, nxt, t0, ALU.add)

        t0 = T[:, 0:256].rearrange("p (r g c) -> p r g c", r=2, g=8)
        t1 = T[:, 256:512].rearrange("p (r g c) -> p r g c", r=2, g=8)
        with eng.Fori(1, 16) as j:
            ch.enter(j, 1, 4)
            prev = hv[:, :, :, :, bass.ds(j - 1, 1)].rearrange("p r g c j -> p r g (c j)")
            nxt = hv[:, :, :, :, bass.ds(j, 1)].rearrange("p r g c j -> p r g (c j)")
            advance(0, prev, nxt, t0, t1, True)
            ch.leave(16)
        t0, t1 = (t.rearrange("p r g c -> p (r g c)")[:, 0:16].rearrange("p (r g) -> p r g", r=2) for t in (t0, t1))
        with eng.Fori(1, 16) as c:
            ch.enter(c, 1, 4)
            prev = h[:, :, :, bass.ds(c * 16 - 1, 1)].rearrange("p r g t -> p r (g t)")
            nxt = h[:, :, :, bass.ds(c * 16 + 15, 1)].rearrange("p r g t -> p r (g t)")
            advance(1, prev, nxt, t0, t1, False)
            ch.leave(16)
        t = T[:, 0:8 * 225].rearrange("p (g c j) -> p g c j", g=8, c=15)
        for ro, pi, ei, op in ((0, 0, 0, ALU.add), (0, 1, 1, ALU.subtract), (1, 0, 1, ALU.add), (1, 1, 0, ALU.add)):
            pw = apow[:, pi, g, 0:15].unsqueeze(2).broadcast_to([P, 8, 15, 15])
            end = hv[:, ei, :, 0:15, 15:16].broadcast_to([P, 8, 15, 15])
            tt(t, pw, end, ALU.mult)
            o = hv[:, ro, :, 1:16, 0:15]
            tt(o, o, t, op)
        isa.tensor_copy(T[:, 0:1], T[:, 1:2]).then_inc(s_scan[who], 1)

    def y_pe(pe, q):
        pe.wait_ge(s_scan[("pool", "dve")[q % 2]], q // 2 + 1)
        if q == 0:
            pe.wait_ge(s_cneg, 1)
            pe.wait_ge(s_ya, 8)
        if q == 2:
            pe.wait_ge(s_al, 4)
        h = (hA, hB)[q % 2]
        for sl in range(2):
            for pp in range(4):
                for ri in range(2):
                    ins = nc.tensor.matmul(psum[32 * pp:32 * pp + 32, q, sl * S:(sl + 1) * S],
                                           cpad[:, ri, 8 * q + 4 * sl + pp], h[:, ri, 4 * sl + pp],
                                           start=(ri == 0), stop=(ri == 1))
        ins.then_inc(s_y, 1)

    def y_dve(dve, q):
        dve.wait_ge(s_y, q + 1)
        for sl in range(2):
            st = 2 * q + sl
            d = cols[:, COLS["ssmd"].start + st:COLS["ssmd"].start + st + 1]
            ins = nc.vector.scalar_tensor_tensor(out=uT(st)[:, 0], in0=uT(st)[:, 0], scalar=d,
                                                 in1=psum[:, q, sl * S:(sl + 1) * S], op0=ALU.mult, op1=ALU.add)
        ins.then_inc(s_yv, 1)

    def y_act(act, q):
        act.wait_ge(s_yv, q + 1)
        y = uT(2 * q, 2)
        nc.scalar.activation(y, y, ACT.Gelu_apprx_tanh).then_inc(s_yg, 1)
        act.wait_ge(s_yg, q + 1)
        nc.scalar.copy(hh[:, 2 * q:2 * q + 2], y).then_inc(s_yh, 1)

    def y_low(dve, q):
        dve.wait_ge(s_yh, q + 1)
        nc.vector.tensor_tensor(hl[:, 2 * q:2 * q + 2], uT(2 * q, 2), hh[:, 2 * q:2 * q + 2].bitcast(F32),
                                ALU.subtract).then_inc(s_yl, 1)

    def a1_norms_dve(dve, ch):
        dve.wait_ge(s_inev, 8)
        sq = hB[:].rearrange("p r g t -> p (r g t)")
        for t in range(TT):
            o = sq[:, 2048 * t:2048 * t + 2048]
            ch(nc.vector.tensor_tensor(o, proj[:, t, 1024:3072], proj[:, t, 1024:3072], ALU.mult))
            ch.wait()
            ch(nc.vector.tensor_reduce(msq[:, t], o.rearrange("p (h e) -> p h e", h=16), AX, ALU.add))
        ch.wait()
        nc.vector.tensor_scalar(msq[:], msq[:], 1.0 / HD, RMS_EPS, ALU.mult, ALU.add).then_inc(s_ms, 1)
        nc.vector.tensor_scalar(qcol[:], cols[:, COLS["qn"]], HD ** -0.5, None, ALU.mult).then_inc(s_qc, 1)
        dve.wait_ge(s_rq, 1)
        for t in range(TT):
            v = proj[:, t, 1024:3072].rearrange("p (h e) -> p h e", h=16)
            ins = nc.vector.tensor_tensor(v, v, rqk[:, t].unsqueeze(2).broadcast_to([P, 16, HD]), ALU.mult)
        ins.then_inc(s_ms, 1)

    def a1_norms_pool(pool):
        pool.wait_ge(s_ms, 1)
        e = mhalf[:].rearrange("p (t h) -> p t h", t=TT)
        nc.gpsimd.tensor_tensor(rqk[:], msq[:], e, ALU.pow).then_inc(s_rq, 1)

    qk = proj[:, :, 1024:3072].rearrange("p t (q n) -> p t q n", q=2)

    def a1_stage_act(act, h, i=None):
        if i is not None or h >= 1:
            act.wait_ge(s_qkt, at(h, 1, i))
        nc.scalar.copy(staged, qk[:, :, :, bass.ds(at(h * HD, HD, i), HD)]).then_inc(s_stg, 1)

    def a1_turn_pe(pe, h, i=None):
        pe.wait_ge(s_stg, at(h + 1, 1, i))
        if i is not None or h >= 1:
            pe.wait_ge(s_qkT, at(h, 1, i))
        for qq in range(2):
            for t in range(TT):
                ins = nc.tensor.transpose(psum[:, 0, qq * S + t * P:qq * S + t * P + P], staged[:, t, qq], ident[:])
        ins.then_inc(s_qkt, 1)

    def a1_qkT_act(act, h, i=None):
        act.wait_ge(s_qkt, at(h + 1, 1, i))
        if i is not None or h >= 1:
            act.wait_ge(s_sc, at(h, 1, i))
        nc.scalar.activation(qkT[:, 0], psum[:, 0, 0:S], ACT.Copy, scale=qcol[:, 0:1])
        nc.scalar.activation(qkT[:, 1], psum[:, 0, S:2 * S], ACT.Copy, scale=cols[:, COLS["kn"]]).then_inc(s_qkT, 1)

    def a1_scores_pe(pe, h, i=None):
        pe.wait_ge(s_qkT, at(h + 1, 1, i))
        if i is not None or h >= 1:
            pe.wait_ge(s_mx, at(h, 1, i))
        for t in range(TT):
            ins = nc.tensor.matmul(psum[:, 1, t * S:(t + 1) * S], qkT[:, 0, t * P:(t + 1) * P], qkT[:, 1],
                                   start=True, stop=True)
        ins.then_inc(s_sc, 1)

    def a1_max_dve(dve, ch, h, i=None):
        dve.wait_ge(s_sc, at(h + 1, 1, i))
        if i is not None or h >= 1:
            dve.wait_ge(s_pt, at(h, 1, i))
        sl = cols[:, bass.ds(at(COLS["slope"].start + h, 1, i), 1)]
        ch(nc.vector.scalar_tensor_tensor(out=prob.rearrange("p t s -> p (t s)"), in0=dist.rearrange("p t s -> p (t s)"),
                                          scalar=sl, in1=psum[:, 1], op0=ALU.mult, op1=ALU.add))
        ch.wait()
        ch(nc.vector.tensor_reduce(neg[:], prob, AX, ALU.max))
        ch.wait()
        nc.vector.tensor_scalar(neg[:], neg[:], -1.0, None, ALU.mult).then_inc(s_mx, 1)

    def a1_exp_act(act, h, i=None):
        act.wait_ge(s_mx, at(h + 1, 1, i))
        for t in range(TT):
            ins = nc.scalar.activation(prob[:, t], prob[:, t], ACT.Exp, bias=neg[:, t:t + 1])
        ins.then_inc(s_ex, 1)

    def a1_prob_dve(dve, ch, h, i=None):
        dve.wait_ge(s_ex, at(h + 1, 1, i))
        ch(nc.vector.tensor_tensor(prob, prob, count, ALU.mult))
        ch.wait()
        ch(nc.vector.tensor_reduce(den[:], prob, AX, ALU.add))
        ch.wait()
        nc.vector.reciprocal(rden[:, 0], den[:]).then_inc(s_pr, 1)

    def a1_pturn_pe(pe, h, i=None):
        pe.wait_ge(s_pr, at(h + 1, 1, i))
        if i is not None or h >= 1:
            pe.wait_ge(s_pT, at(h, 1, i))
        for kt in range(2):
            for t in range(TT):
                ins = nc.tensor.transpose(psum[:, 2, kt * S + t * P:kt * S + t * P + P],
                                          prob[:, t, kt * P:(kt + 1) * P], ident[:])
        ins.then_inc(s_pt, 1)

    def a1_pT_act(act, h, i=None):
        act.wait_ge(s_pt, at(h + 1, 1, i))
        if i is not None or h >= 1:
            act.wait_ge(s_pv, at(h, 1, i))
        nc.scalar.copy(probT, psum[:, 2].rearrange("p (k s) -> p k s", k=2)).then_inc(s_pT, 1)

    def a1_pv_pe(pe, h, i=None):
        pe.wait_ge(s_pT, at(h + 1, 1, i))
        if i is not None or h >= 1:
            pe.wait_ge(s_ya, at(h, 1, i))
        for t in range(TT):
            for kt in range(t + 1):
                ins = nc.tensor.matmul(psum[:, 3, t * P:(t + 1) * P], probT[:, kt, t * P:(t + 1) * P],
                                       proj[:, kt, bass.ds(at(3072 + h * HD, HD, i), HD)], start=(kt == 0), stop=(kt == t))
        ins.then_inc(s_pv, 1)

    def a1_y_dve(dve, h, i=None):
        dve.wait_ge(s_pv, at(h + 1, 1, i))
        for t in range(TT):
            ins = nc.vector.tensor_scalar(proj[:, t, bass.ds(at(1024 + h * HD, HD, i), HD)], psum[:, 3, t * P:(t + 1) * P],
                                          rden[:, 0, t:t + 1], None, ALU.mult)
        ins.then_inc(s_ya, 1)

    def a1_pe(pe):
        a1_turn_pe(pe, 0)
        a1_scores_pe(pe, 0)

        def step(h, i, last=False):
            if not last:
                a1_turn_pe(pe, h + 1, i)
            a1_pturn_pe(pe, h, i)
            if not last:
                a1_scores_pe(pe, h + 1, i)
            a1_pv_pe(pe, h, i)
        step(0, None)
        with pe.Fori(1, HEADS - 1) as i:
            step(0, i)
        step(HEADS - 1, None, True)

    def a1_act(act):
        act.wait_ge(s_ms, 2)
        act.wait_ge(s_qc, 1)
        a1_stage_act(act, 0)
        a1_qkT_act(act, 0)
        a1_stage_act(act, 1)
        a1_exp_act(act, 0)

        def step(h, i, left=2):
            if left > 0:
                a1_qkT_act(act, h + 1, i)
            a1_pT_act(act, h, i)
            if left > 1:
                a1_stage_act(act, h + 2, i)
            if left > 0:
                a1_exp_act(act, h + 1, i)
        step(0, None)
        with act.Fori(1, HEADS - 2) as i:
            step(0, i)
        step(HEADS - 2, None, 1)
        step(HEADS - 1, None, 0)

    def a1_dve(dve, ch):
        dve.wait_ge(s_dist, 32)
        a1_max_dve(dve, ch, 0)
        a1_prob_dve(dve, ch, 0)

        def step(h, i, last=False):
            if not last:
                a1_max_dve(dve, ch, h + 1, i)
            a1_y_dve(dve, h, i)
            if not last:
                a1_prob_dve(dve, ch, h + 1, i)
        step(0, None)
        with dve.Fori(1, HEADS - 1) as i:
            ch.enter(i, 1, 4)
            step(0, i)
            ch.leave(HEADS - 1)
        step(HEADS - 1, None, True)

    def a1_out_pe(pe):
        pe.wait_ge(s_ya, 8)
        for r in range(4):
            if r >= 2:
                pe.wait_ge(s_al, r - 1)
            for j in range(2):
                for t in range(TT):
                    ft = 2 * r + j
                    ins = nc.tensor.transpose(psum[:, 2 + r % 2, j * S + t * P:j * S + t * P + P],
                                              proj[:, t, 1024 + ft * P:1024 + (ft + 1) * P], ident[:])
            ins.then_inc(s_at, 1)

    def a1_out_act(act):
        for r in range(4):
            act.wait_ge(s_at, r + 1)
            nc.scalar.copy(hh[:, 8 + 2 * r:10 + 2 * r], psum[:, 2 + r % 2].rearrange("p (a b) -> p a b", a=2)
                           ).then_inc(s_ah, 1)

    def a1_out_dve(dve):
        for r in range(4):
            dve.wait_ge(s_ah, r + 1)
            nc.vector.tensor_tensor(hl[:, 8 + 2 * r:10 + 2 * r], psum[:, 2 + r % 2].rearrange("p (a b) -> p a b", a=2),
                                    hh[:, 8 + 2 * r:10 + 2 * r].bitcast(F32), ALU.subtract).then_inc(s_al, 1)

    sg = xacc[:].rearrange("p a (c n) -> p c a n", c=4)

    def glu_sp(sp):
        w = dram["ssm_w_glu"][0]
        for c in range(2):
            for j in range(4):
                load(sp, U_GLU + 4 * c + j, w_rows(w, 2 * j, 2)[:, :, c * CW:(c + 1) * CW])

    def glu_pe(pe):
        pe.wait_ge(s_yl, 4)
        for c in range(2):
            for j in range(4):
                multiply(pe, U_GLU + 4 * c + j, lat(2 * c), 2 * j, 7)
        for c in range(2):
            pe.wait_ge(s_sg, c + 1)
            for r in range(2):
                n = 2 * c + r
                if n >= 2:
                    pe.wait_ge(s_gy, n - 1)
                for j in range(2):
                    for t in range(TT):
                        f = 2 * r + j
                        ins = nc.tensor.transpose(psum[:, 4 + n % 2, j * S + t * P:j * S + t * P + P],
                                                  sg[:, c, t, f * P:(f + 1) * P], ident[:])
                ins.then_inc(s_gt, 1)

    def glu_act(act):
        for n in range(8):
            high(act, U_GLU + n)
        for c in range(2):
            act.wait_ge(s_mm, U_GLU + 4 * c + 4)
            nc.scalar.activation(sg[:, c], psum[:, 2 * c:2 * c + 2], ACT.Sigmoid).then_inc(s_sg, 1)
        for n in range(4):
            act.wait_ge(s_gy, n + 1)
            nc.scalar.copy(hh[:, 2 * n:2 * n + 2], uT(2 * n, 2)).then_inc(s_gh, 1)

    def glu_dve(dve):
        for n in range(8):
            low(dve, U_GLU + n)
        for n in range(5):
            if n < 4:
                dve.wait_ge(s_gt, n + 1)
                v = uT(2 * n, 2)
                nc.vector.tensor_tensor(v, v, psum[:, 4 + n % 2].rearrange("p (a b) -> p a b", a=2),
                                        ALU.mult).then_inc(s_gy, 1)
            if n >= 1:
                k = slice(2 * n - 2, 2 * n)
                dve.wait_ge(s_gh, n)
                nc.vector.tensor_tensor(hl[:, k], uT(2 * n - 2, 2), hh[:, k].bitcast(F32), ALU.subtract).then_inc(s_gl, 1)

    ADA_AFTER = (0, 2, 3, 5, 6, 8, 9, 11)

    def pairs_sp(sp, u0, w, q0, steps, i0=0, c0=0, peel=False):
        def step(i):
            for j in range(2 * UPC):
                load(sp, u0 + j, w_rows(w, 2 * (j % UPC), 2)[:, :, bass.ds(at(c0 + (j // UPC) * CW, 2 * CW, i), CW)],
                     per=2 * UPC, i=i)
                if q0 is not None and j in ADA_AFTER:
                    a = ADA_AFTER.index(j)
                    ada_load(sp, q0 + a // 4, a % 4, 2, i)
        if peel:
            step(None)
        with sp.Fori(int(peel), steps) as i:
            step(i)

    def pairs_act(act, u0, steps, evac, peel=False):
        def step(i, first=False):
            for j in range(2 * UPC):
                if evac and j % UPC == 3 and not (first and j == 3):
                    evac(act, j // UPC - 1, 2, i)
                high(act, u0 + j, per=2 * UPC, i=i)
        step(None, True)
        with act.Fori(1, steps) as i:
            step(i)
        if evac:
            evac(act, 2 * steps - 1, 0, None)

    def pairs_dve(dve, u0, q0, steps, evac=None, ch=None, ch_per=0):
        def step(i, first=False):
            for j in range(2 * UPC):
                if evac and j % UPC == 3 and not (first and j == 3):
                    evac(dve, j // UPC - 1, 2, i)
                low(dve, u0 + j, per=2 * UPC, i=i)
                if q0 is not None and j in ADA_AFTER:
                    a = ADA_AFTER.index(j)
                    ada_sum(dve, q0 + a // 4, a % 4, 2, i)
            if q0 is not None:
                ada_store(dve, q0, 2, i)
        step(None, True)
        with dve.Fori(1, steps) as i:
            if ch:
                ch.enter(i, 1, ch_per)
            step(i)
            if ch:
                ch.leave(steps)
        if evac:
            evac(dve, 2 * steps - 1, 0, None)

    def pairs_pe(pe, u0, q0, steps, s_ev, b0=0):
        def step(i, first=False):
            for j in range(2 * UPC):
                c = j // UPC
                if j % UPC == 0 and not first:
                    pe.wait_ge(s_ev, at(c - 1, 2, i))
                multiply(pe, u0 + j, lat(b0 + 2 * c), 2 * (j % UPC), KT - 1, per=2 * UPC, i=i)
                if j == 2 * UPC - 3 and q0 is not None:
                    ada_reduce(pe, q0, 2, i)
        step(None, True)
        with pe.Fori(1, steps) as i:
            step(i)

    def in_evac(act, c, per, i):
        act.wait_ge(s_mm, at(U_IN + UPC * (c + 1), UPC * per, i))
        b = 2 * (c % 2)
        nc.scalar.copy(proj[:, :, bass.ds(at(c * CW, per * CW, i), CW)], psum[:, b:b + 2]).then_inc(s_inev, 1)

    s_oev, s_om = sem("mixed_added"), sem("mixed_gated")
    mixed_tmp = hB[:].rearrange("p r g t -> p (r g t)")[:, 0:2 * CW].rearrange("p (t n) -> p t n", t=TT)

    def gated(dve, ch, c, per, i, u0, dst, src, scale, s_ev, row, mixed_tmp, b0=0):
        dve.wait_ge(s_mm, at(u0 + UPC * (c + 1), UPC * per, i))
        b = b0 + 2 * (c % 2)
        cs = bass.ds(at(c * CW, per * CW, i), CW)
        ch(nc.vector.tensor_tensor(mixed_tmp, psum[:, b:b + 2], row[:, cs].unsqueeze(1).broadcast_to([P, TT, CW]), ALU.mult))
        ch.wait()
        nc.vector.scalar_tensor_tensor(out=dst[:, :, cs], in0=src[:, :, cs], scalar=scale, in1=mixed_tmp,
                                       op0=ALU.mult, op1=ALU.add).then_inc(s_ev, 1)

    f = ExitStack()
    sgb = sb(f, "sgb", [P, TT, CW])
    hid = sb(f, "hid", [P, TT, CW])
    hidh = sb(f, "hidh", [P, 4, S], F32R)
    hidl = sb(f, "hidl", [P, 4, S], F32R)
    row2 = sb(f, "row2", [P, D])
    ub = sb(f, "ub", [P, TT, CW])
    dfts = sb(f, "dfts", [P, 4, CW], F32)
    dft = sb(f, "dft", [P, TT, 2 * S])
    dft2 = sb(f, "dft2", [P, TT, S])
    lng = sb(f, "lng", [P, D])
    lnb = sb(f, "lnb", [P, D])
    f.close()
    s_zero, s_dft = sem("xacc_zero"), sem("dft_landed")
    ADA24 = (0, 2, 5, 7, 9, 11, 13, 15)
    BANK = (0, 4, 0, 4)

    class Hidden:
        def __init__(self, name, u0, wg, wu, wd, gcol, ucol, steps, fourier):
            self.u0, self.wg, self.wu, self.wd, self.gcol, self.ucol = u0, wg, wu, wd, gcol, ucol
            self.steps, self.fourier = steps, fourier
            self.sg, self.a, self.t, self.h, self.l, self.dv, self.ub, self.f1, self.v, self.f2 = (
                sem(name + n) for n in ("_silu", "_product", "_turned", "_high", "_low", "_added", "_up", "_dft1",
                                        "_dft1_stored", "_dft2"))

        def unit(self, c, j):
            if isinstance(c, int):
                return {"u": self.u0 + (j if c == 0 else 24 * c - 8 + j)}
            return {"u": self.u0 - 8 + j, "per": 24, "i": c}

        def used(self, c, j):
            return (self.u0 + j + 1) if isinstance(c, int) and c == 0 else c * 24 + (self.u0 - 8 + j + 1)

    def hidden_sp(sp, H, c, q=None, perq=0, lo=0):
        n = 24 if not isinstance(c, int) or c > 0 else 16
        before = (c - 1) * CW if isinstance(c, int) else sp.snap((c - 1) * CW)
        for j in range(n):
            if j < 16:
                w, col = ((H.wg, H.gcol), (H.wu, H.ucol))[j // 8]
                src = w_rows(w, 2 * (j % 8), 2)[:, :, bass.ds(before + (CW + col), CW)]
            else:
                jj = j - 16
                rows = H.wd.rearrange("(k p) n -> k p n", p=P)[bass.ds(4 * (c - 1) + 2 * (jj % 2), 2)]
                src = rows.rearrange("k p n -> p k n")[:, :, (jj // 2) * CW:(jj // 2 + 1) * CW]
            load(sp, src=src, **H.unit(c, j))
            pos = ADA24 if n == 24 else ADA_AFTER
            if q is not None and j in pos:
                a = pos.index(j)
                ada_load(sp, q + a // 4, a % 4, perq, None if isinstance(c, int) else c - lo)

    def hidden_end_sp(sp, H):
        c = H.steps
        for jj in range(8):
            src = w_rows(H.wd, 4 * (c - 1) + 2 * (jj % 2), 2)[:, :, (jj // 2) * CW:(jj // 2 + 1) * CW]
            load(sp, H.u0 + 24 * c - 8 + jj, src)

    def hidden_turn_act(act, H, c, r):
        act.wait_ge(H.t, c * 2 + (r - 1))
        if r == 0:
            act.wait_ge(s_mm, H.used(c, -1))
        nc.scalar.copy(hidh[:, 2 * r:2 * r + 2], psum[:, 6].rearrange("p (a b) -> p a b", a=2)).then_inc(H.h, 1)

    def hidden_turn_dve(dve, H, c, r):
        dve.wait_ge(H.h, c * 2 + (r - 1))
        if r == 0:
            dve.wait_ge(s_mm, H.used(c, -1))
        nc.vector.tensor_tensor(hidl[:, 2 * r:2 * r + 2], psum[:, 6].rearrange("p (a b) -> p a b", a=2),
                                hidh[:, 2 * r:2 * r + 2].bitcast(F32), ALU.subtract).then_inc(H.l, 1)

    def hidden_silu_act(act, H, c):
        act.wait_ge(s_mm, H.used(c, 7))
        if not isinstance(c, int) or c >= 1:
            act.wait_ge(H.a, c * 1)
        nc.scalar.activation(sgb[:], psum[:, 0:2], ACT.Silu).then_inc(H.sg, 1)

    def hidden_store_act(act, H, c, g):
        act.wait_ge(H.f1, c * 2 + (g + 1))
        if g == 0 and (not isinstance(c, int) or c >= 1):
            act.wait_ge(H.f2, c * 1)
        nc.scalar.copy(dfts[:, 2 * g:2 * g + 2], psum[:, 2:4]).then_inc(H.v, 1)

    TURN_AT = {False: ((1, 6), (9, 14)), True: ((9, 13), (12, 16))}

    def hidden_act(act, H, c):
        first = isinstance(c, int) and c == 0
        for j in range(16 if first else 24):
            if not first:
                for r in range(2):
                    if j == TURN_AT[H.fourier][r][1]:
                        hidden_turn_act(act, H, c, r)
                if H.fourier and j == 1:
                    hidden_store_act(act, H, c - 1, 1)
            if j == 11:
                hidden_silu_act(act, H, c)
            if H.fourier and j == 23:
                hidden_store_act(act, H, c, 0)
            high(act, **H.unit(c, j))
        if H.fourier and first:
            hidden_store_act(act, H, c, 0)

    def hidden_end_act(act, H):
        c = H.steps
        if H.fourier:
            hidden_store_act(act, H, c - 1, 1)
        for r in range(2):
            hidden_turn_act(act, H, c, r)
        for jj in range(8):
            high(act, H.u0 + 24 * c - 8 + jj)

    def hidden_up_dve(dve, H, c):
        dve.wait_ge(s_mm, H.used(c, 15))
        later = not isinstance(c, int) or c >= 1
        if H.fourier:
            if later:
                dve.wait_ge(H.f1, c * 2)
            nc.vector.tensor_copy(ub[:], psum[:, 2:4]).then_inc(H.ub, 1)
        else:
            dve.wait_ge(H.sg, c + 1)
            if later:
                dve.wait_ge(H.t, c * 2)
            nc.vector.tensor_tensor(hid[:], sgb[:], psum[:, 2:4], ALU.mult).then_inc(H.a, 1)

    def hidden_product_dve(dve, H, c):
        dve.wait_ge(H.f2, c + 1)
        dve.wait_ge(H.sg, c + 1)
        if not isinstance(c, int) or c >= 1:
            dve.wait_ge(H.t, c * 2)
        nc.vector.tensor_tensor(hid[:], sgb[:], psum[:, 2:4], ALU.mult).then_inc(H.a, 1)

    def hidden_add_dve(dve, H, c, n):
        dve.wait_ge(s_mm, H.used(c, 17 + 2 * n))
        o = xacc[:, :, n * CW:(n + 1) * CW]
        nc.vector.tensor_tensor(o, o, psum[:, BANK[n]:BANK[n] + 2], ALU.add).then_inc(H.dv, 1)

    def hidden_dve(dve, H, c, q=None, perq=0, lo=0):
        first, second = (isinstance(c, int) and c == v for v in (0, 1))
        n = 16 if first else 24
        for j in range(n):
            if not first:
                for r in range(2):
                    if j == TURN_AT[H.fourier][r][1]:
                        hidden_turn_dve(dve, H, c, r)
                if second and j == 3 and not H.fourier:
                    hidden_up_dve(dve, H, 0)
                if not second and j in (1, 3):
                    hidden_add_dve(dve, H, c - 1, 2 + j // 2)
                if H.fourier and j == 7:
                    hidden_product_dve(dve, H, c - 1)
                if j == 19:
                    hidden_up_dve(dve, H, c)
                if second and j == 21:
                    dve.wait_ge(s_zero, 2 if H.fourier else 1)
                if j in (21, 23):
                    hidden_add_dve(dve, H, c, (j - 21) // 2)
            low(dve, **H.unit(c, j))
            pos = ADA24 if n == 24 else ADA_AFTER
            if q is not None and j in pos:
                a = pos.index(j)
                ada_sum(dve, q + a // 4, a % 4, perq, None if isinstance(c, int) else c - lo)
        if H.fourier and first:
            hidden_up_dve(dve, H, 0)
        if q is not None:
            ada_store(dve, q, perq, None if isinstance(c, int) else c - lo)

    def hidden_end_dve(dve, H):
        c = H.steps
        for n in (2, 3):
            hidden_add_dve(dve, H, c - 1, n)
        if H.fourier:
            hidden_product_dve(dve, H, c - 1)
        for r in range(2):
            hidden_turn_dve(dve, H, c, r)
        for jj in range(8):
            low(dve, H.u0 + 24 * c - 8 + jj)
            if jj in (4, 6):
                dve.wait_ge(s_mm, H.u0 + 24 * c - 8 + jj - 2)
                hidden_tail_add(dve, H, (jj - 4) // 2)
        for n in (2, 3):
            dve.wait_ge(s_mm, H.u0 + 24 * c - 8 + 2 * n + 2)
            hidden_tail_add(dve, H, n)

    def hidden_tail_add(dve, H, n):
        o = xacc[:, :, n * CW:(n + 1) * CW]
        nc.vector.tensor_tensor(o, o, psum[:, BANK[n]:BANK[n] + 2], ALU.add).then_inc(H.dv, 1)

    def hidden_turn_pe(pe, H, c, r):
        if r == 0:
            pe.wait_ge(H.a, c * 1)
            if not isinstance(c, int) or c >= 2:
                pe.wait_ge(H.l, c * 2 - 2)
        else:
            pe.wait_ge(H.l, c * 2 - 1)
        for j in range(2):
            for t in range(TT):
                k = 2 * r + j
                ins = nc.tensor.transpose(psum[:, 6, j * S + t * P:j * S + t * P + P], hid[:, t, k * P:(k + 1) * P],
                                          ident[:])
        ins.then_inc(H.t, 1)

    def hidden_dft1_pe(pe, H, c, g):
        if g == 0:
            pe.wait_ge(H.ub, c + 1)
            if isinstance(c, int) and c == 0:
                pe.wait_ge(s_dft, 32)
        else:
            pe.wait_ge(H.v, c * 2 + 1)
        for half in range(2):
            for t in range(TT):
                ins = nc.tensor.matmul(psum[:, 2 + half], ub[:, t, g * S + half * P:g * S + half * P + P], dft[:, t],
                                       start=(t == 0), stop=(t == TT - 1))
        ins.then_inc(H.f1, 1)

    def hidden_dft2_pe(pe, H, c):
        pe.wait_ge(H.v, c * 2 + 2)
        for g in range(2):
            for t in range(TT):
                for half in range(2):
                    a = dfts[:, 2 * g + half]
                    o = psum[:, 2 + t, g * S:(g + 1) * S]
                    nc.tensor.matmul(o, a[:, t * P:t * P + P], dft[:, half, 0:S], start=(half == 0), stop=False)
                    ins = nc.tensor.matmul(o, a[:, S + t * P:S + t * P + P], dft2[:, half], start=False, stop=(half == 1))
        ins.then_inc(H.f2, 1)

    def hidden_down_pe(pe, H, c, jj, unit):
        n = jj // 2
        if jj == 0:
            pe.wait_ge(H.l, c * 2)
            if isinstance(c, int) and c == H.steps:
                pe.wait_ge(H.dv, 4 * c - 5)
            else:
                pe.wait_ge(H.sg, c + 1)
        if jj == 2 and (not isinstance(c, int) or c >= 2):
            pe.wait_ge(H.dv, c * 4 - 4)
        if jj in (4, 6):
            pe.wait_ge(H.dv, c * 4 + (n - 5))
        multiply(pe, tiles=[(hidh, hidl, t, BANK[n] + t) for t in range(TT)], kt=2 * (jj % 2), last_kt=3, **unit)

    def hidden_pe(pe, H, c, q=None, perq=0, lo=0):
        first = isinstance(c, int) and c == 0
        later = not isinstance(c, int) or c >= 2
        for j in range(16 if first else 24):
            if j == 0 and not first:
                pe.wait_ge(H.sg, c * 1)
                if later:
                    pe.wait_ge(H.dv, c * 4 - 5)
            if j == 8 and not first:
                pe.wait_ge(H.a, c * 1)
            if j < 16:
                multiply(pe, tiles=lat(2 * (j // 8)), kt=2 * (j % 8), last_kt=KT - 1, **H.unit(c, j))
            else:
                hidden_down_pe(pe, H, c, j - 16, H.unit(c, j))
            if not first:
                for r in range(2):
                    if j == TURN_AT[H.fourier][r][0]:
                        hidden_turn_pe(pe, H, c, r)
                if H.fourier and j == 3:
                    hidden_dft2_pe(pe, H, c - 1)
                if H.fourier and j in (19, 21):
                    hidden_dft1_pe(pe, H, c, (j - 19) // 2)
            if q is not None and j == (13 if first else 19):
                ada_reduce(pe, q, perq, None if isinstance(c, int) else c - lo)
        if H.fourier and first:
            hidden_dft1_pe(pe, H, c, 0)
            hidden_dft1_pe(pe, H, c, 1)

    def hidden_end_pe(pe, H):
        c = H.steps
        if H.fourier:
            hidden_dft2_pe(pe, H, c - 1)
        for r in range(2):
            hidden_turn_pe(pe, H, c, r)
        for jj in range(8):
            hidden_down_pe(pe, H, c, jj, {"u": H.u0 + 24 * c - 8 + jj})

    ffn = Hidden("ffn", U_FFN, dram["w_ffn_gate"][0], dram["w_ffn_up"][0], dram["w_ffn_down"][0], 0, 0, FFN_CH, False)
    fou = Hidden("fourier", U_FOU, dram["w_in_fourier_2"][0], dram["w_in_fourier_2"][0], dram["w_out_fourier_2"][0],
                 4096, 0, FCH, True)

    def ffn_steps(eng, step):
        step(0, 20, 0, 0)
        step(1, 22, 0, 0)
        with eng.Fori(2, 6) as c:
            step(c, 24, 2, 2)
        with eng.Fori(6, 8) as c:
            step(c, 32, 2, 6)
        with eng.Fori(8, FFN_CH) as c:
            step(c, 36, 2, 8)

    def fourier_steps(eng, step):
        step(0, None, 0, 0)
        step(1, None, 0, 0)
        with eng.Fori(2, FCH) as c:
            step(c, None, 0, 2)

    g1 = ExitStack()
    ch_h = sb(g1, "ctxh", [P, KT, S], F32R)
    ch_l = sb(g1, "ctxl", [P, KT, S], F32R)
    g1.close()
    g2 = ExitStack()
    sgate = sb(g2, "sgate", [P, TT, D])
    qb = sb(g2, "qb", [P, TT, 1024])
    cq = sb(g2, "cq", [P, TT, QL])
    g3 = sb(g2, "rope_rows", [P, 512])
    ckv = sb(g2, "ckv", [P, 4, KVL])
    kvb = sb(g2, "kvb", [P, 4, 512])
    kpe = sb(g2, "kpe", [P, 4, ROPE])
    kpeT = sb(g2, "kpeT", [P, 512])
    kbT = sb(g2, "kbT", [P, 2, 512])
    rope_b = sb(g2, "rope_b_t", [P, TT, 256])
    rope_a = sb(g2, "rope_a_t", [P, TT, 128])
    wqk = sb(g2, "wqk", [P, 2, HD])
    st6 = sb(g2, "st6", [P, 8, 6])
    mv6 = sb(g2, "mv6", [P, 6, 2])
    ms6 = sb(g2, "ms6", [P, 30])
    r6 = sb(g2, "r6", [P, 30])
    g2.close()
    xaf = xacc[:].rearrange("p a b -> p (a b)")
    qp = xaf[:, 0:768].rearrange("p (t n) -> p t n", t=TT)
    kvp = xaf[:, 768:2816].rearrange("p (t n) -> p t n", t=4)
    kT2 = xaf[:, 2816:3328]
    qT2 = xaf[:, 3328:3840].rearrange("p (h s) -> p h s", h=2)
    prob2 = arawf[:, 0:1024].rearrange("p (t s) -> p t s", t=TT)
    pT2 = arawf[:, 1024:2048].rearrange("p (k s) -> p k s", k=4)
    stq = arawf[:, 2048:2560].rearrange("p (h t e) -> p h t e", h=2, t=TT)
    rtmp = arawf[:, 2560:3584]
    sq = xaf
    yA = ckv[:].rearrange("p a b -> p (a b)").rearrange("p (t n) -> p t n", t=TT)
    row3 = sgate[:, 0]
    tmp3 = sgate[:, 1, 0:2 * CW].rearrange("p (t n) -> p t n", t=TT)
    gain3 = kvb[:].rearrange("p a b -> p (a b)")
    bias3 = ckv[:].rearrange("p a b -> p (a b)")
    cqTh, cqTl = hh[:, 0:6], hl[:, 0:6]
    ckvTh, ckvTl = (v[:, 6:14].rearrange("p (k a) s -> p k (a s)", a=2) for v in (hh, hl))

    s_ctx, s_ropes, s_e, s_ge = sem("ctx_landed"), sem("rope_landed"), sem("z_stored"), sem("silu_gate")
    s_m2, s_r2, s_nz, s_qbr = sem("z_squares"), sem("z_rstd"), sem("z_normed"), sem("b_ready")
    s_zt, s_zh, s_zl = sem("z_turned"), sem("z_high"), sem("z_low")
    s_kt, s_ke = sem("k_turned"), sem("k_stored")
    s_pq, s_qr, s_sq = sem("pair_stored"), sem("pair_rotated"), sem("q_staged")
    s_ta, s_te, s_s2, s_mx2, s_ex2, s_rc2, s_tp2, s_pe2, s_pf2, s_pv2, s_y2 = (sem("a2_" + n) for n in (
        "turned", "stored", "scores", "max", "exp", "recip", "p_turned", "pT_act", "pT_dve", "pv", "y"))
    s_yt, s_yh2, s_yl2 = sem("y_turned"), sem("y2_high"), sem("y2_low")
    s_aev, s_rows = sem("attn_added"), sem("rows_landed")

    AIN = ((768, 512, True, 0, lambda: ckv[:]), (1280, 64, True, 4, lambda: kpe[:]), (2368, 512, True, 0, lambda: kvb[:]),
           (0, 512, False, 4, lambda: cq[:, :, 0:512]), (512, 256, False, 0, lambda: cq[:, :, 512:768]),
           (1344, 512, False, 2, lambda: qb[:, :, 0:512]), (1856, 512, False, 4, lambda: qb[:, :, 512:1024]))
    NEED = (0, 0, 1, 2, 3, 3, 4)

    def ain_sp(sp):
        w = dram["w_in_attn_2"][0]
        for n, (c, wd, both, b, d) in enumerate(AIN):
            for j in range(UPC):
                load(sp, U_AIN + UPC * n + j, w_rows(w, 2 * j, 2)[:, :, c:c + wd], wd)

    def ain_act(act):
        def store(n):
            c, wd, both, b, d = AIN[n]
            act.wait_ge(s_mm, U_AIN + UPC * (n + 1))
            nc.scalar.copy(d(), psum[:, b:b + (4 if both else 2), 0:wd]).then_inc(s_e, 1)
        for n, (c, wd, both, b, d) in enumerate(AIN):
            for j in range(UPC):
                if j == 3 and n:
                    store(n - 1)
                high(act, U_AIN + UPC * n + j, wd)
        store(len(AIN) - 1)

    def ain_dve(dve):
        for n, (c, wd, both, b, d) in enumerate(AIN):
            for j in range(UPC):
                low(dve, U_AIN + UPC * n + j, wd)

    def ain_pe(pe):
        for n, (c, wd, both, b, d) in enumerate(AIN):
            if NEED[n]:
                pe.wait_ge(s_e, NEED[n])
            tiles = lat(b) + ([(ch_h, ch_l, t, b + 2 + t) for t in range(TT)] if both else [])
            for j in range(UPC):
                multiply(pe, U_AIN + UPC * n + j, tiles, 2 * j, KT - 1, wd)
        pe.wait_ge(s_e, 7)

    def gate_evac(act, c, per, i):
        act.wait_ge(s_mm, at(U_AIN + 56 + UPC * (c + 1), UPC * per, i))
        b = 2 * (c % 2)
        nc.scalar.activation(sgate[:, :, bass.ds(at(c * CW, per * CW, i), CW)], psum[:, b:b + 2], ACT.Silu).then_inc(s_ge, 1)

    def ada_tail_dve(dve):
        for q in (46, 47):
            for j in range(4):
                ada_sum(dve, q, j)
        ada_store(dve, 46)

    def z_dve(dve, ch):
        V = nc.vector
        dve.wait_ge(s_e, 7)
        dve.wait_ge(s_ropes, 48)
        for t in range(TT):
            for c in range(2):
                ch(V.bn_stats(st6[:, 2 * t + c], cq[:, t, 384 * c:384 * c + 384]))
        for t in range(4):
            ch(V.bn_stats(st6[:, 4 + t], ckv[:, t]))
        ch.wait()
        for t in range(TT):
            ch(V.bn_aggr(mv6[:, t], st6[:, 2 * t:2 * t + 2].rearrange("p c s -> p (c s)")))
        for t in range(4):
            ch(V.bn_aggr(mv6[:, 2 + t], st6[:, 4 + t]))
        ch.wait()
        ch(V.tensor_tensor(ms6[:, 0:6].unsqueeze(2), mv6[:, :, 0:1], mv6[:, :, 0:1], ALU.mult))
        qsq = sq[:, 0:2048].rearrange("p (t n) -> p t n", t=TT)
        ksq = sq[:, 2048:3072].rearrange("p (t n) -> p t n", t=4)
        ch(V.tensor_tensor(qsq, qb[:], qb[:], ALU.mult))
        ch(V.tensor_tensor(ksq, kvb[:, :, 0:256], kvb[:, :, 0:256], ALU.mult))
        ch.wait()
        ch(V.tensor_tensor(ms6[:, 0:6].unsqueeze(2), ms6[:, 0:6].unsqueeze(2), mv6[:, :, 1:2], ALU.add))
        ch(V.tensor_reduce(ms6[:, 6:22], sq[:, 0:2048].rearrange("p (h e) -> p h e", e=HD), AX, ALU.add))
        ch(V.tensor_reduce(ms6[:, 22:30], sq[:, 2048:3072].rearrange("p (h e) -> p h e", e=HD), AX, ALU.add))
        ch.wait()
        ch(V.tensor_scalar(ms6[:, 0:6], ms6[:, 0:6], RMS_EPS, None, ALU.add))
        V.tensor_scalar(ms6[:, 6:30], ms6[:, 6:30], 1.0 / HD, RMS_EPS, ALU.mult, ALU.add).then_inc(s_m2, 1)
        dve.wait_ge(s_r2, 1)
        for t in range(TT):
            ch(V.tensor_scalar(cq[:, t], cq[:, t], r6[:, t:t + 1], None, ALU.mult))
        for t in range(4):
            ins = V.tensor_scalar(ckv[:, t], ckv[:, t], r6[:, 2 + t:3 + t], None, ALU.mult)
        ins.then_inc(s_nz, 1)
        for t in range(TT):
            v = qb[:, t].rearrange("p (h e) -> p h e", h=8)
            ch(V.tensor_tensor(v, v, r6[:, 6 + 8 * t:14 + 8 * t].unsqueeze(2).broadcast_to([P, 8, HD]), ALU.mult))
        for t in range(4):
            v = kvb[:, t, 0:256].rearrange("p (h e) -> p h e", h=2)
            ch(V.tensor_tensor(v, v, r6[:, 22 + 2 * t:24 + 2 * t].unsqueeze(2).broadcast_to([P, 2, HD]), ALU.mult))
        ch.wait()
        for t in range(TT):
            v = qb[:, t].rearrange("p (h e) -> p h e", h=8)
            ch(V.tensor_tensor(v, v, wqk[:, 0:1].broadcast_to([P, 8, HD]), ALU.mult))
        for t in range(4):
            v = kvb[:, t, 0:256].rearrange("p (h e) -> p h e", h=2)
            ch(V.tensor_tensor(v, v, wqk[:, 1:2].broadcast_to([P, 2, HD]), ALU.mult))
        ch.wait()
        for t in range(TT):
            rope(ch, kpe[:, t:t + 1], 1, 64, rope_a[:, t], sq)
            rope(ch, kvb[:, t, 0:256].rearrange("p (h e) -> p h e", h=2), 2, 128, rope_b[:, t], sq)
            rope(ch, qb[:, t].rearrange("p (h e) -> p h e", h=8), 8, 128, rope_b[:, t], sq)
        V.tensor_copy(st6[:, 0, 0:1], st6[:, 0, 1:2]).then_inc(s_qbr, 1)

    def rope(ch, v, heads, n, table, tmp):
        V = nc.vector
        t = tmp[:, 0:heads * n].rearrange("p (h e) -> p h e", h=heads)
        cs = table[:, 0:n].unsqueeze(1).broadcast_to([P, heads, n])
        sn = table[:, n:2 * n]
        for a in range(2):
            ch(V.tensor_tensor(t[:, :, a::2], v[:, :, 1 - a::2], sn[:, a::2].unsqueeze(1).broadcast_to([P, heads, n // 2]),
                               ALU.mult))
        ch.wait()
        ch(V.tensor_tensor(v, v, cs, ALU.mult))
        ch.wait()
        ch(V.tensor_tensor(v, v, t, ALU.add))
        ch.wait()

    def z_pool(pool):
        pool.wait_ge(s_m2, 1)
        nc.gpsimd.tensor_tensor(r6[:], ms6[:], mhalf[:, 0:30], ALU.pow).then_inc(s_r2, 1)

    def z_turn_pe(pe):
        pe.wait_ge(s_nz, 1)
        pe.wait_ge(s_mod, 48)
        pe.wait_ge(s_ge, 4)
        for r in range(7):
            if r >= 2:
                pe.wait_ge(s_zl, r - 1)
            for j in range(4):
                if r < 3:
                    src = cq[:, j % 2, (2 * r + j // 2) * P:(2 * r + j // 2 + 1) * P]
                else:
                    src = ckv[:, j, (r - 3) * P:(r - 2) * P]
                ins = nc.tensor.transpose(psum[:, 4 + r % 2, j * P:(j + 1) * P], src, ident[:])
            ins.then_inc(s_zt, 1)
        pe.wait_ge(s_qbr, 1)
        for r in range(3):
            for j in range(4):
                if r == 0:
                    ins = nc.tensor.transpose(psum[0:64, 6, j * P:(j + 1) * P], kpe[:, j], ident[:])
                else:
                    ins = nc.tensor.transpose(psum[:, 1 + r, j * P:(j + 1) * P], kvb[:, j, (r - 1) * HD:r * HD], ident[:])
            ins.then_inc(s_kt, 1)

    def z_turn_act(act):
        act.wait_ge(s_mm, U_PAIR)
        for r in range(7):
            act.wait_ge(s_zt, r + 1)
            if r < 3:
                for j in range(2):
                    c = COLS["ql"].start + 2 * r + j
                    ins = nc.scalar.activation(cqTh[:, 2 * r + j], psum[:, 4 + r % 2, j * S:(j + 1) * S], ACT.Copy,
                                               scale=cols[:, c:c + 1])
            else:
                c = COLS["kvl"].start + r - 3
                ins = nc.scalar.activation(ckvTh[:, r - 3], psum[:, 4 + r % 2], ACT.Copy, scale=cols[:, c:c + 1])
            ins.then_inc(s_zh, 1)
        for r in range(3):
            act.wait_ge(s_kt, r + 1)
            if r == 0:
                ins = nc.scalar.copy(kpeT[0:64], psum[0:64, 6])
            else:
                ins = nc.scalar.copy(kbT[:, r - 1], psum[:, 1 + r])
            ins.then_inc(s_ke, 1)

    def z_turn_dve(dve):
        for r in range(7):
            dve.wait_ge(s_zh, r + 1)
            for j in range(2 if r < 3 else 1):
                if r < 3:
                    c, i0, o, h = (COLS["ql"].start + 2 * r + j, psum[:, 4 + r % 2, j * S:(j + 1) * S],
                                   cqTl[:, 2 * r + j], cqTh[:, 2 * r + j])
                else:
                    c, i0, o, h = COLS["kvl"].start + r - 3, psum[:, 4 + r % 2], ckvTl[:, r - 3], ckvTh[:, r - 3]
                ins = nc.vector.scalar_tensor_tensor(out=o, in0=i0, scalar=cols[:, c:c + 1], in1=h.bitcast(F32),
                                                     op0=ALU.mult, op1=ALU.subtract)
            ins.then_inc(s_zl, 1)

    PU = tuple((1, 384) for _ in range(6)) + ((2, 512), (2, 512))

    def pair_sp(sp, i):
        wq, wk = dram["wq_b_2"][0], dram["wkv_b_2"][0]
        for j, (kn, w) in enumerate(PU):
            if j < 6:
                src = w_rows(wq, j, 1)[:, :, bass.ds(at(0, 384, i), 384)]
            else:
                src = w_rows(wk, 2 * (j - 6), 2)[:, :, bass.ds(at(0, 512, i), 512)]
            load(sp, U_PAIR + j, src, w, per=8, i=i)

    def pair_act(act, i):
        for j, (kn, w) in enumerate(PU):
            high(act, U_PAIR + j, w, kn, per=8, i=i)
        act.wait_ge(s_mm, at(U_PAIR + 8, 8, i))
        if i is not None:
            act.wait_ge(s_ta, at(0, 4, i))
            act.wait_ge(s_pv2, at(0, 4, i))
        else:
            act.wait_ge(s_qbr, 1)
        nc.scalar.copy(qp, psum[:, 0:2, 0:384])
        nc.scalar.copy(kvp, psum[:, 2:6]).then_inc(s_pq, 1)
        nc.scalar.copy(stq[:, 0], qb[:, :, bass.ds(at(0, HD, i), HD)])
        nc.scalar.copy(stq[:, 1], qb[:, :, bass.ds(at(512, HD, i), HD)]).then_inc(s_sq, 1)

        def te(k):
            act.wait_ge(s_ta, at(k + 1, 4, i))
            if i is not None or k:
                act.wait_ge(s_s2, at(k, 4, i))
            ins = nc.scalar.copy(qT2[:, 0], psum[:, 6, 0:S])
            if k < 2:
                nc.scalar.copy(qT2[0:64, 1], psum[0:64, 6, S:2 * S])
                ins = nc.scalar.copy(kT2, psum[:, 7])
            ins.then_inc(s_te, 1)

        def ex(k):
            act.wait_ge(s_mx2, at(k + 1, 4, i))
            if i is not None or k:
                act.wait_ge(s_tp2, at(k, 4, i))
                act.wait_ge(s_rc2, at(k, 4, i))
            sc = A_SCALE if k < 2 else B_SCALE
            for t in range(TT):
                ins = nc.scalar.activation(prob2[:, t], psum[:, t], ACT.Exp, bias=neg[:, t:t + 1], scale=sc,
                                           accum_out=den[:, t:t + 1])
            ins.then_inc(s_ex2, 1)

        def pt(k):
            act.wait_ge(s_tp2, at(k + 1, 4, i))
            if i is not None or k:
                act.wait_ge(s_pv2, at(k, 4, i))
            nc.scalar.copy(pT2[:, 0:2], psum[:, 2].rearrange("p (k s) -> p k s", k=2)).then_inc(s_pe2, 1)
        te(0)
        ex(0)
        for k in range(1, 4):
            te(k)
            pt(k - 1)
            ex(k)
        pt(3)

    def pair_dve(dve, ch, i):
        for j, (kn, w) in enumerate(PU):
            low(dve, U_PAIR + j, w, kn, per=8, i=i)
        dve.wait_ge(s_pq, at(1, 1, i))
        for t in range(TT):
            rope(ch, qp[:, t].rearrange("p (h e) -> p h e", h=2)[:, :, 128:192], 2, 64, rope_a[:, t], rtmp)
        nc.vector.tensor_copy(st6[:, 0, 0:1], st6[:, 0, 1:2]).then_inc(s_qr, 1)

        def mx(k):
            dve.wait_ge(s_s2, at(k + 1, 4, i))
            if i is not None or k:
                dve.wait_ge(s_ex2, at(k, 4, i))
            ch(nc.vector.tensor_reduce(neg[:], psum[:, 0:2], AX, ALU.max))
            ch.wait()
            nc.vector.tensor_scalar(neg[:], neg[:], -(A_SCALE if k < 2 else B_SCALE), None, ALU.mult).then_inc(s_mx2, 1)

        def rc(k):
            dve.wait_ge(s_ex2, at(k + 1, 4, i))
            nc.vector.reciprocal(rden[:, k % 2], den[:]).then_inc(s_rc2, 1)

        def pt(k):
            dve.wait_ge(s_tp2, at(k + 1, 4, i))
            if i is not None or k:
                dve.wait_ge(s_pv2, at(k, 4, i))
            nc.vector.tensor_copy(pT2[:, 2:4], psum[:, 3].rearrange("p (k s) -> p k s", k=2)).then_inc(s_pf2, 1)

        def y(k):
            dve.wait_ge(s_pv2, at(k + 1, 4, i))
            dve.wait_ge(s_rc2, at(k + 1, 4, i))
            if i is None and k == 0:
                dve.wait_ge(s_ge, 4)
            if k < 2:
                o, gc = yA[:, :, bass.ds(at(k * HD, 2 * HD, i), HD)], at(k * HD, 2 * HD, i)
            else:
                o, gc = qb[:, :, bass.ds(at((k - 2) * 512, HD, i), HD)], at(1024 + (k - 2) * 512, HD, i)
            for t in range(TT):
                ins = nc.vector.scalar_tensor_tensor(out=o[:, t], in0=psum[:, 4, t * P:(t + 1) * P],
                                                     scalar=rden[:, k % 2, t:t + 1],
                                                     in1=sgate[:, t, bass.ds(gc, HD)], op0=ALU.mult, op1=ALU.mult)
            ins.then_inc(s_y2, 1)
        mx(0)
        rc(0)
        for k in range(1, 4):
            pt(k - 1)
            mx(k)
            y(k - 1)
            rc(k)
        pt(3)
        y(3)

    def pair_pe(pe, i):
        if i is not None:
            pe.wait_ge(s_y2, at(0, 4, i))
            pe.wait_ge(s_pe2, at(0, 4, i))
            pe.wait_ge(s_pf2, at(0, 4, i))
        else:
            pe.wait_ge(s_zl, 7)
            pe.wait_ge(s_ke, 3)
        for j, (kn, w) in enumerate(PU):
            if j < 6:
                tiles, kt, last = [(cqTh, cqTl, t, t) for t in range(TT)], j, 5
            else:
                tiles, kt, last = [(ckvTh, ckvTl, t, 2 + t) for t in range(4)], 2 * (j - 6), 3
            multiply(pe, U_PAIR + j, tiles, kt, last, w, kn, per=8, i=i)

        def turn(k):
            if k == 0:
                pe.wait_ge(s_qr, at(1, 1, i))
            if k == 2:
                pe.wait_ge(s_sq, at(1, 1, i))
            if i is not None or k:
                pe.wait_ge(s_te, at(k, 4, i))
            for t in range(TT):
                if k < 2:
                    nc.tensor.transpose(psum[:, 6, t * P:(t + 1) * P], qp[:, t, 192 * k:192 * k + 128], ident[:])
                    ins = nc.tensor.transpose(psum[0:64, 6, S + t * P:S + (t + 1) * P], qp[:, t, 192 * k + 128:192 * k + 192],
                                              ident[:])
                else:
                    ins = nc.tensor.transpose(psum[:, 6, t * P:(t + 1) * P], stq[:, k - 2, t], ident[:])
            if k < 2:
                for t in range(4):
                    ins = nc.tensor.transpose(psum[:, 7, t * P:(t + 1) * P], kvp[:, t, 256 * k:256 * k + 128], ident[:])
            ins.then_inc(s_ta, 1)

        def scores(k):
            pe.wait_ge(s_te, at(k + 1, 4, i))
            if i is not None or k:
                pe.wait_ge(s_ex2, at(k, 4, i))
            for t in range(TT):
                a = slice(t * P, t * P + P)
                if k < 2:
                    nc.tensor.matmul(psum[:, t], qT2[:, 0, a], kT2, start=True, stop=False)
                    ins = nc.tensor.matmul(psum[:, t], qT2[0:64, 1, a], kpeT[0:64], start=False, stop=True)
                else:
                    ins = nc.tensor.matmul(psum[:, t], qT2[:, 0, a], kbT[:, k - 2], start=True, stop=True)
            ins.then_inc(s_s2, 1)

        def turn_p(k):
            pe.wait_ge(s_ex2, at(k + 1, 4, i))
            if i is not None or k:
                pe.wait_ge(s_pe2, at(k, 4, i))
                pe.wait_ge(s_pf2, at(k, 4, i))
            for kt in range(4):
                for t in range(TT):
                    o = (kt % 2) * S + t * P
                    ins = nc.tensor.transpose(psum[:, 2 + kt // 2, o:o + P], prob2[:, t, kt * P:(kt + 1) * P], ident[:])
            ins.then_inc(s_tp2, 1)

        def pv(k):
            pe.wait_ge(s_pe2, at(k + 1, 4, i))
            pe.wait_ge(s_pf2, at(k + 1, 4, i))
            if i is not None or k:
                pe.wait_ge(s_y2, at(k, 4, i))
            for t in range(TT):
                for kt in range(4):
                    v = kvp[:, kt, 256 * k + 128:256 * k + 256] if k < 2 else kvb[:, kt, 256 + (k - 2) * HD:256 + (k - 1) * HD]
                    ins = nc.tensor.matmul(psum[:, 4, t * P:(t + 1) * P], pT2[:, kt, t * P:(t + 1) * P], v,
                                           start=(kt == 0), stop=(kt == 3))
            ins.then_inc(s_pv2, 1)
        turn(0)
        scores(0)
        for k in range(1, 4):
            turn(k)
            turn_p(k - 1)
            scores(k)
            pv(k - 1)
        turn_p(3)
        pv(3)

    def y2_turn_pe(pe):
        pe.wait_ge(s_y2, 16)
        for r in range(8):
            if r >= 2:
                pe.wait_ge(s_yl2, r - 1)
            for j in range(4):
                ft = 2 * r + j // 2
                src = (yA if ft < 8 else qb)[:, j % 2, (ft % 8) * P:(ft % 8 + 1) * P]
                ins = nc.tensor.transpose(psum[:, r % 2, j * P:(j + 1) * P], src, ident[:])
            ins.then_inc(s_yt, 1)

    def y2_turn_act(act):
        for r in range(8):
            act.wait_ge(s_yt, r + 1)
            nc.scalar.copy(hh[:, 2 * r:2 * r + 2], psum[:, r % 2].rearrange("p (a b) -> p a b", a=2)).then_inc(s_yh2, 1)

    def y2_turn_dve(dve):
        for r in range(8):
            dve.wait_ge(s_yh2, r + 1)
            nc.vector.tensor_tensor(hl[:, 2 * r:2 * r + 2], psum[:, r % 2].rearrange("p (a b) -> p a b", a=2),
                                    hh[:, 2 * r:2 * r + 2].bitcast(F32), ALU.subtract).then_inc(s_yl2, 1)

    s_post = sem("post_normed")

    def post_norm_dve(dve, ch, k, gain, bias):
        norm_dve(dve, ch, k, x, x, False)
        dve.wait_ge(s_xn, 2 * k + 2)
        for t in range(TT):
            ch(nc.vector.tensor_tensor(x[:, t], x[:, t], gain, ALU.mult))
        ch.wait()
        for t in range(TT):
            ins = nc.vector.tensor_tensor(x[:, t], x[:, t], bias, ALU.add)
            ins.then_inc(s_post, 1)
        dve.wait_ge(s_post, 2 if k == 4 else 4)

    def add_hidden_dve(dve, ch, H, scale, grow, n_rows):
        dve.wait_ge(H.dv, 4 * H.steps)
        dve.wait_ge(s_growc, n_rows)
        for t in range(TT):
            ch(nc.vector.tensor_tensor(xacc[:, t], xacc[:, t], grow, ALU.mult))
        ch.wait()
        for t in range(TT):
            ch(nc.vector.scalar_tensor_tensor(out=x[:, t], in0=x[:, t], scalar=scale, in1=xacc[:, t],
                                              op0=ALU.mult, op1=ALU.add))
        ch.wait()

    s_out = sem("out_stored")

    actx = arawf.rearrange("p (t n) -> p t n", t=TT)

    def rest_sp(sp):
        sp.wait_ge(s_acc, acc_ops(42))
        sp.dma_start(actx, dram["ctx_2"][0].rearrange("(t p) n -> p t n", p=P)).then_inc(s_ctx, 16)
        sp.dma_start(rope_a[:], dram["rope_a"].rearrange("(t p) n -> p t n", p=P)).then_inc(s_ropes, 16)
        sp.dma_start(rope_b[:], dram["rope_b"].rearrange("(t p) n -> p t n", p=P)).then_inc(s_ropes, 16)
        sp.dma_start(wqk[:, 0], dram["q_norm_b_2"][0].partition_broadcast(P)).then_inc(s_ropes, 16)
        sp.dma_start(wqk[:, 1], dram["k_norm_b_2"][0].partition_broadcast(P)).then_inc(s_ropes, 16)
        ain_sp(sp)
        sp.wait_ge(s_tp, 32)
        pairs_sp(sp, U_AIN + 56, dram["w_in_attn_2"][0], 42, 2, c0=2880)
        for q in (46, 47):
            for j in range(4):
                ada_load(sp, q, j)
        pair_sp(sp, None)
        with sp.Fori(1, 4) as i:
            pair_sp(sp, i)
        sp.wait_ge(s_yt, 8)
        sp.dma_start(gain3, dram["ln_g_2"][0].partition_broadcast(P)).then_inc(s_rows, 16)
        sp.dma_start(bias3, dram["ln_b_2"][0].partition_broadcast(P)).then_inc(s_rows, 16)
        pairs_sp(sp, U_AOUT, dram["w_out_attn_2"][0], None, 2)
        sp.wait_ge(s_post, 2)
        sp.dma_start(dft[:], dram["dft"].rearrange("(t p) n -> p t n", p=P)).then_inc(s_dft, 16)
        sp.dma_start(dft2[:], dram["dft2"].rearrange("(t p) n -> p t n", p=P)).then_inc(s_dft, 16)
        sp.dma_start(lng[:], dram["ln_g_2"][1].partition_broadcast(P)).then_inc(s_rows, 16)
        sp.dma_start(lnb[:], dram["ln_b_2"][1].partition_broadcast(P)).then_inc(s_rows, 16)
        fourier_steps(sp, lambda c, q, per, lo: hidden_sp(sp, fou, c, q, per, lo))
        hidden_end_sp(sp, fou)
        for t in range(TT):
            sp.wait_ge(s_post, 3 + t)
            sp.dma_start(out[0, t * P:(t + 1) * P], x[:, t]).then_inc(s_out, 16)
        sp.wait_ge(s_out, 32)

    def rest_pool(pool):
        norm_pool(pool, 2)
        norm_pool(pool, 3)
        turn_pool(pool, 2, h32, hh, hl)
        turn_pool(pool, 3, h32, ch_h, ch_l)
        z_pool(pool)
        norm_pool(pool, 4)
        norm_pool(pool, 5)
        turn_pool(pool, 4, h32, hh, hl)
        pool.wait_ge(s_tp, 40)
        nc.gpsimd.memset(xacc[:], 0.0).then_inc(s_zero, 1)
        norm_pool(pool, 6)

    def rest_act(act):
        turn_act(act, 2, h32, hh)
        turn_act(act, 3, h32, ch_h)
        ain_act(act)
        pairs_act(act, U_AIN + 56, 2, gate_evac)
        z_turn_act(act)
        pair_act(act, None)
        with act.Fori(1, 4) as i:
            pair_act(act, i)
        y2_turn_act(act)
        gate_act(act, 2, row3)
        pairs_act(act, U_AOUT, 2, None)
        turn_act(act, 4, h32, hh)
        fourier_steps(act, lambda c, q, per, lo: hidden_act(act, fou, c))
        hidden_end_act(act, fou)
        gate_act(act, 3, row2)

    def rest_dve(dve, ch):
        dve.wait_ge(s_ctx, 16)
        norm_dve(dve, ch, 2, actx, actx, False)
        add_hidden_dve(dve, ch, ffn, 1.0, row2[:], 8)
        norm_dve(dve, ch, 3, x, xn, False)
        ch(nc.vector.tensor_scalar(mscale[:], modc[:, 112:128], 1.0, None, ALU.add))
        ch(nc.vector.tensor_scalar(mscalex[:], modx[:, 16:32], 1.0, None, ALU.add))
        ch.wait()
        turn_dve(dve, 2, h32, mscale, modc[:, 96:112])
        turn_dve(dve, 3, h32, mscalex, modx[:, 0:16])
        ain_dve(dve)
        pairs_dve(dve, U_AIN + 56, 42, 2)
        ada_tail_dve(dve)
        z_dve(dve, ch)
        z_turn_dve(dve)
        pair_dve(dve, ch, None)
        with dve.Fori(1, 4) as i:
            ch.enter(i, 1, 12)
            pair_dve(dve, ch, i)
            ch.leave(4)
        y2_turn_dve(dve)
        gate_dve(dve, 2, 128, diag)
        dve.wait_ge(s_growc, 12)
        pairs_dve(dve, U_AOUT, None, 2, ch=ch, ch_per=2,
                  evac=lambda e, c, per, i: gated(e, ch, c, per, i, U_AOUT, x, x, ALPHA, s_aev, row3, tmp3))
        dve.wait_ge(s_aev, 4)
        dve.wait_ge(s_rows, 32)
        post_norm_dve(dve, ch, 4, gain3, bias3)
        norm_dve(dve, ch, 5, x, xn, False)
        ch(nc.vector.tensor_scalar(mscale[:], modc[:, 160:176], 1.0, None, ALU.add))
        ch.wait()
        turn_dve(dve, 4, h32, mscale, modc[:, 144:160])
        fourier_steps(dve, lambda c, q, per, lo: hidden_dve(dve, fou, c, q, per, lo))
        hidden_end_dve(dve, fou)
        gate_dve(dve, 3, 176, diag)
        add_hidden_dve(dve, ch, fou, ALPHA, row2[:], 16)
        dve.wait_ge(s_rows, 64)
        post_norm_dve(dve, ch, 6, lng[:], lnb[:])

    def rest_pe(pe):
        turn_pe(pe, 2, xn, 3)
        turn_pe(pe, 3, actx, 2)
        pe.wait_ge(s_hl, 32)
        pe.wait_ge(s_mod, 42)
        pe.wait_ge(s_growc, 8)
        ain_pe(pe)
        pairs_pe(pe, U_AIN + 56, 42, 2, s_ge)
        ada_reduce(pe, 46)
        z_turn_pe(pe)
        pair_pe(pe, None)
        with pe.Fori(1, 4) as i:
            pair_pe(pe, i)
        y2_turn_pe(pe)
        gate_pe(pe, 2, diag)
        pe.wait_ge(s_yl2, 8)
        pairs_pe(pe, U_AOUT, None, 2, s_aev)
        turn_pe(pe, 4, xn, 5)
        pe.wait_ge(s_hl, 40)
        fourier_steps(pe, lambda c, q, per, lo: hidden_pe(pe, fou, c, q, per, lo))
        hidden_end_pe(pe, fou)
        gate_pe(pe, 3, diag)

    @block.sync
    def _(sp):
        sp.dma_start(cols[:], dram["cols"]).then_inc(s_const, 16)
        sp.dma_start(ident[:], dram["ident"]).then_inc(s_one, 16)
        sp.dma_start(rawf[:, 1024:3072].rearrange("p (r n) -> p r n", r=2), dram["b_pad"].rearrange("r p n -> p r n")).then_inc(s_b, 16)
        sp.dma_start(x[:], dram["x"][0].rearrange("(t p) n -> p t n", p=P)).then_inc(s_x, 16)
        for j in range(4):
            ada_load(sp, 0, j)
        for j in range(4):
            ada_load(sp, 1, j)
        with sp.Fori(1, 4) as i:
            for j in range(8):
                ada_load(sp, j // 4, j % 4, 2, i)
        sp.wait_ge(s_BT, 4)
        sp.wait_ge(s_chd_ssm, 1)
        pairs_sp(sp, U_IN, dram["w_in"][0], 8, 4, peel=True)
        sp.wait_ge(s_lo, U_GLU)
        sp.dma_start(dist, dram["dist"].rearrange("(t p) s -> p t s", p=P)).then_inc(s_dist, 16)
        sp.dma_start(count, dram["count"].rearrange("(t p) s -> p t s", p=P)).then_inc(s_dist, 16)
        sp.wait_ge(s_acc, acc_ops(16))
        sp.dma_start(arawf[:, 0:2048].rearrange("p (r n) -> p r n", r=2), dram["c_pad"].rearrange("r p n -> p r n")).then_inc(s_cpad, 16)
        sp.wait_ge(s_scan["pool"], 2)
        sp.wait_ge(s_scan["dve"], 2)
        sp.wait_ge(s_ya, 8)
        glu_sp(sp)
        sp.wait_ge(s_yl, 4)
        pairs_sp(sp, U_OUT, dram["w_out"][0], 16, 2)
        ffn_steps(sp, lambda c, q, per, lo: hidden_sp(sp, ffn, c, q, per, lo))
        hidden_end_sp(sp, ffn)
        rest_sp(sp)

    @block.gpsimd
    def _(pool):
        ch = Chain(pool, s_chp)
        nc.gpsimd.memset(mhalf[:], -0.5).then_inc(s_mh, 1)
        nc.gpsimd.memset(ones[:], 1.0).then_inc(s_ones, 1)
        pool.wait_ge(s_mh, 1)
        norm_pool(pool, 0)
        turn_pool(pool, 0, h32, hh, hl)
        a1_norms_pool(pool)
        scan(pool, nc.gpsimd, ch, 0, "pool")
        scan(pool, nc.gpsimd, ch, 2, "pool")
        norm_pool(pool, 1)
        turn_pool(pool, 1, h32, hh, hl)
        pool.wait_ge(s_tp, 16)
        nc.gpsimd.memset(xacc[:], 0.0).then_inc(s_zero, 1)
        rest_pool(pool)

    @block.scalar
    def _(act):
        ssm_params_act(act)
        nc.scalar.activation(cond[:], cols[:, 0:48], ACT.Silu).then_inc(s_sil, 1)
        bbar_turn_act(act)
        turn_act(act, 0, h32, hh)
        pairs_act(act, U_IN, 4, in_evac)
        u_turn_act(act)
        act.wait_ge(s_cpad, 16)
        nc.scalar.mul(cpad[:, 1], cpad[:, 1], -1.0).then_inc(s_cneg, 1)
        bu_act(act, 0)
        bu_act(act, 1)
        a1_act(act)
        a1_out_act(act)
        bu_act(act, 2)
        y_act(act, 0)
        bu_act(act, 3)
        for q in (1, 2, 3):
            y_act(act, q)
        glu_act(act)
        gate_act(act, 0, row1)
        pairs_act(act, U_OUT, 2, None)
        turn_act(act, 1, h32, hh)
        ffn_steps(act, lambda c, q, per, lo: hidden_act(act, ffn, c))
        hidden_end_act(act, ffn)
        gate_act(act, 1, row2)
        rest_act(act)

    @block.vector
    def _(dve):
        ch = Chain(dve, s_chd)
        dve.wait_ge(s_const, 16)
        ssm_params_dve(dve, ch)
        nc.vector.memset(neg[:], 0.0).then_inc(s_chd_ssm, 1)
        dve.wait_ge(s_sil, 1)
        for q in range(2):
            for j in range(4):
                ada_sum(dve, q, j)
        ada_store(dve, 0)
        with dve.Fori(1, 4) as i:
            for q in range(2):
                for j in range(4):
                    ada_sum(dve, q, j, 2, i)
            ada_store(dve, 0, 2, i)
        dve.wait_ge(s_x, 16)
        norm_dve(dve, ch, 0, x, xn, True)
        dve.wait_ge(s_mod, 8)
        ch(nc.vector.scalar_tensor_tensor(out=mscale[:], in0=modc[:, 16:32], scalar=1.0, in1=cols[:, COLS["n1"]],
                                          op0=ALU.add, op1=ALU.mult))
        ch.wait()
        turn_dve(dve, 0, h32, mscale, modc[:, 0:16])
        pairs_dve(dve, U_IN, 8, 4)
        a1_norms_dve(dve, ch)
        a1_dve(dve, ch)
        a1_out_dve(dve)
        scan(dve, nc.vector, ch, 1, "dve")
        y_dve(dve, 0)
        y_dve(dve, 1)
        scan(dve, nc.vector, ch, 3, "dve")
        y_low(dve, 0)
        y_low(dve, 1)
        y_dve(dve, 2)
        y_dve(dve, 3)
        y_low(dve, 2)
        y_low(dve, 3)
        glu_dve(dve)
        gate_dve(dve, 0, 32, diag)
        dve.wait_ge(s_growc, 4)
        pairs_dve(dve, U_OUT, 16, 2, ch=ch, ch_per=2,
                  evac=lambda e, c, per, i: gated(e, ch, c, per, i, U_OUT, x, x, 1.0, s_oev, row1, mixed_tmp))
        dve.wait_ge(s_oev, 4)
        norm_dve(dve, ch, 1, x, xn, True)
        dve.wait_ge(s_mod, 20)
        ch(nc.vector.scalar_tensor_tensor(out=mscale[:], in0=modc[:, 64:80], scalar=1.0, in1=cols[:, COLS["n2"]],
                                          op0=ALU.add, op1=ALU.mult))
        ch.wait()
        turn_dve(dve, 1, h32, mscale, modc[:, 48:64])
        ffn_steps(dve, lambda c, q, per, lo: hidden_dve(dve, ffn, c, q, per, lo))
        hidden_end_dve(dve, ffn)
        gate_dve(dve, 1, 80, diag)
        rest_dve(dve, ch)

    @block.tensor
    def _(pe):
        pe.wait_ge(s_one, 16)
        bbar_turn_pe(pe)
        pe.wait_ge(s_ones, 1)
        ada_reduce(pe, 0)
        with pe.Fori(1, 4) as i:
            ada_reduce(pe, 0, 2, i)
        turn_pe(pe, 0, xn, 0)
        pe.wait_ge(s_hl, 8)
        pairs_pe(pe, U_IN, 8, 4, s_inev)
        u_turn_pe(pe)
        bu_pe(pe, 0)
        bu_pe(pe, 1)
        a1_pe(pe)
        a1_out_pe(pe)
        y_pe(pe, 0)
        bu_pe(pe, 2)
        y_pe(pe, 1)
        bu_pe(pe, 3)
        y_pe(pe, 2)
        y_pe(pe, 3)
        glu_pe(pe)
        gate_pe(pe, 0, diag)
        pe.wait_ge(s_gl, 4)
        pe.wait_ge(s_al, 4)
        pairs_pe(pe, U_OUT, 16, 2, s_oev)
        turn_pe(pe, 1, xn, 1)
        pe.wait_ge(s_hl, 16)
        ffn_steps(pe, lambda c, q, per, lo: hidden_pe(pe, ffn, c, q, per, lo))
        hidden_end_pe(pe, ffn)
        gate_pe(pe, 1, diag)
        rest_pe(pe)
    ctx.close()


def col(a):
    a = np.asarray(a, np.float32).reshape(-1, P)
    return a.T


def shape_tables():
    t, k = np.arange(S)[:, None], np.arange(S)[None, :]
    d = t - k
    n = ((d >= 0) & (d <= 128)).astype(np.float32) + ((d >= 0) & (d <= 512) & (d % 4 == 0)) \
        + ((d >= 0) & (d <= 2048) & (d % 16 == 0))
    ang = 2 * np.pi * (np.outer(np.arange(S), np.arange(S)) % S) / S
    dft = np.concatenate([np.cos(ang), np.sin(ang)], 1) / 16
    out = {
        "dist": np.where(n > 0, d, 1e33).astype(np.float32), "count": n.astype(np.float32),
        "ident": np.eye(P, dtype=np.float32),
        "dft": dft.astype(np.float32), "dft2": (-np.sin(ang) / 16).astype(np.float32),
    }
    r, c = np.meshgrid(np.arange(S // 64), np.arange(64), indexing="ij")
    for name, rot in (("rope_a", 64), ("rope_b", 128)):
        nf = rot // 4
        inv = (np.float32(10000.0) ** (-np.arange(nf, dtype=np.float32) / np.float32(nf))).astype(np.float32)
        a = np.concatenate([r.reshape(-1, 1).astype(np.float32) * inv, c.reshape(-1, 1).astype(np.float32) * inv], 1)
        cs, sn = np.cos(a).astype(np.float32), np.sin(a).astype(np.float32)
        out[name] = np.concatenate([np.repeat(cs, 2, 1), np.stack([-sn, sn], 2).reshape(S, rot)], 1)
    return out


def kernel(**inputs):
    import concourse.bacc as bacc
    from concourse.bass_utils import run_bass_kernel_spmd

    a = {k: np.asarray(v) for k, v in inputs.items()}
    tables = shape_tables()

    def states(v):
        return v.reshape(PAIRS, 2, STATE).transpose(1, 2, 0).reshape(P, PAIRS)

    def pad(v):
        v = v.reshape(PAIRS, 2, STATE, GCH)
        o = np.zeros((2, STATE, PAIRS, 2, GCH), np.float32)
        for g in range(2):
            o[g, :, :, g] = v[:, g].transpose(1, 0, 2)
        return o.reshape(P, PAIRS * 2 * GCH)

    slope = -(2.0 ** -np.arange(1, HEADS + 1, dtype=np.float32))
    parts = {
        "c": col(a["c"]), "c2": col(a["c_2"]), "cctx": col(a["c_ctx_2"]), "n1": col(a["norm1_w"]),
        "n2": col(a["norm2_w"]), "bada": col(a["b_ada"]), "bada2": col(a["ada_b_2"]), "qn": col(a["q_norm_w"]),
        "kn": col(a["k_norm_w"]), "ssmd": col(a["ssm_d"]), "ql": col(a["q_lora_norm_2"]),
        "kvl": col(a["kv_lora_norm_2"]), "are": states(a["ssm_a_re"][0]), "aim": states(a["ssm_a_im"][0]),
        "ldt": states(np.repeat(a["ssm_log_dt"][0][:, None], STATE, 1)), "slope": np.repeat(slope[None], P, 0),
    }
    arrays = {
        "cols": np.concatenate([parts[k] for k in COLS], 1),
        "b_pad": np.stack([pad(a["ssm_b_re"][0]), pad(a["ssm_b_im"][0])]),
        "c_pad": np.stack([pad(a["ssm_c_re"][0].transpose(0, 2, 1)), pad(a["ssm_c_im"][0].transpose(0, 2, 1))]),
    }
    arrays.update(tables)
    for k in ("x", "ctx_2", "w_ada", "ada_w_2", "w_in", "ssm_w_glu", "w_out", "w_ffn_gate", "w_ffn_up", "w_ffn_down",
              "w_in_attn_2", "wq_b_2", "wkv_b_2", "w_out_attn_2", "w_in_fourier_2", "w_out_fourier_2",
              "ln_g_2", "ln_b_2", "q_norm_b_2", "k_norm_b_2"):
        arrays[k] = a[k]
    arrays = {k: np.ascontiguousarray(v) for k, v in arrays.items()}
    nc = bacc.Bacc("TRN2", target_bir_lowering=False, num_devices=1, dynamic_dma_scratch_size=1024)
    dram = {k: nc.dram_tensor("in_" + k, v.shape, F32, kind="ExternalInput").ap() for k, v in arrays.items()}
    out = nc.dram_tensor("out", (1, S, D), F32, kind="ExternalOutput").ap()
    program(nc, dram, out)
    r = run_bass_kernel_spmd(nc, [{"in_" + k: v for k, v in arrays.items()}], core_ids=[0])
    return r.results[0]["out"]
```

```python
from contextlib import ExitStack

import numpy as np

import concourse.bass as bass
from concourse import mybir

P = 128
D = 2048
S = 256
TT = S // P
KT = D // P
CW = 512
F32 = mybir.dt.float32
F32R = mybir.dt.float32r
ACT = mybir.ActivationFunctionType
ALU = mybir.AluOpType
AX = mybir.AxisListType.X

SSM_W = 1024
GROUPS, STATE, GCH = 64, 64, 16
PAIRS = GROUPS // 2
HEADS, HD = 8, 128
FFN = 5632
FFN_CH = FFN // CW
QL, KVL, ROPE = 768, 512, 64
LN_EPS = RMS_EPS = 1e-6
ALPHA = 4.0 ** 0.25
A_SCALE = (128 + 64) ** -0.5
B_SCALE = 128 ** -0.5
FCH = 8

RING = 8
SPLITS = 4
UPC = KT // 2

U_IN = 0
U_GLU = U_IN + 8 * UPC
U_OUT = U_GLU + 8
U_FFN = U_OUT + 4 * UPC
U_AIN = U_FFN + FFN_CH * 24
U_PAIR = U_AIN + 11 * UPC
U_AOUT = U_PAIR + 4 * 8
U_FOU = U_AOUT + 4 * UPC

COLS = {}
_o = 0
for _n, _w in (("c", 16), ("c2", 16), ("cctx", 16), ("n1", 16), ("n2", 16), ("bada", 96), ("bada2", 96), ("qn", 1),
               ("kn", 1), ("ssmd", 8), ("ql", 6), ("kvl", 4), ("are", 32), ("aim", 32), ("ldt", 32), ("slope", 8)):
    COLS[_n] = slice(_o, _o + _w)
    _o += _w
NCOLS = _o


def at(n, per=0, i=None):
    return n if i is None else i * per + n


class Chain:

    def __init__(self, eng, sem):
        self.eng, self.sem, self.n, self.i, self.lo, self.per, self.n0 = eng, sem, 0, None, 0, 0, 0

    def __call__(self, ins):
        ins.then_inc(self.sem, 1)
        self.n += 1

    def wait(self):
        if self.i is None:
            self.eng.wait_ge(self.sem, self.n)
        else:
            self.eng.wait_ge(self.sem, self.i * self.per + (self.n - self.lo * self.per))

    def enter(self, i, lo, per):
        self.i, self.lo, self.per, self.n0 = i, lo, per, self.n

    def leave(self, hi):
        assert self.n - self.n0 == self.per, (self.n - self.n0, self.per)
        self.n = self.n0 + self.per * (hi - self.lo)
        self.i = None


def program(nc, dram, out):
    ctx = ExitStack()
    sem_names = {}

    def sem(name):
        if name not in sem_names:
            sem_names[name] = ctx.enter_context(nc.semaphore(name))
        return sem_names[name]

    def sb(stack, name, shape, dt=F32):
        return stack.enter_context(nc.sbuf_tensor(name, shape, dt))

    raw = sb(ctx, "raw", [P, RING, 2, CW])
    whi = sb(ctx, "whi", [P, SPLITS, 2, CW], F32R)
    wlo = sb(ctx, "wlo", [P, SPLITS, 2, CW], F32R)
    araw = sb(ctx, "araw", [P, 4, 2, CW])
    acc = sb(ctx, "acc", [P, 2, CW])
    powers = sb(ctx, "powers", [P, 2, CW])
    a1 = ExitStack()
    squares = sb(a1, "qk_square", [P, 8 * CW])
    a1.close()
    hh = sb(ctx, "hh", [P, KT, S], F32R)
    a1 = ExitStack()
    hlf = sb(a1, "a1_buffers", [P, 4 * CW])
    a1.close()
    hl = sb(ctx, "hl", [P, KT, S], F32R)
    x = sb(ctx, "x", [P, TT, D])
    xacc = sb(ctx, "xacc", [P, TT, D])
    ident = sb(ctx, "ident", [P, P])
    ones = sb(ctx, "ones", [P, P])
    cols = sb(ctx, "cols", [P, NCOLS])
    cond = sb(ctx, "cond", [P, 48])
    modc = sb(ctx, "modc", [P, 192])
    modx = sb(ctx, "modx", [P, 32])
    mscalex = sb(ctx, "mscalex", [P, KT])
    mscale = sb(ctx, "mscale", [P, KT])
    stat = sb(ctx, "stat", [P, TT, 4, 6])
    mv = sb(ctx, "mv", [P, TT, 2])
    rstd = sb(ctx, "rstd", [P, TT, 1])
    ms = sb(ctx, "ms", [P, TT, 1])
    mhalf = sb(ctx, "mhalf", [P, 32])

    psum = ctx.enter_context(nc.psum_tensor("psum", [P, 8, CW], F32))

    h32 = sb(ctx, "h32", [P, 2, 2, S])
    aim2 = sb(ctx, "aim2", [P, 2, 2, PAIRS])
    msq = sb(ctx, "msq", [P, TT, 16])
    rqk = sb(ctx, "rqk", [P, TT, 16])
    neg = sb(ctx, "neg", [P, TT])
    den = sb(ctx, "den", [P, TT])
    rden = sb(ctx, "rden", [P, 2, TT])
    qcol = sb(ctx, "qcol", [P, 1])

    m = ExitStack()
    proj = sb(m, "proj", [P, TT, 4096])
    hB = sb(m, "hB", [P, 2, 8, S])
    BT = sb(m, "BT", [P, 2, 8, P])
    ptmp = sb(m, "pool_scan_tmp", [P, 900])
    m.close()
    row1 = proj[:, 1, 1024:3072]
    hA = xacc[:].rearrange("p a b -> p (a b)").rearrange("p (r g t) -> p r g t", r=2, g=8)

    s_raw = [sem(f"raw_landed{j}") for j in range(RING)]
    s_araw = [sem(f"ada_landed{j}") for j in range(4)]
    s_hi, s_lo, s_mm = sem("unit_high"), sem("unit_low"), sem("unit_used")
    s_acc, s_red, s_mod = sem("ada_ops"), sem("ada_reduced"), sem("mod_ready")
    s_arow, s_atr, s_col = sem("ada_row"), sem("ada_row_turned"), sem("ada_columns")
    arow = h32[:].rearrange("p a b c -> p (a b c)")[:, 0:CW]
    block = ctx.enter_context(nc.Block())

    def w_rows(w, kt, kn):
        return w.rearrange("(k p) n -> p k n", p=P)[:, kt:kt + kn]

    def load(sp, u, src, w=CW, per=0, i=None):
        kn = src.shape[1]
        if i is not None or u >= RING:
            sp.wait_ge(s_lo, at(u - RING + 1, per, i))
        sp.dma_start(raw[:, u % RING, 0:kn, 0:w], src).then_inc(s_raw[u % RING], 16)

    def high(act, u, w=CW, kn=2, per=0, i=None):
        act.wait_ge(s_raw[u % RING], at(16 * (u // RING + 1), 16 * (per // RING), i))
        if i is not None or u >= SPLITS:
            act.wait_ge(s_mm, at(u - SPLITS + 1, per, i))
        nc.scalar.copy(whi[:, u % SPLITS, 0:kn, 0:w], raw[:, u % RING, 0:kn, 0:w]).then_inc(s_hi, 1)

    def low(dve, u, w=CW, kn=2, per=0, i=None):
        dve.wait_ge(s_hi, at(u + 1, per, i))
        if i is not None or u >= SPLITS:
            dve.wait_ge(s_mm, at(u - SPLITS + 1, per, i))
        nc.vector.tensor_tensor(wlo[:, u % SPLITS, 0:kn, 0:w], raw[:, u % RING, 0:kn, 0:w],
                                whi[:, u % SPLITS, 0:kn, 0:w].bitcast(F32), ALU.subtract).then_inc(s_lo, 1)

    def multiply(pe, u, tiles, kt, last_kt, w=CW, kn=2, per=0, i=None, first_kt=0):
        pe.wait_ge(s_lo, at(u + 1, per, i))
        for k in range(kn):
            for ah, al, t, bank in tiles:
                o = psum[:, bank, 0:w]
                a = slice(t * P, t * P + P)
                h, lw = whi[:, u % SPLITS, k, 0:w], wlo[:, u % SPLITS, k, 0:w]
                nc.tensor.matmul(o, ah[:, kt + k, a], h, start=(kt + k == first_kt), stop=False)
                nc.tensor.matmul(o, ah[:, kt + k, a], lw, start=False, stop=False)
                ins = nc.tensor.matmul(o, al[:, kt + k, a], h, start=False, stop=(kt + k == last_kt))
        ins.then_inc(s_mm, 1)

    def lat(b0):
        return [(hh, hl, t, b0 + t) for t in range(TT)]

    def place(q):
        return q - 8 if 24 <= q < 32 else q + 8 if 16 <= q < 24 else q

    def rank(g):
        return g if g < 8 else g - 8

    def dve_rank(g):
        return g - 8 if g < 16 else g - 16

    def ada_src(q, perq=0, i=None):
        if q < 24:
            w, c = dram["w_ada"][0], q
        elif q < 36:
            w, c = dram["ada_w_2"][0], q - 24
        else:
            w, c = dram["ada_w_2"][1], q - 36
        return w.rearrange("(k p) n -> p k n", p=P), at(c * CW, perq * CW, i)

    def ada_load(sp, q, jj, perq=0, i=None):
        src, c = ada_src(q, perq, i)
        for n in (2 * jj, 2 * jj + 1):
            if i is not None or q >= 1 or n >= 4:
                sp.wait_ge(s_acc, at(16 * place(q) + 2 * (n - 3), 16 * perq, i))
            sp.dma_start(araw[:, n % 4], src[:, 2 * n:2 * n + 2, bass.ds(c, CW)]).then_inc(s_araw[n % 4], 16)

    def ada_landed(eng, g, kt, perq, i):
        eng.wait_ge(s_araw[kt // 2 % 4], at(16 * (2 * g + kt // 8 + 1), 32 * perq, i))

    def ada_mult(pe, g, jj, perq=0, i=None):
        if jj == 0 and (i is not None or g >= 1):
            pe.wait_ge(s_arow, at(rank(g), perq, i))
        for kt in range(4 * jj, 4 * jj + 4):
            if kt % 2 == 0:
                ada_landed(pe, g, kt, perq, i)
            v = cond[:, kt:kt + 1] if g < 8 else cond[:, 16 + kt:48:16]
            ins = nc.tensor.matmul(psum[0:1 if g < 8 else 2, 6], v, araw[:, kt // 2 % 4, kt % 2], start=(kt == 0),
                                   stop=(kt == 15))
            if kt % 2:
                ins.then_inc(s_acc, 2)

    def ada_turn(pe, g, perq=0, i=None):
        pe.wait_ge(s_arow, at(rank(g) + 1, perq, i))
        if i is not None or g >= 1:
            pe.wait_ge(s_col, at(rank(g), perq, i))
        n = 1 if g < 8 else 2
        for j in range(4):
            ins = nc.tensor.matmul(psum[:, 7, n * j:n * j + n], arow[0:n, j * P:(j + 1) * P], ident[0:n, 0:n],
                                   start=True, stop=True)
        ins.then_inc(s_atr, 1)

    def ada_row(act, g, perq=0, i=None):
        act.wait_ge(s_acc, at(16 * g + 16, 16 * perq, i))
        if i is not None or g >= 1:
            act.wait_ge(s_atr, at(rank(g), perq, i))
        n = 1 if g < 8 else 2
        nc.scalar.copy(arow[0:n], psum[0:n, 6]).then_inc(s_arow, 1)

    def ada_col(act, g, perq=0, i=None):
        act.wait_ge(s_atr, at(rank(g) + 1, perq, i))
        if g >= 8:
            nc.scalar.copy(modx[:, bass.ds(at(4 * (g - 16), 4 * perq, i), 4)], psum[:, 7, 1:8:2])
        q = g + 8 if g >= 8 else g
        nc.scalar.copy(modc[:, bass.ds(at(4 * q, 4 * perq, i), 4)],
                       psum[:, 7, 0:8:2] if g >= 8 else psum[:, 7, 0:4]).then_inc(s_col, 1)

    def ada_chunk_pe(pe, g, perq=0, i=None, turn=True):
        for jj in range(4):
            ada_mult(pe, g, jj, perq, i)
            if jj == 1 and turn:
                ada_turn(pe, g - 1, perq, i)

    def ada_chunk_act(act, g, perq=0, i=None):
        ada_row(act, g - 1, perq, i)
        ada_col(act, g - 1, perq, i)

    def add_bias(ch, dst, c0, n):
        ch(nc.vector.tensor_tensor(dst, dst, cols[:, COLS["bada"].start + c0:COLS["bada"].start + c0 + n], ALU.add))

    def ada_sum(dve, q, jj, perq=0, i=None):
        g = place(q)
        if jj == 0 and (i is not None or g >= 10):
            dve.wait_ge(s_red, at(dve_rank(g) - g % 2, perq, i))
        for kt in range(4 * jj, 4 * jj + 4):
            if kt % 2 == 0:
                ada_landed(dve, g, kt, perq, i)
            c0 = 0 if q < 24 else 16
            dst, w, s = acc[:, q % 2], araw[:, kt // 2 % 4, kt % 2], cond[:, c0 + kt:c0 + kt + 1]
            if kt == 0:
                ins = nc.vector.tensor_scalar(dst, w, s, None, ALU.mult)
            else:
                dve.wait_ge(s_acc, at(16 * g + kt, 16 * perq, i))
                ins = nc.vector.scalar_tensor_tensor(out=dst, in0=w, scalar=s, in1=dst, op0=ALU.mult, op1=ALU.add)
            ins.then_inc(s_acc, 1)

    def ada_reduce(pe, q, perq=0, i=None):
        g = place(q)
        pe.wait_ge(s_acc, at(16 * (g + 2), 16 * perq, i))
        if i is not None or g not in (8, 24):
            pe.wait_ge(s_mod, at(dve_rank(g), perq, i))
        else:
            pe.wait_ge(s_col, 8 if g == 8 else 16)
        for c in range(2):
            for j in range(4):
                ins = nc.tensor.matmul(psum[:, 7, 4 * c + j:4 * c + j + 1], acc[:, c, j * P:(j + 1) * P], ones[:, 0:1],
                                       start=True, stop=True)
        ins.then_inc(s_red, 2)

    def ada_store(dve, q, perq=0, i=None):
        dve.wait_ge(s_red, at(dve_rank(place(q)) + 2, perq, i))
        bias = cols[:, bass.ds(at(COLS["bada"].start + 4 * q, 4 * perq, i), 8)]
        nc.vector.tensor_tensor(modc[:, bass.ds(at(4 * q, 4 * perq, i), 8)], psum[:, 7, 0:8], bias,
                                ALU.add).then_inc(s_mod, 2)

    s_st, s_rs, s_xn = sem("norm_stats"), sem("norm_rstd"), sem("normed")
    s_tp, s_h32, s_hh, s_hl = sem("turned"), sem("turned32"), sem("turned_high"), sem("turned_low")
    s_turn_mod = sem("turn_factors")

    def norm_dve(dve, ch, k, src, xn, rms):
        for t in range(TT):
            for c in range(4):
                ch(nc.vector.bn_stats(stat[:, t, c], src[:, t, c * CW:(c + 1) * CW]))
        ch.wait()
        for t in range(TT):
            ch(nc.vector.bn_aggr(mv[:, t], stat[:, t].rearrange("p c s -> p (c s)")))
        ch.wait()
        if rms:
            ch(nc.vector.tensor_tensor(ms[:], mv[:, :, 0:1], mv[:, :, 0:1], ALU.mult))
            ch.wait()
            ch(nc.vector.tensor_tensor(ms[:], ms[:], mv[:, :, 1:2], ALU.add))
            ch.wait()
            nc.vector.tensor_scalar(ms[:], ms[:], LN_EPS, None, ALU.add).then_inc(s_st, 1)
        else:
            nc.vector.tensor_scalar(ms[:], mv[:, :, 1:2], LN_EPS, None, ALU.add).then_inc(s_st, 1)
        dve.wait_ge(s_rs, k + 1)
        for t in range(TT):
            if rms:
                ins = nc.vector.tensor_scalar(xn[:, t], src[:, t], rstd[:, t], None, ALU.mult)
            else:
                ins = nc.vector.tensor_scalar(xn[:, t], src[:, t], mv[:, t, 0:1], rstd[:, t], ALU.subtract, ALU.mult)
            ins.then_inc(s_xn, 1)

    def norm_pool(pool, k):
        pool.wait_ge(s_st, k + 1)
        nc.gpsimd.tensor_tensor(rstd[:], ms[:], mhalf[:, 0:2].unsqueeze(2), ALU.pow).then_inc(s_rs, 1)

    def turn_pe(pe, k, xn, kn):
        pe.wait_ge(s_xn, 2 * kn + 2)
        for r in range(8):
            if 8 * k + r >= 2:
                pe.wait_ge(s_h32, 8 * k + r - 1)
            for j in range(2):
                for t in range(TT):
                    kt = 2 * r + j
                    ins = nc.tensor.transpose(psum[:, 4 + r % 2, j * S + t * P:j * S + t * P + P],
                                              xn[:, t, kt * P:(kt + 1) * P], ident[:])
            ins.then_inc(s_tp, 1)

    def turn_dve(dve, k, h32, scale, shift):
        for r in range(8):
            n = 8 * k + r
            dve.wait_ge(s_tp, n + 1)
            if n >= 2:
                dve.wait_ge(s_hl, n - 1)
            for j in range(2):
                kt = 2 * r + j
                ins = nc.vector.tensor_scalar(h32[:, r % 2, j], psum[:, 4 + r % 2, j * S:(j + 1) * S],
                                              scale[:, kt:kt + 1], shift[:, kt:kt + 1], ALU.mult, ALU.add)
            ins.then_inc(s_h32, 1)

    def turn_act(act, k, h32, oh):
        for r in range(8):
            act.wait_ge(s_h32, 8 * k + r + 1)
            nc.scalar.copy(oh[:, 2 * r:2 * r + 2], h32[:, r % 2]).then_inc(s_hh, 1)

    def turn_pool(pool, k, h32, oh, ol):
        for r in range(8):
            pool.wait_ge(s_hh, 8 * k + r + 1)
            nc.gpsimd.tensor_tensor(ol[:, 2 * r:2 * r + 2], h32[:, r % 2], oh[:, 2 * r:2 * r + 2].bitcast(F32),
                                    ALU.subtract).then_inc(s_hl, 1)

    s_diag, s_grow, s_growc = sem("gate_diag"), sem("gate_spread"), sem("gate_row")

    def gate_dve(dve, k, col0, diag):
        for r in range(4):
            n = 4 * k + r
            if n >= 2:
                dve.wait_ge(s_grow, n - 1)
            for j in range(4):
                c = col0 + 4 * r + j
                ins = nc.vector.tensor_scalar(diag[:, r % 2, j * P:(j + 1) * P], ident[:], modc[:, c:c + 1], None,
                                              ALU.mult)
            ins.then_inc(s_diag, 1)

    def gate_pe(pe, k, diag):
        for r in range(4):
            n = 4 * k + r
            pe.wait_ge(s_diag, n + 1)
            if n >= 1:
                pe.wait_ge(s_growc, n)
            nc.tensor.matmul(psum[:, 6], ones[:], diag[:, r % 2], start=True, stop=True).then_inc(s_grow, 1)

    def gate_act(act, k, row):
        for r in range(4):
            act.wait_ge(s_grow, 4 * k + r + 1)
            nc.scalar.copy(row[:, r * CW:(r + 1) * CW], psum[:, 6]).then_inc(s_growc, 1)

    rawf = raw[:].rearrange("p a b c -> p (a b c)")
    arawf = araw[:].rearrange("p a b c -> p (a b c)")
    xn = xacc
    diag = h32[:].rearrange("p a b c -> p a (b c)")

    small = [rawf[:, 32 * n:32 * n + 32] for n in range(24)]
    bpad = rawf[:, 1024:3072].rearrange("p (r g c) -> p r g c", r=2, g=PAIRS)
    bbar = rawf[:, 3072:5120].rearrange("p (r g c) -> p r g c", r=2, g=PAIRS)
    btmp = rawf[:, 5120:6144].rearrange("p (g c) -> p g c", g=PAIRS)
    apow = powers[:].rearrange("p a b -> p (a b)").rearrange("p (r g j) -> p r g j", r=2, g=PAIRS)
    cpad = rawf[:, 6144:8192].rearrange("p (r g c) -> p r g c", r=2, g=PAIRS)
    staged = hlf[:, 0:512].rearrange("p (t q e) -> p t q e", t=TT, q=2)
    qkT = hlf[:, 512:1024].rearrange("p (q s) -> p q s", q=2)
    prob = hlf[:, 1024:1536].rearrange("p (t s) -> p t s", t=TT)
    probT = hlf[:, 1536:2048].rearrange("p (k s) -> p k s", k=2)
    dist = rawf[:, 0:512].rearrange("p (t s) -> p t s", t=TT)
    count = rawf[:, 512:1024].rearrange("p (t s) -> p t s", t=TT)
    scan_tmp = {"pool": ptmp, "dve": rawf[:, 4096:4996]}

    s_const, s_x, s_sil, s_one = sem("consts_landed"), sem("x_landed"), sem("cond_ready"), sem("ones_set")
    s_b, s_cpad, s_dist = sem("b_landed"), sem("c_landed"), sem("masks_landed")
    s_fun, s_arg = sem("ssm_functions"), sem("ssm_arguments")
    s_bbar, s_bt, s_BT = sem("bbar_ready"), sem("bbar_turned"), sem("BT_ready")
    s_inev = sem("proj_stored")
    s_ut, s_uT = sem("u_turned"), sem("uT_ready")
    s_bu, s_H = sem("bu_summed"), sem("bu_stored")
    s_scan = {"pool": sem("pool_scanned"), "dve": sem("dve_scanned")}
    s_y, s_yv, s_yg, s_yh, s_yl = (sem(n) for n in ("y_summed", "y_skipped", "y_gelu", "y_high", "y_low"))
    s_stg, s_qkt, s_qkT, s_sc, s_mx, s_ex, s_pr, s_pt, s_pT, s_pv, s_ya = (sem("a1_" + n) for n in (
        "staged", "qk_turned", "qkT", "scores", "max", "exp", "prob", "p_turned", "pT", "pv", "y"))
    s_ms, s_rq, s_qc = sem("qk_squares"), sem("qk_rstd"), sem("q_factor")
    s_at, s_ah, s_al = sem("attn_turned"), sem("attn_high"), sem("attn_low")
    s_glu, s_sg, s_gt, s_gy, s_gh, s_gl = (sem("glu_" + n) for n in ("done", "sigmoid", "turned", "y", "high", "low"))
    s_chd, s_chp, s_cha = sem("dve_chain"), sem("pool_chain"), sem("act_chain")
    s_cneg = sem("c_negated")
    s_chd_ssm, s_mh, s_ones = sem("ssm_params"), sem("minus_half"), sem("ones")

    TWO_PI = 2.0 * np.pi
    C1 = 6.28125
    C2 = float(np.float32(np.round((TWO_PI - C1) * 2 ** 20) / 2 ** 20))
    C3 = float(np.float32(TWO_PI - C1 - C2))
    MAGIC = 12582912.0
    PI_IN = float(np.nextafter(np.float32(np.pi), np.float32(0)))

    def ssm_params_dve(dve, ch):
        V = nc.vector
        def tt(o, a, b, op):
            ch(V.tensor_tensor(o, a, b, op))
            ch.wait()
        are, aim = cols[:, COLS["are"]], cols[:, COLS["aim"]]
        dt, lg, th, mag, kk, r, r2, cs, sn, nr, dn, zr, zi, t0, t1 = small[:15]
        dve.wait_ge(s_fun, 1)
        V.tensor_tensor(lg, are, dt, ALU.mult).then_inc(s_arg, 1)
        tt(th, aim, dt, ALU.mult)
        ch(V.tensor_scalar(kk, th, float(np.float32(1 / TWO_PI)), MAGIC, ALU.mult, ALU.add))
        ch.wait()
        ch(V.tensor_scalar(kk, kk, MAGIC, None, ALU.subtract))
        ch.wait()
        for n, (c, a) in enumerate(((C1, th), (C2, r), (C3, r))):
            ch(V.scalar_tensor_tensor(out=r, in0=kk, scalar=-c, in1=a, op0=ALU.mult, op1=ALU.add))
            ch.wait()
        ch(V.tensor_scalar(r, r, PI_IN, -PI_IN, ALU.min, ALU.max))
        ch.wait()
        ch(V.scalar_tensor_tensor(out=r2, in0=r, scalar=-1.0, in1=r, op0=ALU.mult, op1=ALU.max))
        ch.wait()
        V.tensor_scalar(r2, r2, -1.0, float(np.pi / 2), ALU.mult, ALU.add).then_inc(s_arg, 1)
        dve.wait_ge(s_fun, 4)
        ar, ai = apow[:, 0, :, 0], apow[:, 1, :, 0]
        tt(ar, mag, cs, ALU.mult)
        tt(ai, mag, sn, ALU.mult)
        ch(V.tensor_scalar(nr, ar, 1.0, None, ALU.subtract))
        tt(t0, are, are, ALU.mult)
        tt(t1, aim, aim, ALU.mult)
        tt(dn, t0, t1, ALU.add)
        ch(V.reciprocal(dn, dn))
        tt(t0, nr, are, ALU.mult)
        tt(t1, ai, aim, ALU.mult)
        tt(zr, t0, t1, ALU.add)
        tt(zr, zr, dn, ALU.mult)
        tt(t0, ai, are, ALU.mult)
        tt(t1, nr, aim, ALU.mult)
        tt(zi, t0, t1, ALU.subtract)
        tt(zi, zi, dn, ALU.mult)
        zrb, zib = (z.unsqueeze(2).broadcast_to([P, PAIRS, 2 * GCH]) for z in (zr, zi))
        dve.wait_ge(s_b, 16)
        tt(bbar[:, 0], zrb, bpad[:, 0], ALU.mult)
        tt(btmp, zib, bpad[:, 1], ALU.mult)
        tt(bbar[:, 0], bbar[:, 0], btmp, ALU.subtract)
        tt(bbar[:, 1], zrb, bpad[:, 1], ALU.mult)
        tt(btmp, zib, bpad[:, 0], ALU.mult)
        V.tensor_tensor(bbar[:, 1], bbar[:, 1], btmp, ALU.add).then_inc(s_bbar, 1)
        for n in (1, 2, 4, 8):
            br, bi = (apow[:, q, :, n - 1:n].broadcast_to([P, PAIRS, n]) for q in range(2))
            pr, pi = apow[:, 0, :, 0:n], apow[:, 1, :, 0:n]
            ta, tb = (rawf[:, 6144 + 512 * q:6144 + 512 * q + PAIRS * n].rearrange("p (g j) -> p g j", g=PAIRS)
                      for q in range(2))
            tt(ta, pr, br, ALU.mult)
            tt(tb, pi, bi, ALU.mult)
            tt(apow[:, 0, :, n:2 * n], ta, tb, ALU.subtract)
            tt(ta, pr, bi, ALU.mult)
            tt(tb, pi, br, ALU.mult)
            tt(apow[:, 1, :, n:2 * n], ta, tb, ALU.add)
        for e, j in enumerate((0, 15)):
            ch(V.tensor_scalar(aim2[:, e, 1], apow[:, 1, :, j], -1.0, None, ALU.mult))
            ch(V.tensor_copy(aim2[:, e, 0], apow[:, 1, :, j]))
        ch.wait()

    def ssm_params_act(act):
        act.wait_ge(s_const, 16)
        nc.scalar.activation(small[0], cols[:, COLS["ldt"]], ACT.Exp).then_inc(s_fun, 1)
        act.wait_ge(s_arg, 1)
        nc.scalar.activation(small[3], small[1], ACT.Exp).then_inc(s_fun, 1)
        act.wait_ge(s_arg, 2)
        nc.scalar.activation(small[8], small[5], ACT.Sin).then_inc(s_fun, 1)
        nc.scalar.activation(small[7], small[6], ACT.Sin).then_inc(s_fun, 1)

    def bbar_turn_pe(pe):
        pe.wait_ge(s_bbar, 1)
        for n in range(4):
            if n >= 2:
                pe.wait_ge(s_BT, n - 1)
            for j in range(4):
                st = 4 * (n % 2) + j
                ins = nc.tensor.transpose(psum[:, n % 2, j * P:(j + 1) * P], bbar[:, n // 2, 4 * st:4 * st + 4]
                                          .rearrange("p g c -> p (g c)"), ident[:])
            ins.then_inc(s_bt, 1)

    def bbar_turn_act(act):
        for n in range(4):
            act.wait_ge(s_bt, n + 1)
            nc.scalar.copy(BT[:, n // 2, 4 * (n % 2):4 * (n % 2) + 4], psum[:, n % 2]
                           .rearrange("p (a b) -> p a b", a=4)).then_inc(s_BT, 1)

    def uT(a, n=1):
        return proj[:, a // 4, (a % 4) * S:(a % 4 + n) * S].rearrange("p (f s) -> p f s", f=n)

    def u_turn_pe(pe):
        pe.wait_ge(s_inev, 2)
        pe.wait_ge(s_mod, 4)
        for r in range(4):
            for j in range(2):
                for t in range(TT):
                    ft = 2 * r + j
                    ins = nc.tensor.transpose(psum[:, 4 + r, j * S + t * P:j * S + t * P + P],
                                              proj[:, t, ft * P:(ft + 1) * P], ident[:])
            ins.then_inc(s_ut, 1)

    def u_turn_act(act):
        for r in range(4):
            act.wait_ge(s_ut, 4)
            nc.scalar.copy(uT(2 * r, 2), psum[:, 4 + r].rearrange("p (a b) -> p a b", a=2)
                           ).then_inc(s_uT, 1)

    def bu_pe(pe, n):
        if n >= 8 and n % 4 == 0:
            pe.wait_ge(s_yv, n // 4 - 1)
        st = n // 2
        pe.wait_ge(s_uT, 4)
        if n >= 1:
            pe.wait_ge(s_H, n)
        for b in range(2):
            pp = 2 * (n % 2) + b
            rows = slice(32 * pp, 32 * pp + 32)
            for ri in range(2):
                ins = nc.tensor.matmul(psum[:, 4 + b, ri * S:(ri + 1) * S], BT[rows, ri, st], uT(st)[rows, 0],
                                       start=True, stop=True)
        ins.then_inc(s_bu, 1)

    def bu_act(act, n):
        h = (hA, hB)[n // 4 % 2]
        if n >= 8 and n % 4 == 0:
            act.wait_ge(s_y, n // 4 - 1)
        act.wait_ge(s_bu, n + 1)
        for ri in range(2):
            ins = nc.scalar.copy(h[:, ri, 2 * (n % 4):2 * (n % 4) + 2], psum[:, 4:6, ri * S:(ri + 1) * S])
        ins.then_inc(s_H, 1)

    def beside_pe(pe, j):
        if j == 0:
            u_turn_pe(pe)
        if 2 <= j < 10:
            bu_pe(pe, j - 2)

    def beside_act(act, j):
        if j == 2:
            u_turn_act(act)
        if 4 <= j < 12:
            bu_act(act, j - 4)

    SCANS = (("pool", 1), ("pool", 2), ("dve", 1), ("pool", 3))

    def scan(eng, isa, ch, q, who):
        h = (hA, hB)[q % 2]
        hv = h.rearrange("p r g (c j) -> p r g c j", j=16)
        g = slice(8 * q, 8 * q + 8)
        T = scan_tmp[who]
        if SCANS[q][1] > 1:
            eng.wait_ge(s_scan[who], SCANS[q][1] - 1)
        eng.wait_ge(s_H, 4 * q + 4)

        def tt(o, a, b, op):
            ch(isa.tensor_tensor(o, a, b, op))
            ch.wait()

        def advance(e, prev, nxt, t0, t1, wide):
            ar = apow[:, 0:1, g, 15 * e:15 * e + 1].rearrange("p r g j -> p r (g j)").broadcast_to([P, 2, 8])
            ai = aim2[:, e, :, g]
            if wide:
                ar, ai = ar.unsqueeze(3).broadcast_to([P, 2, 8, 16]), ai.unsqueeze(3).broadcast_to([P, 2, 8, 16])
            ch(isa.tensor_tensor(t0, ar, prev, ALU.mult))
            tt(t1[:, ::-1], ai, prev, ALU.mult)
            tt(t0, t0, t1, ALU.add)
            tt(nxt, nxt, t0, ALU.add)

        t0 = T[:, 0:256].rearrange("p (r g c) -> p r g c", r=2, g=8)
        t1 = T[:, 256:512].rearrange("p (r g c) -> p r g c", r=2, g=8)
        with eng.Fori(1, 16) as j:
            ch.enter(j, 1, 4)
            prev = hv[:, :, :, :, bass.ds(j - 1, 1)].rearrange("p r g c j -> p r g (c j)")
            nxt = hv[:, :, :, :, bass.ds(j, 1)].rearrange("p r g c j -> p r g (c j)")
            advance(0, prev, nxt, t0, t1, True)
            ch.leave(16)
        t0, t1 = (t.rearrange("p r g c -> p (r g c)")[:, 0:16].rearrange("p (r g) -> p r g", r=2) for t in (t0, t1))
        with eng.Fori(1, 16) as c:
            ch.enter(c, 1, 4)
            prev = h[:, :, :, bass.ds(c * 16 - 1, 1)].rearrange("p r g t -> p r (g t)")
            nxt = h[:, :, :, bass.ds(c * 16 + 15, 1)].rearrange("p r g t -> p r (g t)")
            advance(1, prev, nxt, t0, t1, False)
            ch.leave(16)
        t = T[:, 0:4 * 225].rearrange("p (g c j) -> p g c j", g=4, c=15)
        for half in (0, 4):
            gh = slice(8 * q + half, 8 * q + half + 4)
            for ro, pi, ei, op in ((0, 0, 0, ALU.add), (0, 1, 1, ALU.subtract), (1, 0, 1, ALU.add), (1, 1, 0, ALU.add)):
                pw = apow[:, pi, gh, 0:15].unsqueeze(2).broadcast_to([P, 4, 15, 15])
                end = hv[:, ei, half:half + 4, 0:15, 15:16].broadcast_to([P, 4, 15, 15])
                tt(t, pw, end, ALU.mult)
                o = hv[:, ro, half:half + 4, 1:16, 0:15]
                tt(o, o, t, op)
        isa.tensor_copy(T[:, 0:1], T[:, 1:2]).then_inc(s_scan[who], 1)

    def y_pe(pe, q):
        who, n = SCANS[q]
        pe.wait_ge(s_scan[who], n)
        pe.wait_ge(s_H, min(4 * q + 8, 16))
        if q == 0:
            pe.wait_ge(s_cneg, 1)
        if q >= 2:
            pe.wait_ge(s_yv, q - 1)
        h = (hA, hB)[q % 2]
        for sl in range(2):
            for pp in range(4):
                for ri in range(2):
                    ins = nc.tensor.matmul(psum[32 * pp:32 * pp + 32, 4 + q % 2, sl * S:(sl + 1) * S],
                                           cpad[:, ri, 8 * q + 4 * sl + pp], h[:, ri, 4 * sl + pp],
                                           start=(ri == 0), stop=(ri == 1))
        ins.then_inc(s_y, 1)

    def y_dve(dve, q):
        dve.wait_ge(s_y, q + 1)
        for sl in range(2):
            st = 2 * q + sl
            d = cols[:, COLS["ssmd"].start + st:COLS["ssmd"].start + st + 1]
            ins = nc.vector.scalar_tensor_tensor(out=uT(st)[:, 0], in0=uT(st)[:, 0], scalar=d,
                                                 in1=psum[:, 4 + q % 2, sl * S:(sl + 1) * S], op0=ALU.mult, op1=ALU.add)
        ins.then_inc(s_yv, 1)

    def y_act(act, q):
        act.wait_ge(s_yv, q + 1)
        y = uT(2 * q, 2)
        nc.scalar.activation(y, y, ACT.Gelu_apprx_tanh).then_inc(s_yg, 1)
        act.wait_ge(s_yg, q + 1)
        nc.scalar.copy(hh[:, 2 * q:2 * q + 2], y).then_inc(s_yh, 1)

    def y_low(dve, q):
        dve.wait_ge(s_yh, q + 1)
        nc.vector.tensor_tensor(hl[:, 2 * q:2 * q + 2], uT(2 * q, 2), hh[:, 2 * q:2 * q + 2].bitcast(F32),
                                ALU.subtract).then_inc(s_yl, 1)

    def a1_norms_dve(dve, ch):
        dve.wait_ge(s_inev, 8)
        sq = squares
        for t in range(TT):
            o = sq[:, 2048 * t:2048 * t + 2048]
            ch(nc.vector.tensor_tensor(o, proj[:, t, 1024:3072], proj[:, t, 1024:3072], ALU.mult))
            ch.wait()
            ch(nc.vector.tensor_reduce(msq[:, t], o.rearrange("p (h e) -> p h e", h=16), AX, ALU.add))
        ch.wait()
        nc.vector.tensor_scalar(msq[:], msq[:], 1.0 / HD, RMS_EPS, ALU.mult, ALU.add).then_inc(s_ms, 1)
        nc.vector.tensor_scalar(qcol[:], cols[:, COLS["qn"]], HD ** -0.5, None, ALU.mult).then_inc(s_qc, 1)
        dve.wait_ge(s_rq, 1)
        for t in range(TT):
            v = proj[:, t, 1024:3072].rearrange("p (h e) -> p h e", h=16)
            ins = nc.vector.tensor_tensor(v, v, rqk[:, t].unsqueeze(2).broadcast_to([P, 16, HD]), ALU.mult)
        ins.then_inc(s_ms, 1)

    def a1_norms_pool(pool):
        pool.wait_ge(s_ms, 1)
        e = mhalf[:].rearrange("p (t h) -> p t h", t=TT)
        nc.gpsimd.tensor_tensor(rqk[:], msq[:], e, ALU.pow).then_inc(s_rq, 1)

    qk = proj[:, :, 1024:3072].rearrange("p t (q n) -> p t q n", q=2)

    def a1_stage_act(act, h, i=None):
        if i is not None or h >= 1:
            act.wait_ge(s_qkt, at(h, 1, i))
        nc.scalar.copy(staged, qk[:, :, :, bass.ds(at(h * HD, HD, i), HD)]).then_inc(s_stg, 1)

    def a1_turn_pe(pe, h, i=None):
        pe.wait_ge(s_stg, at(h + 1, 1, i))
        if i is not None or h >= 1:
            pe.wait_ge(s_qkT, at(h, 1, i))
        for qq in range(2):
            for t in range(TT):
                ins = nc.tensor.transpose(psum[:, 0, qq * S + t * P:qq * S + t * P + P], staged[:, t, qq], ident[:])
        ins.then_inc(s_qkt, 1)

    def a1_qkT_act(act, h, i=None):
        act.wait_ge(s_qkt, at(h + 1, 1, i))
        if i is not None or h >= 1:
            act.wait_ge(s_sc, at(h, 1, i))
        nc.scalar.activation(qkT[:, 0], psum[:, 0, 0:S], ACT.Copy, scale=qcol[:, 0:1])
        nc.scalar.activation(qkT[:, 1], psum[:, 0, S:2 * S], ACT.Copy, scale=cols[:, COLS["kn"]]).then_inc(s_qkT, 1)

    def a1_scores_pe(pe, h, i=None):
        pe.wait_ge(s_qkT, at(h + 1, 1, i))
        if i is not None or h >= 1:
            pe.wait_ge(s_mx, at(h, 1, i))
        for t in range(TT):
            ins = nc.tensor.matmul(psum[:, 1, t * S:(t + 1) * S], qkT[:, 0, t * P:(t + 1) * P], qkT[:, 1],
                                   start=True, stop=True)
        ins.then_inc(s_sc, 1)

    def a1_max_dve(dve, ch, h, i=None):
        dve.wait_ge(s_sc, at(h + 1, 1, i))
        if i is not None or h >= 1:
            dve.wait_ge(s_pt, at(h, 1, i))
        sl = cols[:, bass.ds(at(COLS["slope"].start + h, 1, i), 1)]
        ch(nc.vector.scalar_tensor_tensor(out=prob.rearrange("p t s -> p (t s)"), in0=dist.rearrange("p t s -> p (t s)"),
                                          scalar=sl, in1=psum[:, 1], op0=ALU.mult, op1=ALU.add))
        ch.wait()
        ch(nc.vector.tensor_reduce(neg[:], prob, AX, ALU.max))
        ch.wait()
        nc.vector.tensor_scalar(neg[:], neg[:], -1.0, None, ALU.mult).then_inc(s_mx, 1)

    def a1_exp_act(act, h, i=None):
        act.wait_ge(s_mx, at(h + 1, 1, i))
        for t in range(TT):
            ins = nc.scalar.activation(prob[:, t], prob[:, t], ACT.Exp, bias=neg[:, t:t + 1])
        ins.then_inc(s_ex, 1)

    def a1_prob_dve(dve, ch, h, i=None):
        dve.wait_ge(s_ex, at(h + 1, 1, i))
        ch(nc.vector.tensor_tensor(prob, prob, count, ALU.mult))
        ch.wait()
        ch(nc.vector.tensor_reduce(den[:], prob, AX, ALU.add))
        ch.wait()
        nc.vector.reciprocal(rden[:, 0], den[:]).then_inc(s_pr, 1)

    def a1_pturn_pe(pe, h, i=None):
        pe.wait_ge(s_pr, at(h + 1, 1, i))
        if i is not None or h >= 1:
            pe.wait_ge(s_pT, at(h, 1, i))
        for kt in range(2):
            for t in range(TT):
                ins = nc.tensor.transpose(psum[:, 2, kt * S + t * P:kt * S + t * P + P],
                                          prob[:, t, kt * P:(kt + 1) * P], ident[:])
        ins.then_inc(s_pt, 1)

    def a1_pT_act(act, h, i=None):
        act.wait_ge(s_pt, at(h + 1, 1, i))
        if i is not None or h >= 1:
            act.wait_ge(s_pv, at(h, 1, i))
        nc.scalar.copy(probT, psum[:, 2].rearrange("p (k s) -> p k s", k=2)).then_inc(s_pT, 1)

    def a1_pv_pe(pe, h, i=None):
        pe.wait_ge(s_pT, at(h + 1, 1, i))
        if i is not None or h >= 1:
            pe.wait_ge(s_ya, at(h, 1, i))
        for t in range(TT):
            for kt in range(t + 1):
                ins = nc.tensor.matmul(psum[:, 3, t * P:(t + 1) * P], probT[:, kt, t * P:(t + 1) * P],
                                       proj[:, kt, bass.ds(at(3072 + h * HD, HD, i), HD)], start=(kt == 0), stop=(kt == t))
        ins.then_inc(s_pv, 1)

    def a1_y_dve(dve, h, i=None):
        dve.wait_ge(s_pv, at(h + 1, 1, i))
        for t in range(TT):
            ins = nc.vector.tensor_scalar(proj[:, t, bass.ds(at(1024 + h * HD, HD, i), HD)], psum[:, 3, t * P:(t + 1) * P],
                                          rden[:, 0, t:t + 1], None, ALU.mult)
        ins.then_inc(s_ya, 1)

    def a1_pe(pe):
        a1_turn_pe(pe, 0)
        a1_scores_pe(pe, 0)

        for h in range(HEADS):
            last, g = h == HEADS - 1, 16 + h // 2
            if not last:
                a1_turn_pe(pe, h + 1)
            ada_mult(pe, g, 2 * (h % 2))
            a1_pturn_pe(pe, h)
            ada_mult(pe, g, 2 * (h % 2) + 1)
            if h % 2 == 0 and h:
                ada_turn(pe, g - 1)
            if not last:
                a1_scores_pe(pe, h + 1)
            a1_pv_pe(pe, h)

    def a1_act(act):
        act.wait_ge(s_ms, 2)
        act.wait_ge(s_qc, 1)
        a1_stage_act(act, 0)
        a1_qkT_act(act, 0)
        a1_stage_act(act, 1)
        a1_exp_act(act, 0)

        for h in range(HEADS):
            left = HEADS - 1 - h
            if left > 0:
                a1_qkT_act(act, h + 1)
            if h % 2 == 0 and h:
                ada_row(act, 15 + h // 2)
            a1_pT_act(act, h)
            if h % 2 == 0 and h:
                ada_col(act, 15 + h // 2)
            if left > 1:
                a1_stage_act(act, h + 2)
            if left > 0:
                a1_exp_act(act, h + 1)

    def a1_dve(dve, ch):
        dve.wait_ge(s_dist, 32)
        a1_max_dve(dve, ch, 0)
        a1_prob_dve(dve, ch, 0)

        def step(h, i, last=False):
            if not last:
                a1_max_dve(dve, ch, h + 1, i)
            a1_y_dve(dve, h, i)
            if not last:
                a1_prob_dve(dve, ch, h + 1, i)
        step(0, None)
        with dve.Fori(1, HEADS - 1) as i:
            ch.enter(i, 1, 4)
            step(0, i)
            ch.leave(HEADS - 1)
        step(HEADS - 1, None, True)

    def a1_out_pe(pe):
        pe.wait_ge(s_ya, 8)
        for r in range(4):
            if r >= 2:
                pe.wait_ge(s_al, r - 1)
            for j in range(2):
                for t in range(TT):
                    ft = 2 * r + j
                    ins = nc.tensor.transpose(psum[:, 2 + r % 2, j * S + t * P:j * S + t * P + P],
                                              proj[:, t, 1024 + ft * P:1024 + (ft + 1) * P], ident[:])
            ins.then_inc(s_at, 1)

    def a1_out_act(act):
        for r in range(4):
            act.wait_ge(s_at, r + 1)
            nc.scalar.copy(hh[:, 8 + 2 * r:10 + 2 * r], psum[:, 2 + r % 2].rearrange("p (a b) -> p a b", a=2)
                           ).then_inc(s_ah, 1)

    def a1_out_dve(dve):
        for r in range(4):
            dve.wait_ge(s_ah, r + 1)
            nc.vector.tensor_tensor(hl[:, 8 + 2 * r:10 + 2 * r], psum[:, 2 + r % 2].rearrange("p (a b) -> p a b", a=2),
                                    hh[:, 8 + 2 * r:10 + 2 * r].bitcast(F32), ALU.subtract).then_inc(s_al, 1)

    sg = xacc[:].rearrange("p a (c n) -> p c a n", c=4)

    def glu_sp(sp):
        w = dram["ssm_w_glu"][0]
        for c in range(2):
            for j in range(4):
                if (c, j) == (1, 0):
                    sp.wait_ge(s_scan["dve"], 1)
                if (c, j) == (1, 2):
                    sp.wait_ge(s_y, 4)
                load(sp, U_GLU + 4 * c + j, w_rows(w, 2 * j, 2)[:, :, c * CW:(c + 1) * CW])

    def glu_pe(pe):
        pe.wait_ge(s_yl, 4)
        for c in range(2):
            for j in range(4):
                multiply(pe, U_GLU + 4 * c + j, lat(2 * c), 2 * j, 7)
        for c in range(2):
            pe.wait_ge(s_sg, c + 1)
            for r in range(2):
                n = 2 * c + r
                if n >= 2:
                    pe.wait_ge(s_gy, n - 1)
                for j in range(2):
                    for t in range(TT):
                        f = 2 * r + j
                        ins = nc.tensor.transpose(psum[:, 4 + n % 2, j * S + t * P:j * S + t * P + P],
                                                  sg[:, c, t, f * P:(f + 1) * P], ident[:])
                ins.then_inc(s_gt, 1)

    def glu_act(act):
        for n in range(8):
            high(act, U_GLU + n)
        for c in range(2):
            act.wait_ge(s_mm, U_GLU + 4 * c + 4)
            nc.scalar.activation(sg[:, c], psum[:, 2 * c:2 * c + 2], ACT.Sigmoid).then_inc(s_sg, 1)
        for n in range(4):
            act.wait_ge(s_gy, n + 1)
            nc.scalar.copy(hh[:, 2 * n:2 * n + 2], uT(2 * n, 2)).then_inc(s_gh, 1)

    def glu_dve(dve):
        for n in range(8):
            low(dve, U_GLU + n)
        for n in range(5):
            if n < 4:
                dve.wait_ge(s_gt, n + 1)
                v = uT(2 * n, 2)
                nc.vector.tensor_tensor(v, v, psum[:, 4 + n % 2].rearrange("p (a b) -> p a b", a=2),
                                        ALU.mult).then_inc(s_gy, 1)
            if n >= 1:
                k = slice(2 * n - 2, 2 * n)
                dve.wait_ge(s_gh, n)
                nc.vector.tensor_tensor(hl[:, k], uT(2 * n - 2, 2), hh[:, k].bitcast(F32), ALU.subtract).then_inc(s_gl, 1)

    ADA_AFTER = (0, 2, 3, 5, 6, 8, 9, 11)

    def pairs_sp(sp, u0, w, q0, steps, i0=0, c0=0, peel=False):
        def step(i):
            for j in range(2 * UPC):
                load(sp, u0 + j, w_rows(w, 2 * (j % UPC), 2)[:, :, bass.ds(at(c0 + (j // UPC) * CW, 2 * CW, i), CW)],
                     per=2 * UPC, i=i)
                if q0 is not None and j in ADA_AFTER:
                    a = ADA_AFTER.index(j)
                    ada_load(sp, q0 + a // 4, a % 4, 2, i)
        if peel:
            step(None)
        with sp.Fori(int(peel), steps) as i:
            step(i)

    def pairs_act(act, u0, steps, evac, beside=None):
        def step(i, first=False, beside=None):
            for j in range(2 * UPC):
                if evac and j % UPC == 3 and not (first and j == 3):
                    evac(act, j // UPC - 1, 2, i)
                high(act, u0 + j, per=2 * UPC, i=i)
                if beside:
                    beside(act, j)
        step(None, True)
        if beside:
            step(1)
            step(2, beside=beside)
        with act.Fori(3 if beside else 1, steps) as i:
            step(i)
        if evac:
            evac(act, 2 * steps - 1, 0, None)

    def pairs_dve(dve, u0, q0, steps, evac=None, ch=None, ch_per=0):
        def step(i, first=False):
            for j in range(2 * UPC):
                if evac and j % UPC == 3 and not (first and j == 3):
                    evac(dve, j // UPC - 1, 2, i)
                low(dve, u0 + j, per=2 * UPC, i=i)
                if q0 is not None and j in ADA_AFTER:
                    a = ADA_AFTER.index(j)
                    ada_sum(dve, q0 + a // 4, a % 4, 2, i)
            if q0 is not None:
                ada_store(dve, q0, 2, i)
        step(None, True)
        with dve.Fori(1, steps) as i:
            if ch:
                ch.enter(i, 1, ch_per)
            step(i)
            if ch:
                ch.leave(steps)
        if evac:
            evac(dve, 2 * steps - 1, 0, None)

    def pairs_pe(pe, u0, q0, steps, s_ev, b0=0, beside=None):
        def step(i, first=False, beside=None):
            for j in range(2 * UPC):
                c = j // UPC
                if j % UPC == 0 and not first:
                    pe.wait_ge(s_ev, at(c - 1, 2, i))
                multiply(pe, u0 + j, lat(b0 + 2 * c), 2 * (j % UPC), KT - 1, per=2 * UPC, i=i)
                if beside:
                    beside(pe, j)
                if j == 2 * UPC - 3 and q0 is not None:
                    ada_reduce(pe, q0, 2, i)
        step(None, True)
        if beside:
            step(1)
            step(2, beside=beside)
        with pe.Fori(3 if beside else 1, steps) as i:
            step(i)

    def in_evac(act, c, per, i):
        act.wait_ge(s_mm, at(U_IN + UPC * (c + 1), UPC * per, i))
        b = 2 * (c % 2)
        nc.scalar.copy(proj[:, :, bass.ds(at(c * CW, per * CW, i), CW)], psum[:, b:b + 2]).then_inc(s_inev, 1)

    s_oev, s_om = sem("mixed_added"), sem("mixed_gated")
    mixed_tmp = hB[:].rearrange("p r g t -> p (r g t)")[:, 0:2 * CW].rearrange("p (t n) -> p t n", t=TT)

    def gated(dve, ch, c, per, i, u0, dst, src, scale, s_ev, row, mixed_tmp, b0=0):
        dve.wait_ge(s_mm, at(u0 + UPC * (c + 1), UPC * per, i))
        b = b0 + 2 * (c % 2)
        cs = bass.ds(at(c * CW, per * CW, i), CW)
        ch(nc.vector.tensor_tensor(mixed_tmp, psum[:, b:b + 2], row[:, cs].unsqueeze(1).broadcast_to([P, TT, CW]), ALU.mult))
        ch.wait()
        nc.vector.scalar_tensor_tensor(out=dst[:, :, cs], in0=src[:, :, cs], scalar=scale, in1=mixed_tmp,
                                       op0=ALU.mult, op1=ALU.add).then_inc(s_ev, 1)

    f = ExitStack()
    sgb = sb(f, "sgb", [P, TT, CW])
    hid = sb(f, "hid", [P, TT, CW])
    hidh = sb(f, "hidh", [P, 4, S], F32R)
    hidl = sb(f, "hidl", [P, 4, S], F32R)
    row2 = sb(f, "row2", [P, D])
    ub = sb(f, "ub", [P, TT, CW])
    dfts = sb(f, "dfts", [P, 4, CW], F32)
    dft = sb(f, "dft", [P, TT, 2 * S])
    dft2 = sb(f, "dft2", [P, TT, S])
    lng = sb(f, "lng", [P, D])
    lnb = sb(f, "lnb", [P, D])
    f.close()
    s_zero, s_dft = sem("xacc_zero"), sem("dft_landed")
    ADA24 = (0, 2, 5, 7, 9, 11, 13, 15)
    BANK = (0, 4, 0, 4)

    class Hidden:
        def __init__(self, name, u0, wg, wu, wd, gcol, ucol, steps, fourier):
            self.u0, self.wg, self.wu, self.wd, self.gcol, self.ucol = u0, wg, wu, wd, gcol, ucol
            self.steps, self.fourier = steps, fourier
            self.sg, self.a, self.t, self.h, self.l, self.dv, self.ub, self.f1, self.v, self.f2 = (
                sem(name + n) for n in ("_silu", "_product", "_turned", "_high", "_low", "_added", "_up", "_dft1",
                                        "_dft1_stored", "_dft2"))

        def unit(self, c, j):
            if isinstance(c, int):
                return {"u": self.u0 + (j if c == 0 else 24 * c - 8 + j)}
            return {"u": self.u0 - 8 + j, "per": 24, "i": c}

        def used(self, c, j):
            return (self.u0 + j + 1) if isinstance(c, int) and c == 0 else c * 24 + (self.u0 - 8 + j + 1)

    def hidden_sp(sp, H, c, q=None, perq=0, lo=0):
        n = 24 if not isinstance(c, int) or c > 0 else 16
        before = (c - 1) * CW if isinstance(c, int) else sp.snap((c - 1) * CW)
        for j in range(n):
            if j < 16:
                w, col = ((H.wg, H.gcol), (H.wu, H.ucol))[j // 8]
                src = w_rows(w, 2 * (j % 8), 2)[:, :, bass.ds(before + (CW + col), CW)]
            else:
                jj = j - 16
                rows = H.wd.rearrange("(k p) n -> k p n", p=P)[bass.ds(4 * (c - 1) + 2 * (jj % 2), 2)]
                src = rows.rearrange("k p n -> p k n")[:, :, (jj // 2) * CW:(jj // 2 + 1) * CW]
            load(sp, src=src, **H.unit(c, j))
            pos = ADA24 if n == 24 else ADA_AFTER
            if q is not None and j in pos:
                a = pos.index(j)
                ada_load(sp, q + a // 4, a % 4, perq, None if isinstance(c, int) else c - lo)

    def hidden_end_sp(sp, H):
        c = H.steps
        for jj in range(8):
            src = w_rows(H.wd, 4 * (c - 1) + 2 * (jj % 2), 2)[:, :, (jj // 2) * CW:(jj // 2 + 1) * CW]
            load(sp, H.u0 + 24 * c - 8 + jj, src)

    def hidden_turn_act(act, H, c, r):
        act.wait_ge(H.t, c * 2 + (r - 1))
        if r == 0:
            act.wait_ge(s_mm, H.used(c, -1))
        nc.scalar.copy(hidh[:, 2 * r:2 * r + 2], psum[:, 6].rearrange("p (a b) -> p a b", a=2)).then_inc(H.h, 1)

    def hidden_turn_dve(dve, H, c, r):
        dve.wait_ge(H.h, c * 2 + (r - 1))
        if r == 0:
            dve.wait_ge(s_mm, H.used(c, -1))
        nc.vector.tensor_tensor(hidl[:, 2 * r:2 * r + 2], psum[:, 6].rearrange("p (a b) -> p a b", a=2),
                                hidh[:, 2 * r:2 * r + 2].bitcast(F32), ALU.subtract).then_inc(H.l, 1)

    def hidden_silu_act(act, H, c):
        act.wait_ge(s_mm, H.used(c, 7))
        if not isinstance(c, int) or c >= 1:
            act.wait_ge(H.a, c * 1)
        nc.scalar.activation(sgb[:], psum[:, 0:2], ACT.Silu).then_inc(H.sg, 1)

    def hidden_store_act(act, H, c, g):
        act.wait_ge(H.f1, c * 2 + (g + 1))
        if g == 0 and (not isinstance(c, int) or c >= 1):
            act.wait_ge(H.f2, c * 1)
        nc.scalar.copy(dfts[:, 2 * g:2 * g + 2], psum[:, 2:4]).then_inc(H.v, 1)

    TURN_AT = {False: ((1, 6), (9, 14)), True: ((9, 13), (12, 16))}

    def hidden_act(act, H, c):
        first = isinstance(c, int) and c == 0
        for j in range(16 if first else 24):
            if not first:
                for r in range(2):
                    if j == TURN_AT[H.fourier][r][1]:
                        hidden_turn_act(act, H, c, r)
                if H.fourier and j == 1:
                    hidden_store_act(act, H, c - 1, 1)
            if j == 11:
                hidden_silu_act(act, H, c)
            if H.fourier and j == 23:
                hidden_store_act(act, H, c, 0)
            high(act, **H.unit(c, j))
        if H.fourier and first:
            hidden_store_act(act, H, c, 0)

    def hidden_end_act(act, H):
        c = H.steps
        if H.fourier:
            hidden_store_act(act, H, c - 1, 1)
        for r in range(2):
            hidden_turn_act(act, H, c, r)
        for jj in range(8):
            high(act, H.u0 + 24 * c - 8 + jj)

    def hidden_up_dve(dve, H, c):
        dve.wait_ge(s_mm, H.used(c, 15))
        later = not isinstance(c, int) or c >= 1
        if H.fourier:
            if later:
                dve.wait_ge(H.f1, c * 2)
            nc.vector.tensor_copy(ub[:], psum[:, 2:4]).then_inc(H.ub, 1)
        else:
            dve.wait_ge(H.sg, c + 1)
            if later:
                dve.wait_ge(H.t, c * 2)
            nc.vector.tensor_tensor(hid[:], sgb[:], psum[:, 2:4], ALU.mult).then_inc(H.a, 1)

    def hidden_product_dve(dve, H, c):
        dve.wait_ge(H.f2, c + 1)
        dve.wait_ge(H.sg, c + 1)
        if not isinstance(c, int) or c >= 1:
            dve.wait_ge(H.t, c * 2)
        nc.vector.tensor_tensor(hid[:], sgb[:], psum[:, 2:4], ALU.mult).then_inc(H.a, 1)

    def hidden_add_dve(dve, H, c, n):
        dve.wait_ge(s_mm, H.used(c, 17 + 2 * n))
        o = xacc[:, :, n * CW:(n + 1) * CW]
        nc.vector.tensor_tensor(o, o, psum[:, BANK[n]:BANK[n] + 2], ALU.add).then_inc(H.dv, 1)

    def hidden_dve(dve, H, c, q=None, perq=0, lo=0):
        first, second = (isinstance(c, int) and c == v for v in (0, 1))
        n = 16 if first else 24
        for j in range(n):
            if not first:
                for r in range(2):
                    if j == TURN_AT[H.fourier][r][1]:
                        hidden_turn_dve(dve, H, c, r)
                if second and j == 3 and not H.fourier:
                    hidden_up_dve(dve, H, 0)
                if not second and j in (1, 3):
                    hidden_add_dve(dve, H, c - 1, 2 + j // 2)
                if H.fourier and j == 7:
                    hidden_product_dve(dve, H, c - 1)
                if j == 19:
                    hidden_up_dve(dve, H, c)
                if second and j == 21:
                    dve.wait_ge(s_zero, 2 if H.fourier else 1)
                if j in (21, 23):
                    hidden_add_dve(dve, H, c, (j - 21) // 2)
            low(dve, **H.unit(c, j))
            pos = ADA24 if n == 24 else ADA_AFTER
            if q is not None and j in pos:
                a = pos.index(j)
                ada_sum(dve, q + a // 4, a % 4, perq, None if isinstance(c, int) else c - lo)
        if H.fourier and first:
            hidden_up_dve(dve, H, 0)
        if q is not None:
            ada_store(dve, q, perq, None if isinstance(c, int) else c - lo)

    def hidden_end_dve(dve, H):
        c = H.steps
        for n in (2, 3):
            hidden_add_dve(dve, H, c - 1, n)
        if H.fourier:
            hidden_product_dve(dve, H, c - 1)
        for r in range(2):
            hidden_turn_dve(dve, H, c, r)
        for jj in range(8):
            low(dve, H.u0 + 24 * c - 8 + jj)
            if jj in (4, 6):
                dve.wait_ge(s_mm, H.u0 + 24 * c - 8 + jj - 2)
                hidden_tail_add(dve, H, (jj - 4) // 2)
        for n in (2, 3):
            dve.wait_ge(s_mm, H.u0 + 24 * c - 8 + 2 * n + 2)
            hidden_tail_add(dve, H, n)

    def hidden_tail_add(dve, H, n):
        o = xacc[:, :, n * CW:(n + 1) * CW]
        nc.vector.tensor_tensor(o, o, psum[:, BANK[n]:BANK[n] + 2], ALU.add).then_inc(H.dv, 1)

    def hidden_turn_pe(pe, H, c, r):
        if r == 0:
            pe.wait_ge(H.a, c * 1)
            if not isinstance(c, int) or c >= 2:
                pe.wait_ge(H.l, c * 2 - 2)
        else:
            pe.wait_ge(H.l, c * 2 - 1)
        for j in range(2):
            for t in range(TT):
                k = 2 * r + j
                ins = nc.tensor.transpose(psum[:, 6, j * S + t * P:j * S + t * P + P], hid[:, t, k * P:(k + 1) * P],
                                          ident[:])
        ins.then_inc(H.t, 1)

    def hidden_dft1_pe(pe, H, c, g):
        if g == 0:
            pe.wait_ge(H.ub, c + 1)
            if isinstance(c, int) and c == 0:
                pe.wait_ge(s_dft, 32)
        else:
            pe.wait_ge(H.v, c * 2 + 1)
        for half in range(2):
            for t in range(TT):
                ins = nc.tensor.matmul(psum[:, 2 + half], ub[:, t, g * S + half * P:g * S + half * P + P], dft[:, t],
                                       start=(t == 0), stop=(t == TT - 1))
        ins.then_inc(H.f1, 1)

    def hidden_dft2_pe(pe, H, c):
        pe.wait_ge(H.v, c * 2 + 2)
        for g in range(2):
            for t in range(TT):
                for half in range(2):
                    a = dfts[:, 2 * g + half]
                    o = psum[:, 2 + t, g * S:(g + 1) * S]
                    nc.tensor.matmul(o, a[:, t * P:t * P + P], dft[:, half, 0:S], start=(half == 0), stop=False)
                    ins = nc.tensor.matmul(o, a[:, S + t * P:S + t * P + P], dft2[:, half], start=False, stop=(half == 1))
        ins.then_inc(H.f2, 1)

    def hidden_down_pe(pe, H, c, jj, unit):
        n = jj // 2
        if jj == 0:
            pe.wait_ge(H.l, c * 2)
            if isinstance(c, int) and c == H.steps:
                pe.wait_ge(H.dv, 4 * c - 5)
            else:
                pe.wait_ge(H.sg, c + 1)
        if jj == 2 and (not isinstance(c, int) or c >= 2):
            pe.wait_ge(H.dv, c * 4 - 4)
        if jj in (4, 6):
            pe.wait_ge(H.dv, c * 4 + (n - 5))
        multiply(pe, tiles=[(hidh, hidl, t, BANK[n] + t) for t in range(TT)], kt=2 * (jj % 2), last_kt=3, **unit)

    def hidden_pe(pe, H, c, q=None, perq=0, lo=0):
        first = isinstance(c, int) and c == 0
        later = not isinstance(c, int) or c >= 2
        for j in range(16 if first else 24):
            if j == 0 and not first:
                pe.wait_ge(H.sg, c * 1)
                if later:
                    pe.wait_ge(H.dv, c * 4 - 5)
            if j == 8 and not first:
                pe.wait_ge(H.a, c * 1)
            if j < 16:
                multiply(pe, tiles=lat(2 * (j // 8)), kt=2 * (j % 8), last_kt=KT - 1, **H.unit(c, j))
            else:
                hidden_down_pe(pe, H, c, j - 16, H.unit(c, j))
            if not first:
                for r in range(2):
                    if j == TURN_AT[H.fourier][r][0]:
                        hidden_turn_pe(pe, H, c, r)
                if H.fourier and j == 3:
                    hidden_dft2_pe(pe, H, c - 1)
                if H.fourier and j in (19, 21):
                    hidden_dft1_pe(pe, H, c, (j - 19) // 2)
            if q is not None and j == (13 if first else 19):
                ada_reduce(pe, q, perq, None if isinstance(c, int) else c - lo)
        if H.fourier and first:
            hidden_dft1_pe(pe, H, c, 0)
            hidden_dft1_pe(pe, H, c, 1)

    def hidden_end_pe(pe, H):
        c = H.steps
        if H.fourier:
            hidden_dft2_pe(pe, H, c - 1)
        for r in range(2):
            hidden_turn_pe(pe, H, c, r)
        for jj in range(8):
            hidden_down_pe(pe, H, c, jj, {"u": H.u0 + 24 * c - 8 + jj})

    ffn = Hidden("ffn", U_FFN, dram["w_ffn_gate"][0], dram["w_ffn_up"][0], dram["w_ffn_down"][0], 0, 0, FFN_CH, False)
    fou = Hidden("fourier", U_FOU, dram["w_in_fourier_2"][0], dram["w_in_fourier_2"][0], dram["w_out_fourier_2"][0],
                 4096, 0, FCH, True)

    def ffn_steps(eng, step):
        step(0, None, 0, 0)
        step(1, 20, 0, 0)
        step(2, 22, 0, 0)
        with eng.Fori(3, 5) as c:
            step(c, 32, 2, 3)
        with eng.Fori(5, FFN_CH) as c:
            step(c, 36, 2, 5)

    def fourier_steps(eng, step):
        step(0, None, 0, 0)
        step(1, None, 0, 0)
        with eng.Fori(2, FCH) as c:
            step(c, None, 0, 2)

    g1 = ExitStack()
    ch_h = sb(g1, "ctxh", [P, KT, S], F32R)
    ch_l = sb(g1, "ctxl", [P, KT, S], F32R)
    g1.close()
    g2 = ExitStack()
    sgate = sb(g2, "sgate", [P, TT, D])
    qb = sb(g2, "qb", [P, TT, 1024])
    cq = sb(g2, "cq", [P, TT, QL])
    g3 = sb(g2, "rope_rows", [P, 512])
    ckv = sb(g2, "ckv", [P, 4, KVL])
    kvb = sb(g2, "kvb", [P, 4, 512])
    kpe = sb(g2, "kpe", [P, 4, ROPE])
    kpeT = sb(g2, "kpeT", [P, 512])
    kbT = sb(g2, "kbT", [P, 2, 512])
    rope_b = sb(g2, "rope_b_t", [P, TT, 256])
    rope_a = sb(g2, "rope_a_t", [P, TT, 128])
    wqk = sb(g2, "wqk", [P, 2, HD])
    st6 = sb(g2, "st6", [P, 8, 6])
    mv6 = sb(g2, "mv6", [P, 6, 2])
    ms6 = sb(g2, "ms6", [P, 30])
    r6 = sb(g2, "r6", [P, 30])
    g2.close()
    xaf = xacc[:].rearrange("p a b -> p (a b)")
    qp = xaf[:, 0:768].rearrange("p (t n) -> p t n", t=TT)
    kvp = xaf[:, 768:2816].rearrange("p (t n) -> p t n", t=4)
    kT2 = xaf[:, 2816:3328]
    qT2 = xaf[:, 3328:3840].rearrange("p (h s) -> p h s", h=2)
    prob2 = arawf[:, 0:1024].rearrange("p (t s) -> p t s", t=TT)
    pT2 = arawf[:, 1024:2048].rearrange("p (k s) -> p k s", k=4)
    stq = arawf[:, 2048:2560].rearrange("p (h t e) -> p h t e", h=2, t=TT)
    rtmp = arawf[:, 2560:3584]
    sq = xaf
    yA = ckv[:].rearrange("p a b -> p (a b)").rearrange("p (t n) -> p t n", t=TT)
    row3 = sgate[:, 0]
    tmp3 = sgate[:, 1, 0:2 * CW].rearrange("p (t n) -> p t n", t=TT)
    gain3 = kvb[:].rearrange("p a b -> p (a b)")
    bias3 = ckv[:].rearrange("p a b -> p (a b)")
    cqTh, cqTl = hh[:, 0:6], hl[:, 0:6]
    ckvTh, ckvTl = (v[:, 6:14].rearrange("p (k a) s -> p k (a s)", a=2) for v in (hh, hl))

    s_ctx, s_ropes, s_e, s_ge = sem("ctx_landed"), sem("rope_landed"), sem("z_stored"), sem("silu_gate")
    s_m2, s_r2, s_nz, s_qbr = sem("z_squares"), sem("z_rstd"), sem("z_normed"), sem("b_ready")
    s_zt, s_zh, s_zl = sem("z_turned"), sem("z_high"), sem("z_low")
    s_kt, s_ke = sem("k_turned"), sem("k_stored")
    s_pq, s_qr, s_sq = sem("pair_stored"), sem("pair_rotated"), sem("q_staged")
    s_ta, s_te, s_s2, s_mx2, s_ex2, s_rc2, s_tp2, s_pe2, s_pf2, s_pv2, s_y2 = (sem("a2_" + n) for n in (
        "turned", "stored", "scores", "max", "exp", "recip", "p_turned", "pT_act", "pT_dve", "pv", "y"))
    s_yt, s_yh2, s_yl2 = sem("y_turned"), sem("y2_high"), sem("y2_low")
    s_aev, s_rows = sem("attn_added"), sem("rows_landed")

    AIN = ((768, 512, True, 0, lambda: ckv[:]), (1280, 64, True, 4, lambda: kpe[:]), (2368, 512, True, 0, lambda: kvb[:]),
           (0, 512, False, 4, lambda: cq[:, :, 0:512]), (512, 256, False, 0, lambda: cq[:, :, 512:768]),
           (1344, 512, False, 2, lambda: qb[:, :, 0:512]), (1856, 512, False, 4, lambda: qb[:, :, 512:1024]))
    NEED = (0, 0, 1, 2, 3, 3, 4)

    def ain_sp(sp):
        w = dram["w_in_attn_2"][0]
        for n, (c, wd, both, b, d) in enumerate(AIN):
            for j in range(UPC):
                load(sp, U_AIN + UPC * n + j, w_rows(w, 2 * j, 2)[:, :, c:c + wd], wd)

    def ain_act(act):
        def store(n):
            c, wd, both, b, d = AIN[n]
            act.wait_ge(s_mm, U_AIN + UPC * (n + 1))
            nc.scalar.copy(d(), psum[:, b:b + (4 if both else 2), 0:wd]).then_inc(s_e, 1)
        for n, (c, wd, both, b, d) in enumerate(AIN):
            for j in range(UPC):
                if j == 3 and n:
                    store(n - 1)
                high(act, U_AIN + UPC * n + j, wd)
        store(len(AIN) - 1)

    def ain_dve(dve):
        for n, (c, wd, both, b, d) in enumerate(AIN):
            for j in range(UPC):
                low(dve, U_AIN + UPC * n + j, wd)

    def ain_pe(pe):
        for n, (c, wd, both, b, d) in enumerate(AIN):
            if NEED[n]:
                pe.wait_ge(s_e, NEED[n])
            tiles = lat(b) + ([(ch_h, ch_l, t, b + 2 + t) for t in range(TT)] if both else [])
            for j in range(UPC):
                multiply(pe, U_AIN + UPC * n + j, tiles, 2 * j, KT - 1, wd)
        pe.wait_ge(s_e, 7)

    def gate_evac(act, c, per, i):
        act.wait_ge(s_mm, at(U_AIN + 56 + UPC * (c + 1), UPC * per, i))
        b = 2 * (c % 2)
        nc.scalar.activation(sgate[:, :, bass.ds(at(c * CW, per * CW, i), CW)], psum[:, b:b + 2], ACT.Silu).then_inc(s_ge, 1)

    def z_dve(dve, ch):
        V = nc.vector
        dve.wait_ge(s_e, 7)
        dve.wait_ge(s_ropes, 48)
        for t in range(TT):
            for c in range(2):
                ch(V.bn_stats(st6[:, 2 * t + c], cq[:, t, 384 * c:384 * c + 384]))
        for t in range(4):
            ch(V.bn_stats(st6[:, 4 + t], ckv[:, t]))
        ch.wait()
        for t in range(TT):
            ch(V.bn_aggr(mv6[:, t], st6[:, 2 * t:2 * t + 2].rearrange("p c s -> p (c s)")))
        for t in range(4):
            ch(V.bn_aggr(mv6[:, 2 + t], st6[:, 4 + t]))
        ch.wait()
        ch(V.tensor_tensor(ms6[:, 0:6].unsqueeze(2), mv6[:, :, 0:1], mv6[:, :, 0:1], ALU.mult))
        qsq = sq[:, 0:2048].rearrange("p (t n) -> p t n", t=TT)
        ksq = sq[:, 2048:3072].rearrange("p (t n) -> p t n", t=4)
        ch(V.tensor_tensor(qsq, qb[:], qb[:], ALU.mult))
        ch(V.tensor_tensor(ksq, kvb[:, :, 0:256], kvb[:, :, 0:256], ALU.mult))
        ch.wait()
        ch(V.tensor_tensor(ms6[:, 0:6].unsqueeze(2), ms6[:, 0:6].unsqueeze(2), mv6[:, :, 1:2], ALU.add))
        ch(V.tensor_reduce(ms6[:, 6:22], sq[:, 0:2048].rearrange("p (h e) -> p h e", e=HD), AX, ALU.add))
        ch(V.tensor_reduce(ms6[:, 22:30], sq[:, 2048:3072].rearrange("p (h e) -> p h e", e=HD), AX, ALU.add))
        ch.wait()
        ch(V.tensor_scalar(ms6[:, 0:6], ms6[:, 0:6], RMS_EPS, None, ALU.add))
        V.tensor_scalar(ms6[:, 6:30], ms6[:, 6:30], 1.0 / HD, RMS_EPS, ALU.mult, ALU.add).then_inc(s_m2, 1)
        dve.wait_ge(s_r2, 1)
        for t in range(TT):
            ch(V.tensor_scalar(cq[:, t], cq[:, t], r6[:, t:t + 1], None, ALU.mult))
        for t in range(4):
            ins = V.tensor_scalar(ckv[:, t], ckv[:, t], r6[:, 2 + t:3 + t], None, ALU.mult)
        ins.then_inc(s_nz, 1)
        for t in range(TT):
            v = qb[:, t].rearrange("p (h e) -> p h e", h=8)
            ch(V.tensor_tensor(v, v, r6[:, 6 + 8 * t:14 + 8 * t].unsqueeze(2).broadcast_to([P, 8, HD]), ALU.mult))
        for t in range(4):
            v = kvb[:, t, 0:256].rearrange("p (h e) -> p h e", h=2)
            ch(V.tensor_tensor(v, v, r6[:, 22 + 2 * t:24 + 2 * t].unsqueeze(2).broadcast_to([P, 2, HD]), ALU.mult))
        ch.wait()
        for t in range(TT):
            v = qb[:, t].rearrange("p (h e) -> p h e", h=8)
            ch(V.tensor_tensor(v, v, wqk[:, 0:1].broadcast_to([P, 8, HD]), ALU.mult))
        for t in range(4):
            v = kvb[:, t, 0:256].rearrange("p (h e) -> p h e", h=2)
            ch(V.tensor_tensor(v, v, wqk[:, 1:2].broadcast_to([P, 2, HD]), ALU.mult))
        ch.wait()
        for t in range(TT):
            rope(ch, kpe[:, t:t + 1], 1, 64, rope_a[:, t], sq)
            rope(ch, kvb[:, t, 0:256].rearrange("p (h e) -> p h e", h=2), 2, 128, rope_b[:, t], sq)
            rope(ch, qb[:, t].rearrange("p (h e) -> p h e", h=8), 8, 128, rope_b[:, t], sq)
        V.tensor_copy(st6[:, 0, 0:1], st6[:, 0, 1:2]).then_inc(s_qbr, 1)

    def rope(ch, v, heads, n, table, tmp):
        V = nc.vector
        t = tmp[:, 0:heads * n].rearrange("p (h e) -> p h e", h=heads)
        cs = table[:, 0:n].unsqueeze(1).broadcast_to([P, heads, n])
        sn = table[:, n:2 * n]
        for a in range(2):
            ch(V.tensor_tensor(t[:, :, a::2], v[:, :, 1 - a::2], sn[:, a::2].unsqueeze(1).broadcast_to([P, heads, n // 2]),
                               ALU.mult))
        ch.wait()
        ch(V.tensor_tensor(v, v, cs, ALU.mult))
        ch.wait()
        ch(V.tensor_tensor(v, v, t, ALU.add))
        ch.wait()

    def z_pool(pool):
        pool.wait_ge(s_m2, 1)
        nc.gpsimd.tensor_tensor(r6[:], ms6[:], mhalf[:, 0:30], ALU.pow).then_inc(s_r2, 1)

    def z_turn_pe(pe):
        pe.wait_ge(s_nz, 1)
        pe.wait_ge(s_ge, 4)
        for r in range(7):
            if r >= 2:
                pe.wait_ge(s_zl, r - 1)
            for j in range(4):
                if r < 3:
                    src = cq[:, j % 2, (2 * r + j // 2) * P:(2 * r + j // 2 + 1) * P]
                else:
                    src = ckv[:, j, (r - 3) * P:(r - 2) * P]
                ins = nc.tensor.transpose(psum[:, 4 + r % 2, j * P:(j + 1) * P], src, ident[:])
            ins.then_inc(s_zt, 1)
        pe.wait_ge(s_qbr, 1)
        for r in range(3):
            for j in range(4):
                if r == 0:
                    ins = nc.tensor.transpose(psum[0:64, 6, j * P:(j + 1) * P], kpe[:, j], ident[:])
                else:
                    ins = nc.tensor.transpose(psum[:, 1 + r, j * P:(j + 1) * P], kvb[:, j, (r - 1) * HD:r * HD], ident[:])
            ins.then_inc(s_kt, 1)

    def z_turn_act(act):
        act.wait_ge(s_mm, U_PAIR)
        for r in range(7):
            act.wait_ge(s_zt, r + 1)
            if r < 3:
                for j in range(2):
                    c = COLS["ql"].start + 2 * r + j
                    ins = nc.scalar.activation(cqTh[:, 2 * r + j], psum[:, 4 + r % 2, j * S:(j + 1) * S], ACT.Copy,
                                               scale=cols[:, c:c + 1])
            else:
                c = COLS["kvl"].start + r - 3
                ins = nc.scalar.activation(ckvTh[:, r - 3], psum[:, 4 + r % 2], ACT.Copy, scale=cols[:, c:c + 1])
            ins.then_inc(s_zh, 1)
        for r in range(3):
            act.wait_ge(s_kt, r + 1)
            if r == 0:
                ins = nc.scalar.copy(kpeT[0:64], psum[0:64, 6])
            else:
                ins = nc.scalar.copy(kbT[:, r - 1], psum[:, 1 + r])
            ins.then_inc(s_ke, 1)

    def z_turn_dve(dve):
        for r in range(7):
            dve.wait_ge(s_zh, r + 1)
            for j in range(2 if r < 3 else 1):
                if r < 3:
                    c, i0, o, h = (COLS["ql"].start + 2 * r + j, psum[:, 4 + r % 2, j * S:(j + 1) * S],
                                   cqTl[:, 2 * r + j], cqTh[:, 2 * r + j])
                else:
                    c, i0, o, h = COLS["kvl"].start + r - 3, psum[:, 4 + r % 2], ckvTl[:, r - 3], ckvTh[:, r - 3]
                ins = nc.vector.scalar_tensor_tensor(out=o, in0=i0, scalar=cols[:, c:c + 1], in1=h.bitcast(F32),
                                                     op0=ALU.mult, op1=ALU.subtract)
            ins.then_inc(s_zl, 1)

    PU = tuple((1, 384) for _ in range(6)) + ((2, 512), (2, 512))

    def pair_sp(sp, i):
        wq, wk = dram["wq_b_2"][0], dram["wkv_b_2"][0]
        for j, (kn, w) in enumerate(PU):
            if j < 6:
                src = w_rows(wq, j, 1)[:, :, bass.ds(at(0, 384, i), 384)]
            else:
                src = w_rows(wk, 2 * (j - 6), 2)[:, :, bass.ds(at(0, 512, i), 512)]
            load(sp, U_PAIR + j, src, w, per=8, i=i)

    def pair_act(act, i):
        for j, (kn, w) in enumerate(PU):
            high(act, U_PAIR + j, w, kn, per=8, i=i)
        act.wait_ge(s_mm, at(U_PAIR + 8, 8, i))
        if i is not None:
            act.wait_ge(s_ta, at(0, 4, i))
            act.wait_ge(s_pv2, at(0, 4, i))
        else:
            act.wait_ge(s_qbr, 1)
        nc.scalar.copy(qp, psum[:, 0:2, 0:384])
        nc.scalar.copy(kvp, psum[:, 2:6]).then_inc(s_pq, 1)
        nc.scalar.copy(stq[:, 0], qb[:, :, bass.ds(at(0, HD, i), HD)])
        nc.scalar.copy(stq[:, 1], qb[:, :, bass.ds(at(512, HD, i), HD)]).then_inc(s_sq, 1)

        def te(k):
            act.wait_ge(s_ta, at(k + 1, 4, i))
            if i is not None or k:
                act.wait_ge(s_s2, at(k, 4, i))
            ins = nc.scalar.copy(qT2[:, 0], psum[:, 6, 0:S])
            if k < 2:
                nc.scalar.copy(qT2[0:64, 1], psum[0:64, 6, S:2 * S])
                ins = nc.scalar.copy(kT2, psum[:, 7])
            ins.then_inc(s_te, 1)

        def ex(k):
            act.wait_ge(s_mx2, at(k + 1, 4, i))
            if i is not None or k:
                act.wait_ge(s_tp2, at(k, 4, i))
                act.wait_ge(s_rc2, at(k, 4, i))
            sc = A_SCALE if k < 2 else B_SCALE
            for t in range(TT):
                ins = nc.scalar.activation(prob2[:, t], psum[:, t], ACT.Exp, bias=neg[:, t:t + 1], scale=sc,
                                           accum_out=den[:, t:t + 1])
            ins.then_inc(s_ex2, 1)

        def pt(k):
            act.wait_ge(s_tp2, at(k + 1, 4, i))
            if i is not None or k:
                act.wait_ge(s_pv2, at(k, 4, i))
            nc.scalar.copy(pT2[:, 0:2], psum[:, 2].rearrange("p (k s) -> p k s", k=2)).then_inc(s_pe2, 1)
        te(0)
        ex(0)
        for k in range(1, 4):
            te(k)
            pt(k - 1)
            ex(k)
        pt(3)

    def pair_dve(dve, ch, i):
        for j, (kn, w) in enumerate(PU):
            low(dve, U_PAIR + j, w, kn, per=8, i=i)
        dve.wait_ge(s_pq, at(1, 1, i))
        for t in range(TT):
            rope(ch, qp[:, t].rearrange("p (h e) -> p h e", h=2)[:, :, 128:192], 2, 64, rope_a[:, t], rtmp)
        nc.vector.tensor_copy(st6[:, 0, 0:1], st6[:, 0, 1:2]).then_inc(s_qr, 1)

        def mx(k):
            dve.wait_ge(s_s2, at(k + 1, 4, i))
            if i is not None or k:
                dve.wait_ge(s_ex2, at(k, 4, i))
            ch(nc.vector.tensor_reduce(neg[:], psum[:, 0:2], AX, ALU.max))
            ch.wait()
            nc.vector.tensor_scalar(neg[:], neg[:], -(A_SCALE if k < 2 else B_SCALE), None, ALU.mult).then_inc(s_mx2, 1)

        def rc(k):
            dve.wait_ge(s_ex2, at(k + 1, 4, i))
            nc.vector.reciprocal(rden[:, k % 2], den[:]).then_inc(s_rc2, 1)

        def pt(k):
            dve.wait_ge(s_tp2, at(k + 1, 4, i))
            if i is not None or k:
                dve.wait_ge(s_pv2, at(k, 4, i))
            nc.vector.tensor_copy(pT2[:, 2:4], psum[:, 3].rearrange("p (k s) -> p k s", k=2)).then_inc(s_pf2, 1)

        def y(k):
            dve.wait_ge(s_pv2, at(k + 1, 4, i))
            dve.wait_ge(s_rc2, at(k + 1, 4, i))
            if i is None and k == 0:
                dve.wait_ge(s_ge, 4)
            if k < 2:
                o, gc = yA[:, :, bass.ds(at(k * HD, 2 * HD, i), HD)], at(k * HD, 2 * HD, i)
            else:
                o, gc = qb[:, :, bass.ds(at((k - 2) * 512, HD, i), HD)], at(1024 + (k - 2) * 512, HD, i)
            for t in range(TT):
                ins = nc.vector.scalar_tensor_tensor(out=o[:, t], in0=psum[:, 4, t * P:(t + 1) * P],
                                                     scalar=rden[:, k % 2, t:t + 1],
                                                     in1=sgate[:, t, bass.ds(gc, HD)], op0=ALU.mult, op1=ALU.mult)
            ins.then_inc(s_y2, 1)
        mx(0)
        rc(0)
        for k in range(1, 4):
            pt(k - 1)
            mx(k)
            y(k - 1)
            rc(k)
        pt(3)
        y(3)

    def pair_pe(pe, i):
        if i is not None:
            pe.wait_ge(s_y2, at(0, 4, i))
            pe.wait_ge(s_pe2, at(0, 4, i))
            pe.wait_ge(s_pf2, at(0, 4, i))
        else:
            pe.wait_ge(s_zl, 7)
            pe.wait_ge(s_ke, 3)
        for j, (kn, w) in enumerate(PU):
            if j < 6:
                tiles, kt, last = [(cqTh, cqTl, t, t) for t in range(TT)], j, 5
            else:
                tiles, kt, last = [(ckvTh, ckvTl, t, 2 + t) for t in range(4)], 2 * (j - 6), 3
            multiply(pe, U_PAIR + j, tiles, kt, last, w, kn, per=8, i=i)

        def turn(k):
            if k == 0:
                pe.wait_ge(s_qr, at(1, 1, i))
            if k == 2:
                pe.wait_ge(s_sq, at(1, 1, i))
            if i is not None or k:
                pe.wait_ge(s_te, at(k, 4, i))
            for t in range(TT):
                if k < 2:
                    nc.tensor.transpose(psum[:, 6, t * P:(t + 1) * P], qp[:, t, 192 * k:192 * k + 128], ident[:])
                    ins = nc.tensor.transpose(psum[0:64, 6, S + t * P:S + (t + 1) * P], qp[:, t, 192 * k + 128:192 * k + 192],
                                              ident[:])
                else:
                    ins = nc.tensor.transpose(psum[:, 6, t * P:(t + 1) * P], stq[:, k - 2, t], ident[:])
            if k < 2:
                for t in range(4):
                    ins = nc.tensor.transpose(psum[:, 7, t * P:(t + 1) * P], kvp[:, t, 256 * k:256 * k + 128], ident[:])
            ins.then_inc(s_ta, 1)

        def scores(k):
            pe.wait_ge(s_te, at(k + 1, 4, i))
            if i is not None or k:
                pe.wait_ge(s_ex2, at(k, 4, i))
            for t in range(TT):
                a = slice(t * P, t * P + P)
                if k < 2:
                    nc.tensor.matmul(psum[:, t], qT2[:, 0, a], kT2, start=True, stop=False)
                    ins = nc.tensor.matmul(psum[:, t], qT2[0:64, 1, a], kpeT[0:64], start=False, stop=True)
                else:
                    ins = nc.tensor.matmul(psum[:, t], qT2[:, 0, a], kbT[:, k - 2], start=True, stop=True)
            ins.then_inc(s_s2, 1)

        def turn_p(k):
            pe.wait_ge(s_ex2, at(k + 1, 4, i))
            if i is not None or k:
                pe.wait_ge(s_pe2, at(k, 4, i))
                pe.wait_ge(s_pf2, at(k, 4, i))
            for kt in range(4):
                for t in range(TT):
                    o = (kt % 2) * S + t * P
                    ins = nc.tensor.transpose(psum[:, 2 + kt // 2, o:o + P], prob2[:, t, kt * P:(kt + 1) * P], ident[:])
            ins.then_inc(s_tp2, 1)

        def pv(k):
            pe.wait_ge(s_pe2, at(k + 1, 4, i))
            pe.wait_ge(s_pf2, at(k + 1, 4, i))
            if i is not None or k:
                pe.wait_ge(s_y2, at(k, 4, i))
            for t in range(TT):
                for kt in range(4):
                    v = kvp[:, kt, 256 * k + 128:256 * k + 256] if k < 2 else kvb[:, kt, 256 + (k - 2) * HD:256 + (k - 1) * HD]
                    ins = nc.tensor.matmul(psum[:, 4, t * P:(t + 1) * P], pT2[:, kt, t * P:(t + 1) * P], v,
                                           start=(kt == 0), stop=(kt == 3))
            ins.then_inc(s_pv2, 1)
        turn(0)
        scores(0)
        for k in range(1, 4):
            turn(k)
            turn_p(k - 1)
            scores(k)
            pv(k - 1)
        turn_p(3)
        pv(3)

    def y2_turn_pe(pe):
        pe.wait_ge(s_y2, 16)
        for r in range(8):
            if r >= 2:
                pe.wait_ge(s_yl2, r - 1)
            for j in range(4):
                ft = 2 * r + j // 2
                src = (yA if ft < 8 else qb)[:, j % 2, (ft % 8) * P:(ft % 8 + 1) * P]
                ins = nc.tensor.transpose(psum[:, r % 2, j * P:(j + 1) * P], src, ident[:])
            ins.then_inc(s_yt, 1)

    def y2_turn_act(act):
        for r in range(8):
            act.wait_ge(s_yt, r + 1)
            nc.scalar.copy(hh[:, 2 * r:2 * r + 2], psum[:, r % 2].rearrange("p (a b) -> p a b", a=2)).then_inc(s_yh2, 1)

    def y2_turn_dve(dve):
        for r in range(8):
            dve.wait_ge(s_yh2, r + 1)
            nc.vector.tensor_tensor(hl[:, 2 * r:2 * r + 2], psum[:, r % 2].rearrange("p (a b) -> p a b", a=2),
                                    hh[:, 2 * r:2 * r + 2].bitcast(F32), ALU.subtract).then_inc(s_yl2, 1)

    s_post = sem("post_normed")

    def post_norm_dve(dve, ch, k, gain, bias):
        norm_dve(dve, ch, k, x, x, False)
        dve.wait_ge(s_xn, 2 * k + 2)
        for t in range(TT):
            ch(nc.vector.tensor_tensor(x[:, t], x[:, t], gain, ALU.mult))
        ch.wait()
        for t in range(TT):
            ins = nc.vector.tensor_tensor(x[:, t], x[:, t], bias, ALU.add)
            ins.then_inc(s_post, 1)
        dve.wait_ge(s_post, 2 if k == 4 else 4)

    def add_hidden_dve(dve, ch, H, scale, grow, n_rows):
        dve.wait_ge(H.dv, 4 * H.steps)
        dve.wait_ge(s_growc, n_rows)
        for t in range(TT):
            ch(nc.vector.tensor_tensor(xacc[:, t], xacc[:, t], grow, ALU.mult))
        ch.wait()
        for t in range(TT):
            ch(nc.vector.scalar_tensor_tensor(out=x[:, t], in0=x[:, t], scalar=scale, in1=xacc[:, t],
                                              op0=ALU.mult, op1=ALU.add))
        ch.wait()

    s_out = sem("out_stored")

    actx = arawf.rearrange("p (t n) -> p t n", t=TT)

    def rest_sp(sp):
        sp.wait_ge(s_acc, 16 * 48)
        sp.dma_start(actx, dram["ctx_2"][0].rearrange("(t p) n -> p t n", p=P)).then_inc(s_ctx, 16)
        sp.dma_start(rope_a[:], dram["rope_a"].rearrange("(t p) n -> p t n", p=P)).then_inc(s_ropes, 16)
        sp.dma_start(rope_b[:], dram["rope_b"].rearrange("(t p) n -> p t n", p=P)).then_inc(s_ropes, 16)
        sp.dma_start(wqk[:, 0], dram["q_norm_b_2"][0].partition_broadcast(P)).then_inc(s_ropes, 16)
        sp.dma_start(wqk[:, 1], dram["k_norm_b_2"][0].partition_broadcast(P)).then_inc(s_ropes, 16)
        ain_sp(sp)
        sp.wait_ge(s_tp, 32)
        pairs_sp(sp, U_AIN + 56, dram["w_in_attn_2"][0], None, 2, c0=2880)
        pair_sp(sp, None)
        with sp.Fori(1, 4) as i:
            pair_sp(sp, i)
        sp.wait_ge(s_yt, 8)
        sp.dma_start(gain3, dram["ln_g_2"][0].partition_broadcast(P)).then_inc(s_rows, 16)
        sp.dma_start(bias3, dram["ln_b_2"][0].partition_broadcast(P)).then_inc(s_rows, 16)
        pairs_sp(sp, U_AOUT, dram["w_out_attn_2"][0], None, 2)
        sp.wait_ge(s_post, 2)
        sp.dma_start(dft[:], dram["dft"].rearrange("(t p) n -> p t n", p=P)).then_inc(s_dft, 16)
        sp.dma_start(dft2[:], dram["dft2"].rearrange("(t p) n -> p t n", p=P)).then_inc(s_dft, 16)
        sp.dma_start(lng[:], dram["ln_g_2"][1].partition_broadcast(P)).then_inc(s_rows, 16)
        sp.dma_start(lnb[:], dram["ln_b_2"][1].partition_broadcast(P)).then_inc(s_rows, 16)
        fourier_steps(sp, lambda c, q, per, lo: hidden_sp(sp, fou, c, q, per, lo))
        hidden_end_sp(sp, fou)
        for t in range(TT):
            sp.wait_ge(s_post, 3 + t)
            sp.dma_start(out[0, t * P:(t + 1) * P], x[:, t]).then_inc(s_out, 16)
        sp.wait_ge(s_out, 32)

    def rest_pool(pool):
        norm_pool(pool, 2)
        norm_pool(pool, 3)
        turn_pool(pool, 2, h32, hh, hl)
        turn_pool(pool, 3, h32, ch_h, ch_l)
        z_pool(pool)
        norm_pool(pool, 4)
        norm_pool(pool, 5)
        turn_pool(pool, 4, h32, hh, hl)
        pool.wait_ge(s_tp, 40)
        nc.gpsimd.memset(xacc[:], 0.0).then_inc(s_zero, 1)
        norm_pool(pool, 6)

    def rest_act(act):
        turn_act(act, 2, h32, hh)
        turn_act(act, 3, h32, ch_h)
        ain_act(act)
        pairs_act(act, U_AIN + 56, 2, gate_evac)
        z_turn_act(act)
        pair_act(act, None)
        with act.Fori(1, 4) as i:
            pair_act(act, i)
        y2_turn_act(act)
        gate_act(act, 2, row3)
        pairs_act(act, U_AOUT, 2, None)
        turn_act(act, 4, h32, hh)
        fourier_steps(act, lambda c, q, per, lo: hidden_act(act, fou, c))
        hidden_end_act(act, fou)
        gate_act(act, 3, row2)

    def rest_dve(dve, ch):
        dve.wait_ge(s_ctx, 16)
        norm_dve(dve, ch, 2, actx, actx, False)
        add_hidden_dve(dve, ch, ffn, 1.0, row2[:], 8)
        norm_dve(dve, ch, 3, x, xn, False)
        ch(nc.vector.tensor_scalar(mscale[:], modc[:, 112:128], 1.0, None, ALU.add))
        ch(nc.vector.tensor_scalar(mscalex[:], modx[:, 16:32], 1.0, None, ALU.add))
        ch.wait()
        turn_dve(dve, 2, h32, mscale, modc[:, 96:112])
        turn_dve(dve, 3, h32, mscalex, modx[:, 0:16])
        ain_dve(dve)
        pairs_dve(dve, U_AIN + 56, None, 2)
        z_dve(dve, ch)
        z_turn_dve(dve)
        pair_dve(dve, ch, None)
        with dve.Fori(1, 4) as i:
            ch.enter(i, 1, 12)
            pair_dve(dve, ch, i)
            ch.leave(4)
        y2_turn_dve(dve)
        gate_dve(dve, 2, 128, diag)
        dve.wait_ge(s_growc, 12)
        pairs_dve(dve, U_AOUT, None, 2, ch=ch, ch_per=2,
                  evac=lambda e, c, per, i: gated(e, ch, c, per, i, U_AOUT, x, x, ALPHA, s_aev, row3, tmp3))
        dve.wait_ge(s_aev, 4)
        dve.wait_ge(s_rows, 32)
        post_norm_dve(dve, ch, 4, gain3, bias3)
        norm_dve(dve, ch, 5, x, xn, False)
        ch(nc.vector.tensor_scalar(mscale[:], modc[:, 160:176], 1.0, None, ALU.add))
        ch.wait()
        turn_dve(dve, 4, h32, mscale, modc[:, 144:160])
        fourier_steps(dve, lambda c, q, per, lo: hidden_dve(dve, fou, c, q, per, lo))
        hidden_end_dve(dve, fou)
        gate_dve(dve, 3, 176, diag)
        add_hidden_dve(dve, ch, fou, ALPHA, row2[:], 16)
        dve.wait_ge(s_rows, 64)
        post_norm_dve(dve, ch, 6, lng[:], lnb[:])

    def rest_pe(pe):
        turn_pe(pe, 2, xn, 3)
        turn_pe(pe, 3, actx, 2)
        pe.wait_ge(s_hl, 32)
        pe.wait_ge(s_mod, 32)
        pe.wait_ge(s_growc, 8)
        ain_pe(pe)
        pairs_pe(pe, U_AIN + 56, None, 2, s_ge)
        z_turn_pe(pe)
        pair_pe(pe, None)
        with pe.Fori(1, 4) as i:
            pair_pe(pe, i)
        y2_turn_pe(pe)
        gate_pe(pe, 2, diag)
        pe.wait_ge(s_yl2, 8)
        pairs_pe(pe, U_AOUT, None, 2, s_aev)
        turn_pe(pe, 4, xn, 5)
        pe.wait_ge(s_hl, 40)
        fourier_steps(pe, lambda c, q, per, lo: hidden_pe(pe, fou, c, q, per, lo))
        hidden_end_pe(pe, fou)
        gate_pe(pe, 3, diag)

    @block.sync
    def _(sp):
        sp.dma_start(cols[:], dram["cols"]).then_inc(s_const, 16)
        sp.dma_start(ident[:], dram["ident"]).then_inc(s_one, 16)
        sp.dma_start(rawf[:, 1024:3072].rearrange("p (r n) -> p r n", r=2), dram["b_pad"].rearrange("r p n -> p r n")).then_inc(s_b, 16)
        sp.dma_start(x[:], dram["x"][0].rearrange("(t p) n -> p t n", p=P)).then_inc(s_x, 16)
        for j in range(4):
            ada_load(sp, 0, j)
        for j in range(4):
            ada_load(sp, 1, j)
        with sp.Fori(1, 4) as i:
            for j in range(8):
                ada_load(sp, j // 4, j % 4, 2, i)
        sp.wait_ge(s_BT, 4)
        sp.wait_ge(s_chd_ssm, 1)
        pairs_sp(sp, U_IN, dram["w_in"][0], 8, 4, peel=True)
        sp.wait_ge(s_lo, U_GLU)
        sp.dma_start(dist, dram["dist"].rearrange("(t p) s -> p t s", p=P)).then_inc(s_dist, 16)
        sp.dma_start(count, dram["count"].rearrange("(t p) s -> p t s", p=P)).then_inc(s_dist, 16)
        sp.dma_start(rawf[:, 6144:8192].rearrange("p (r n) -> p r n", r=2), dram["c_pad"].rearrange("r p n -> p r n")).then_inc(s_cpad, 16)
        with sp.Fori(0, 4) as i:
            for j in range(8):
                ada_load(sp, 24 + j // 4, j % 4, 2, i)
        sp.wait_ge(s_ya, 8)
        glu_sp(sp)
        sp.wait_ge(s_yl, 4)
        pairs_sp(sp, U_OUT, dram["w_out"][0], 16, 2)
        ffn_steps(sp, lambda c, q, per, lo: hidden_sp(sp, ffn, c, q, per, lo))
        hidden_end_sp(sp, ffn)
        rest_sp(sp)

    @block.gpsimd
    def _(pool):
        ch = Chain(pool, s_chp)
        nc.gpsimd.memset(mhalf[:], -0.5).then_inc(s_mh, 1)
        nc.gpsimd.memset(ones[:], 1.0).then_inc(s_ones, 1)
        pool.wait_ge(s_mh, 1)
        norm_pool(pool, 0)
        turn_pool(pool, 0, h32, hh, hl)
        scan(pool, nc.gpsimd, ch, 0, "pool")
        a1_norms_pool(pool)
        scan(pool, nc.gpsimd, ch, 1, "pool")
        scan(pool, nc.gpsimd, ch, 3, "pool")
        norm_pool(pool, 1)
        turn_pool(pool, 1, h32, hh, hl)
        pool.wait_ge(s_tp, 16)
        nc.gpsimd.memset(xacc[:], 0.0).then_inc(s_zero, 1)
        rest_pool(pool)

    @block.scalar
    def _(act):
        act.wait_ge(s_const, 16)
        nc.scalar.activation(cond[:], cols[:, 0:48], ACT.Silu).then_inc(s_sil, 1)
        ssm_params_act(act)
        ada_chunk_act(act, 1)
        with act.Fori(0, 2) as i:
            ada_chunk_act(act, 2, 1, i)
        bbar_turn_act(act)
        with act.Fori(0, 5) as i:
            ada_chunk_act(act, 4, 1, i)
        turn_act(act, 0, h32, hh)
        pairs_act(act, U_IN, 4, in_evac, beside=beside_act)
        act.wait_ge(s_cpad, 16)
        nc.scalar.mul(cpad[:, 1], cpad[:, 1], -1.0).then_inc(s_cneg, 1)
        for n in range(8, 12):
            bu_act(act, n)
        a1_act(act)
        for n in range(12, 16):
            bu_act(act, n)
        a1_out_act(act)
        y_act(act, 0)
        y_act(act, 1)
        with act.Fori(0, 5) as i:
            ada_chunk_act(act, 20, 1, i)
        y_act(act, 2)
        y_act(act, 3)
        glu_act(act)
        gate_act(act, 0, row1)
        pairs_act(act, U_OUT, 2, None)
        turn_act(act, 1, h32, hh)
        ffn_steps(act, lambda c, q, per, lo: hidden_act(act, ffn, c))
        hidden_end_act(act, ffn)
        gate_act(act, 1, row2)
        rest_act(act)

    @block.vector
    def _(dve):
        ch = Chain(dve, s_chd)
        dve.wait_ge(s_const, 16)
        ssm_params_dve(dve, ch)
        nc.vector.memset(neg[:], 0.0).then_inc(s_chd_ssm, 1)
        dve.wait_ge(s_x, 16)
        norm_dve(dve, ch, 0, x, xn, True)
        dve.wait_ge(s_col, 8)
        add_bias(ch, modc[:, 0:32], 0, 32)
        ch.wait()
        ch(nc.vector.scalar_tensor_tensor(out=mscale[:], in0=modc[:, 16:32], scalar=1.0, in1=cols[:, COLS["n1"]],
                                          op0=ALU.add, op1=ALU.mult))
        ch.wait()
        turn_dve(dve, 0, h32, mscale, modc[:, 0:16])
        pairs_dve(dve, U_IN, 8, 4)
        a1_norms_dve(dve, ch)
        y_dve(dve, 0)
        a1_dve(dve, ch)
        y_dve(dve, 1)
        a1_out_dve(dve)
        scan(dve, nc.vector, ch, 2, "dve")
        y_dve(dve, 2)
        y_low(dve, 0)
        y_low(dve, 1)
        y_dve(dve, 3)
        y_low(dve, 2)
        y_low(dve, 3)
        glu_dve(dve)
        dve.wait_ge(s_col, 16)
        add_bias(ch, modc[:, 96:128], 96, 32)
        add_bias(ch, modx[:], 96, 32)
        ch.wait()
        gate_dve(dve, 0, 32, diag)
        dve.wait_ge(s_growc, 4)
        pairs_dve(dve, U_OUT, 16, 2, ch=ch, ch_per=2,
                  evac=lambda e, c, per, i: gated(e, ch, c, per, i, U_OUT, x, x, 1.0, s_oev, row1, mixed_tmp))
        dve.wait_ge(s_oev, 4)
        norm_dve(dve, ch, 1, x, xn, True)
        dve.wait_ge(s_mod, 12)
        ch(nc.vector.scalar_tensor_tensor(out=mscale[:], in0=modc[:, 64:80], scalar=1.0, in1=cols[:, COLS["n2"]],
                                          op0=ALU.add, op1=ALU.mult))
        ch.wait()
        turn_dve(dve, 1, h32, mscale, modc[:, 48:64])
        ffn_steps(dve, lambda c, q, per, lo: hidden_dve(dve, ffn, c, q, per, lo))
        hidden_end_dve(dve, ffn)
        gate_dve(dve, 1, 80, diag)
        rest_dve(dve, ch)

    @block.tensor
    def _(pe):
        pe.wait_ge(s_one, 16)
        pe.wait_ge(s_sil, 1)
        ada_chunk_pe(pe, 0, turn=False)
        ada_chunk_pe(pe, 1)
        with pe.Fori(0, 2) as i:
            ada_chunk_pe(pe, 2, 1, i)
        bbar_turn_pe(pe)
        with pe.Fori(0, 4) as i:
            ada_chunk_pe(pe, 4, 1, i)
        ada_turn(pe, 7)
        turn_pe(pe, 0, xn, 0)
        pe.wait_ge(s_hl, 8)
        pe.wait_ge(s_ones, 1)
        pairs_pe(pe, U_IN, 8, 4, s_inev, beside=beside_pe)
        y_pe(pe, 0)
        for n in range(8, 12):
            bu_pe(pe, n)
        pe.wait_ge(s_mod, 8)
        a1_pe(pe)
        y_pe(pe, 1)
        for n in range(12, 16):
            bu_pe(pe, n)
        a1_out_pe(pe)
        with pe.Fori(0, 4) as i:
            ada_chunk_pe(pe, 20, 1, i)
        ada_turn(pe, 23)
        y_pe(pe, 2)
        y_pe(pe, 3)
        glu_pe(pe)
        gate_pe(pe, 0, diag)
        pe.wait_ge(s_gl, 4)
        pe.wait_ge(s_al, 4)
        pairs_pe(pe, U_OUT, 16, 2, s_oev)
        turn_pe(pe, 1, xn, 1)
        pe.wait_ge(s_hl, 16)
        ffn_steps(pe, lambda c, q, per, lo: hidden_pe(pe, ffn, c, q, per, lo))
        hidden_end_pe(pe, ffn)
        gate_pe(pe, 1, diag)
        rest_pe(pe)
    ctx.close()


def col(a):
    a = np.asarray(a, np.float32).reshape(-1, P)
    return a.T


def shape_tables():
    t, k = np.arange(S)[:, None], np.arange(S)[None, :]
    d = t - k
    n = ((d >= 0) & (d <= 128)).astype(np.float32) + ((d >= 0) & (d <= 512) & (d % 4 == 0)) \
        + ((d >= 0) & (d <= 2048) & (d % 16 == 0))
    ang = 2 * np.pi * (np.outer(np.arange(S), np.arange(S)) % S) / S
    dft = np.concatenate([np.cos(ang), np.sin(ang)], 1) / 16
    out = {
        "dist": np.where(n > 0, d, 1e33).astype(np.float32), "count": n.astype(np.float32),
        "ident": np.eye(P, dtype=np.float32),
        "dft": dft.astype(np.float32), "dft2": (-np.sin(ang) / 16).astype(np.float32),
    }
    r, c = np.meshgrid(np.arange(S // 64), np.arange(64), indexing="ij")
    for name, rot in (("rope_a", 64), ("rope_b", 128)):
        nf = rot // 4
        inv = (np.float32(10000.0) ** (-np.arange(nf, dtype=np.float32) / np.float32(nf))).astype(np.float32)
        a = np.concatenate([r.reshape(-1, 1).astype(np.float32) * inv, c.reshape(-1, 1).astype(np.float32) * inv], 1)
        cs, sn = np.cos(a).astype(np.float32), np.sin(a).astype(np.float32)
        out[name] = np.concatenate([np.repeat(cs, 2, 1), np.stack([-sn, sn], 2).reshape(S, rot)], 1)
    return out


def kernel(**inputs):
    import concourse.bacc as bacc
    from concourse.bass_utils import run_bass_kernel_spmd

    a = {k: np.asarray(v) for k, v in inputs.items()}
    tables = shape_tables()

    def states(v):
        return v.reshape(PAIRS, 2, STATE).transpose(1, 2, 0).reshape(P, PAIRS)

    def pad(v):
        v = v.reshape(PAIRS, 2, STATE, GCH)
        o = np.zeros((2, STATE, PAIRS, 2, GCH), np.float32)
        for g in range(2):
            o[g, :, :, g] = v[:, g].transpose(1, 0, 2)
        return o.reshape(P, PAIRS * 2 * GCH)

    slope = -(2.0 ** -np.arange(1, HEADS + 1, dtype=np.float32))
    parts = {
        "c": col(a["c"]), "c2": col(a["c_2"]), "cctx": col(a["c_ctx_2"]), "n1": col(a["norm1_w"]),
        "n2": col(a["norm2_w"]), "bada": col(a["b_ada"]), "bada2": col(a["ada_b_2"]), "qn": col(a["q_norm_w"]),
        "kn": col(a["k_norm_w"]), "ssmd": col(a["ssm_d"]), "ql": col(a["q_lora_norm_2"]),
        "kvl": col(a["kv_lora_norm_2"]), "are": states(a["ssm_a_re"][0]), "aim": states(a["ssm_a_im"][0]),
        "ldt": states(np.repeat(a["ssm_log_dt"][0][:, None], STATE, 1)), "slope": np.repeat(slope[None], P, 0),
    }
    arrays = {
        "cols": np.concatenate([parts[k] for k in COLS], 1),
        "b_pad": np.stack([pad(a["ssm_b_re"][0]), pad(a["ssm_b_im"][0])]),
        "c_pad": np.stack([pad(a["ssm_c_re"][0].transpose(0, 2, 1)), pad(a["ssm_c_im"][0].transpose(0, 2, 1))]),
    }
    arrays.update(tables)
    for k in ("x", "ctx_2", "w_ada", "ada_w_2", "w_in", "ssm_w_glu", "w_out", "w_ffn_gate", "w_ffn_up", "w_ffn_down",
              "w_in_attn_2", "wq_b_2", "wkv_b_2", "w_out_attn_2", "w_in_fourier_2", "w_out_fourier_2",
              "ln_g_2", "ln_b_2", "q_norm_b_2", "k_norm_b_2"):
        arrays[k] = a[k]
    arrays = {k: np.ascontiguousarray(v) for k, v in arrays.items()}
    nc = bacc.Bacc("TRN2", target_bir_lowering=False, num_devices=1, dynamic_dma_scratch_size=1024)
    dram = {k: nc.dram_tensor("in_" + k, v.shape, F32, kind="ExternalInput").ap() for k, v in arrays.items()}
    out = nc.dram_tensor("out", (1, S, D), F32, kind="ExternalOutput").ap()
    program(nc, dram, out)
    r = run_bass_kernel_spmd(nc, [{"in_" + k: v for k, v in arrays.items()}], core_ids=[0])
    return r.results[0]["out"]
```
